# Optimizing a Trainium2 kernel written in Bass

```python
import jax, jax.numpy as jnp
from jax import lax
import numpy as np

D_MODEL = 1024
BATCH = 1
SEQ = 512
DEPTH = 2

GRID_W = 64
CTX_LEN = 256
HEAD_DIM = 64
A_HEADS = 8
A_KV_HEADS = 2
C_HEADS = 8
C_KV_HEADS = 2
WINDOW = 128
BLOCK = 128
BRANCH_WIDTH = A_HEADS * HEAD_DIM
B_WIDTH = BRANCH_WIDTH
CONV_W = 3
N_BRANCH = 3
N_MOD = 6
ROPE_THETA = 10000.0
PEER_HEADS = 8
N_KEYS = 128
N_EXPERTS = N_KEYS * N_KEYS
PEER_TOPK = 16
PEER_QDIM = 256
PEER_BLOCK = 128
IN_COLS = (A_HEADS + 2 * A_KV_HEADS + C_HEADS + 2 * C_KV_HEADS) * HEAD_DIM + 3 * B_WIDTH + N_BRANCH * D_MODEL
DEEPNORM_ALPHA = (2 * DEPTH) ** 0.25
DEEPNORM_BETA = (8 * DEPTH) ** -0.25
LN_EPS = 1e-6
RMS_EPS = 1e-6
NEG_INF = -1e30
ATTN_SCALE = HEAD_DIM ** -0.5

kernel_name = 'hybrid_dit_gqa_conv_swa_peer'

def _in_splits():
    sizes = (A_HEADS * HEAD_DIM, A_KV_HEADS * HEAD_DIM, A_KV_HEADS * HEAD_DIM,
             C_HEADS * HEAD_DIM, C_KV_HEADS * HEAD_DIM, C_KV_HEADS * HEAD_DIM,
             B_WIDTH, B_WIDTH, B_WIDTH, N_BRANCH * D_MODEL)
    return [int(v) for v in np.cumsum(sizes)[:-1]]

def layer_norm(x, g, b):
    xf = x.astype(jnp.float32)
    mu = jnp.mean(xf, axis=-1, keepdims=True)
    xc = xf - mu
    var = jnp.mean(xc * xc, axis=-1, keepdims=True)
    return (xc * lax.rsqrt(var + LN_EPS) * g + b).astype(x.dtype)

def rms_norm(x, g):
    xf = x.astype(jnp.float32)
    return (xf * lax.rsqrt(jnp.mean(xf * xf, axis=-1, keepdims=True) + RMS_EPS) * g).astype(x.dtype)

def modulate(x, shift, scale):
    return x * (1 + scale) + shift

def axial_rope(n_tok):
    rows = n_tok // GRID_W
    row = jnp.repeat(jnp.arange(rows, dtype=jnp.int32), GRID_W)
    col = jnp.tile(jnp.arange(GRID_W, dtype=jnp.int32), rows)
    quarter = HEAD_DIM // 4
    inv_freq = ROPE_THETA ** (-jnp.arange(quarter, dtype=jnp.float32) / quarter)
    ang = jnp.stack([row, col], axis=-1).astype(jnp.float32)[..., None] * inv_freq
    return jnp.cos(ang), jnp.sin(ang)

def apply_rope(x, cos, sin):
    xr = x.astype(jnp.float32).reshape(*x.shape[:-1], 2, 2, HEAD_DIM // 4)
    x1, x2 = xr[..., 0, :], xr[..., 1, :]
    c = cos[None, :, None]
    s = sin[None, :, None]
    out = jnp.stack([x1 * c - x2 * s, x2 * c + x1 * s], axis=-2)
    return out.reshape(x.shape).astype(x.dtype)

def to_blocks(x):
    b, l = x.shape[:2]
    return jnp.moveaxis(x.reshape(b, l // BLOCK, BLOCK, *x.shape[2:]), 1, 0)

def from_blocks(x):
    nb, b = x.shape[:2]
    return jnp.moveaxis(x, 0, 1).reshape(b, nb * BLOCK, *x.shape[3:])

def dense_gqa(q, k, v, sink_g=None):
    s = jnp.einsum('bqkgd,bskd->bkgqs', q, k).astype(jnp.float32) * ATTN_SCALE
    if sink_g is not None:
        s_sink = jnp.broadcast_to(sink_g.astype(jnp.float32)[None, :, :, None, None], s.shape[:-1] + (1,))
        p = jax.nn.softmax(jnp.concatenate([s, s_sink], axis=-1), axis=-1)[..., :-1]
    else:
        p = jax.nn.softmax(s, axis=-1)
    return jnp.einsum('bkgqs,bskd->bqkgd', p.astype(v.dtype), v)

def banded_attention(q, k, v, k_ctx, v_ctx, sink_g):
    s_len = q.shape[1]
    pad = ((0, 0), (BLOCK, BLOCK), (0, 0), (0, 0))

    def band(t):
        tb = to_blocks(jnp.pad(t, pad))
        return jnp.concatenate([tb[:-2], tb[1:-1], tb[2:]], axis=2)

    valid = jnp.pad(jnp.ones((s_len,), jnp.bool_), (BLOCK, BLOCK)).reshape(-1, BLOCK)
    valid = jnp.concatenate([valid[:-2], valid[1:-1], valid[2:]], axis=1)
    rel = jnp.arange(3 * BLOCK)[None, :] - BLOCK - jnp.arange(BLOCK)[:, None]
    in_win = jnp.abs(rel) <= WINDOW
    n_loc = 3 * BLOCK
    n_ctx = k_ctx.shape[1]

    def blk(args):
        qb, kb, vb, vmask = args
        s_loc = jnp.einsum('bqkgd,bskd->bkgqs', qb, kb).astype(jnp.float32) * ATTN_SCALE
        s_loc = jnp.where(in_win & vmask[None, :], s_loc, NEG_INF)
        s_ctx = jnp.einsum('bqkgd,bskd->bkgqs', qb, k_ctx).astype(jnp.float32) * ATTN_SCALE
        s_sink = jnp.broadcast_to(sink_g.astype(jnp.float32)[None, :, :, None, None], s_ctx.shape[:-1] + (1,))
        p = jax.nn.softmax(jnp.concatenate([s_loc, s_ctx, s_sink], axis=-1), axis=-1).astype(vb.dtype)
        return (jnp.einsum('bkgqs,bskd->bqkgd', p[..., :n_loc], vb)
                + jnp.einsum('bkgqs,bskd->bqkgd', p[..., n_loc:n_loc + n_ctx], v_ctx))

    out = lax.map(blk, (to_blocks(q), band(k), band(v), valid))
    return from_blocks(out)

def short_conv(xb, gb, gc, w):
    z = gc * xb
    half = CONV_W // 2
    zp = jnp.pad(z, ((0, 0), (half, half), (0, 0)))
    n = z.shape[1]
    y = sum(w[i] * zp[:, i:i + n] for i in range(CONV_W))
    return gb * y

def merge_branches(ya, yb, yc, gate_logits, w_branch, w_out):
    gates = jax.nn.sigmoid(gate_logits).reshape(*gate_logits.shape[:-1], N_BRANCH, D_MODEL)
    m = sum(gates[..., i, :] * (y @ w_branch[i]) for i, y in enumerate((ya, yb, yc)))
    return m @ w_out

def token_mixer(h_lat, h_ctx, w_in, q_g, k_g, conv_w, sink, w_branch, w_out, cos, sin, need_ctx):
    bsz, s_len, _ = h_lat.shape
    c_len = h_ctx.shape[1]
    g_a = A_HEADS // A_KV_HEADS
    g_c = C_HEADS // C_KV_HEADS
    splits = _in_splits()

    def heads(t, n):
        return t.reshape(*t.shape[:-1], n, HEAD_DIM)

    qa, ka, va, qc, kc, vc, xb, gb, gc, glog = jnp.split(h_lat @ w_in, splits, axis=-1)
    qa_x, ka_x, va_x, qc_x, kc_x, vc_x, xb_x, gb_x, gc_x, glog_x = jnp.split(h_ctx @ w_in, splits, axis=-1)

    qa = apply_rope(rms_norm(heads(qa, A_HEADS), q_g), cos, sin).reshape(bsz, s_len, A_KV_HEADS, g_a, HEAD_DIM)
    ka = apply_rope(rms_norm(heads(ka, A_KV_HEADS), k_g), cos, sin)
    va = heads(va, A_KV_HEADS)
    ka_x = rms_norm(heads(ka_x, A_KV_HEADS), k_g)
    va_x = heads(va_x, A_KV_HEADS)
    k_all = jnp.concatenate([ka_x, ka], axis=1)
    v_all = jnp.concatenate([va_x, va], axis=1)
    ya = from_blocks(lax.map(lambda qb: dense_gqa(qb, k_all, v_all), to_blocks(qa)))
    ya = ya.reshape(bsz, s_len, A_HEADS * HEAD_DIM)

    sink_g = sink.reshape(C_KV_HEADS, g_c)
    qc = apply_rope(heads(qc, C_HEADS), cos, sin).reshape(bsz, s_len, C_KV_HEADS, g_c, HEAD_DIM)
    kc = apply_rope(heads(kc, C_KV_HEADS), cos, sin)
    vc = heads(vc, C_KV_HEADS)
    kc_x = heads(kc_x, C_KV_HEADS)
    vc_x = heads(vc_x, C_KV_HEADS)
    yc = banded_attention(qc, kc, vc, kc_x, vc_x, sink_g).reshape(bsz, s_len, C_HEADS * HEAD_DIM)

    yb = short_conv(xb, gb, gc, conv_w)

    y_lat = merge_branches(ya, yb, yc, glog, w_branch, w_out)

    if need_ctx:
        qa_x = rms_norm(heads(qa_x, A_HEADS), q_g).reshape(bsz, c_len, A_KV_HEADS, g_a, HEAD_DIM)
        ya_x = dense_gqa(qa_x, ka_x, va_x).reshape(bsz, c_len, A_HEADS * HEAD_DIM)
        qc_x = heads(qc_x, C_HEADS).reshape(bsz, c_len, C_KV_HEADS, g_c, HEAD_DIM)
        yc_x = dense_gqa(qc_x, kc_x, vc_x, sink_g).reshape(bsz, c_len, C_HEADS * HEAD_DIM)
        yb_x = short_conv(xb_x, gb_x, gc_x, conv_w)
        y_ctx = merge_branches(ya_x, yb_x, yc_x, glog_x, w_branch, w_out)
    else:
        y_ctx = None
    return y_lat, y_ctx

def peer(h, w_pq, sub_keys, u_tab, v_tab):
    shape = h.shape
    blocks = h.reshape(-1, PEER_BLOCK, D_MODEL)
    half = PEER_QDIM // 2

    def blk(xb):
        q = (xb @ w_pq).reshape(PEER_BLOCK, PEER_HEADS, 2, half)
        s = jnp.einsum('thpd,hpnd->thpn', q, sub_keys).astype(jnp.float32)
        s1, i1 = lax.top_k(s[:, :, 0], PEER_TOPK)
        s2, i2 = lax.top_k(s[:, :, 1], PEER_TOPK)
        cand = (s1[..., :, None] + s2[..., None, :]).reshape(PEER_BLOCK, PEER_HEADS, PEER_TOPK * PEER_TOPK)
        cand_idx = (i1[..., :, None] * N_KEYS + i2[..., None, :]).reshape(PEER_BLOCK, PEER_HEADS, PEER_TOPK * PEER_TOPK)
        top, pos = lax.top_k(cand, PEER_TOPK)
        expert = jnp.take_along_axis(cand_idx, pos, axis=-1)
        g = jax.nn.softmax(top, axis=-1).astype(xb.dtype)
        u = jnp.take(u_tab, expert, axis=0)
        v = jnp.take(v_tab, expert, axis=0)
        a = jax.nn.gelu(jnp.einsum('td,thkd->thk', xb, u), approximate=False) * g
        return jnp.einsum('thk,thkd->td', a, v)

    return lax.map(blk, blocks).reshape(shape)

def setup_inputs(seed: int = 0) -> dict:
    key = jax.random.key(seed)
    ks = jax.random.split(key, 21)
    L = DEPTH
    D = D_MODEL

    def nrm(k, shape, scale):
        return jax.random.normal(k, shape, jnp.float32) * scale

    return {
        'x': nrm(ks[0], (BATCH, SEQ, D), 1.0),
        'c': nrm(ks[1], (BATCH, D), 1.0),
        'ctx': nrm(ks[2], (BATCH, CTX_LEN, D), 1.0),
        'c_ctx': nrm(ks[3], (D,), 1.0),
        'w_mod': nrm(ks[4], (L, D, N_MOD * D), 0.5 * D ** -0.5),
        'b_mod': nrm(ks[5], (L, N_MOD * D), 0.02),
        'w_in': nrm(ks[6], (L, D, IN_COLS), D ** -0.5),
        'q_norm': 1.0 + nrm(ks[7], (L, HEAD_DIM), 0.02),
        'k_norm': 1.0 + nrm(ks[8], (L, HEAD_DIM), 0.02),
        'conv_w': nrm(ks[9], (L, CONV_W, B_WIDTH), CONV_W ** -0.5),
        'sink': nrm(ks[10], (L, C_HEADS), 0.5),
        'w_branch': nrm(ks[11], (L, N_BRANCH, BRANCH_WIDTH, D), DEEPNORM_BETA * BRANCH_WIDTH ** -0.5),
        'w_out': nrm(ks[12], (L, D, D), DEEPNORM_BETA * D ** -0.5),
        'ln1_g': 1.0 + nrm(ks[13], (L, D), 0.02),
        'ln1_b': nrm(ks[14], (L, D), 0.02),
        'w_pq': nrm(ks[15], (L, D, PEER_HEADS * PEER_QDIM), D ** -0.5),
        'sub_keys': nrm(ks[16], (L, PEER_HEADS, 2, N_KEYS, PEER_QDIM // 2), (PEER_QDIM // 2) ** -0.5),
        'u_tab': nrm(ks[17], (L, N_EXPERTS, D), D ** -0.5),
        'v_tab': nrm(ks[18], (L, N_EXPERTS, D), DEEPNORM_BETA * PEER_HEADS ** -0.5),
        'ln2_g': 1.0 + nrm(ks[19], (L, D), 0.02),
        'ln2_b': nrm(ks[20], (L, D), 0.02),
    }

def reference(x, c, ctx, c_ctx, w_mod, b_mod, w_in, q_norm, k_norm, conv_w, sink, w_branch, w_out,
              ln1_g, ln1_b, w_pq, sub_keys, u_tab, v_tab, ln2_g, ln2_b):
    s_len = x.shape[1]
    cos, sin = axial_rope(s_len)
    alpha = DEEPNORM_ALPHA
    for layer in range(DEPTH):
        need_ctx = layer < DEPTH - 1
        mod = (jax.nn.silu(c) @ w_mod[layer] + b_mod[layer])[:, None, :]
        mod_x = jax.nn.silu(c_ctx) @ w_mod[layer] + b_mod[layer]
        sh1, sc1, g1, sh2, sc2, g2 = jnp.split(mod, N_MOD, axis=-1)
        xsh1, xsc1, xg1, xsh2, xsc2, xg2 = jnp.split(mod_x, N_MOD, axis=-1)

        y, y_x = token_mixer(modulate(x, sh1, sc1), modulate(ctx, xsh1, xsc1), w_in[layer],
                             q_norm[layer], k_norm[layer], conv_w[layer], sink[layer],
                             w_branch[layer], w_out[layer], cos, sin, need_ctx)
        x = layer_norm(alpha * x + g1 * y, ln1_g[layer], ln1_b[layer])
        f = peer(modulate(x, sh2, sc2), w_pq[layer], sub_keys[layer], u_tab[layer], v_tab[layer])
        x = layer_norm(alpha * x + g2 * f, ln2_g[layer], ln2_b[layer])

        if need_ctx:
            ctx = layer_norm(alpha * ctx + xg1 * y_x, ln1_g[layer], ln1_b[layer])
            f_x = peer(modulate(ctx, xsh2, xsc2), w_pq[layer], sub_keys[layer], u_tab[layer], v_tab[layer])
            ctx = layer_norm(alpha * ctx + xg2 * f_x, ln2_g[layer], ln2_b[layer])
    return x


_drawn_inputs = setup_inputs


def setup_inputs(seed=0):
    import zlib

    import numpy as np

    out = dict(_drawn_inputs(seed))
    spreads = {}
    factors = {'ctx': 8.0, 'c_ctx': 7.128, 'b_mod': 7.952, 'q_norm': 8.0, 'k_norm': 8.0, 'sink': 64.0}
    for name, (base, spread) in spreads.items():
        noise = np.random.default_rng([zlib.crc32(name.encode()), seed]).standard_normal(out[name].shape)
        drawn = base * np.exp(spread * noise) if base else spread * noise
        out[name] = __import__('jax').numpy.asarray(drawn.astype(out[name].dtype))
    for name, factor in factors.items():
        out[name] = (out[name] * factor).astype(out[name].dtype)
    return out
```

```python
from contextlib import ExitStack, contextmanager

import concourse.bass as bass
from concourse import mybir

P = 128
D = 1024
KD = D // P
LAYERS = 2
LAT, CTX = 4, 2
TILES = LAT + CTX
TOK = TILES * P
HD = 64
HEADS = 8
KV = 2
BW = HEADS * HD
BC = BW // P
QKV = 3 * BW
SCALE = HD ** -0.5
ALPHA = (2 * LAYERS) ** 0.25
EPS = 1e-6
NEG = -1e30
LOWEST = -3.4e38

PH = 8
TOPK = 16
NK = 128
EXPERTS = NK * NK
UR, VR = 4, 8
GR = 4
GROUPS = TOPK // GR

F32 = mybir.dt.float32
U32 = mybir.dt.uint32
ALU = mybir.AluOpType
ACT = mybir.ActivationFunctionType
AX = mybir.AxisListType.X
ds = bass.ds


class Chain:

    def __init__(self, eng, sem):
        self.eng, self.sem, self.base, self.k = eng, sem, 0, 0

    def inc(self, ins):
        ins.then_inc(self.sem, 1)
        self.k += 1

    def wait(self, alone=None):
        self.eng.wait_ge(self.sem, self.base + self.k)
        if alone is not None:
            self.eng.sem_inc(alone, 1)

    @contextmanager
    def loop(self, start, n, per):
        base, k = self.base, self.k
        with self.eng.Fori(start, start + n) as r:
            self.base, self.k = base + k + (r - start) * per, 0
            yield r
            assert self.k == per, ("increments of a round", self.k, "not", per)
        self.base, self.k = base, k + n * per


def hybrid_dit_peer(nc, x, ctx, cc, w_mod, b_mod, w_qkv, q_norm, k_norm, conv_w, sink, w_conv, w_gb,
                    w_out, ln1_g, ln1_b, w_pq, sub_keys, u_tab, v_tab, ln2_g, ln2_b, rope_c, rope_s,
                    out):
    with ExitStack() as stack:
        def sb(name, shape, dt=F32):
            return stack.enter_context(nc.sbuf_tensor(name, shape, dt))

        def sem(name):
            return stack.enter_context(nc.semaphore(name))

        x_all = sb("x_all", [P, TILES, D])
        ident = sb("ident", [P, P])
        zeros = sb("zeros", [P, P])
        iota16 = sb("iota16", [P, TOPK])
        ropec = sb("ropec", [P, TILES, HD])
        ropes = sb("ropes", [P, TILES, HD])
        mask = sb("mask", [P, LAT, 2, P])
        qn = sb("qn", [P, LAYERS, HD])
        kn = sb("kn", [P, LAYERS, HD])
        sinks = sb("sinks", [P, LAYERS, HEADS])
        nsink = sb("nsink", [P, LAYERS, HEADS])
        convw = sb("convw", [P, LAYERS, BC, 3])
        ccol = sb("ccol", [P, KD, 2])
        csig = sb("csig", [P, KD, 2])
        csilu = sb("csilu", [P, KD, 2])
        ss = sb("ss", [P, 16])
        rstd = sb("rstd", [P, 16])
        mx = sb("mx", [P, HEADS])
        nm = sb("nm", [P, HEADS])
        sums = sb("sums", [P, HEADS])
        es = sb("es", [P, HEADS])
        rec = sb("rec", [P, HEADS])
        stats = sb("stats", [P, 2, 6])
        mv = sb("mv", [P, 2])
        sd = sb("sd", [P, 2])
        AK = 170
        arena = sb("arena", [P, AK * 256])

        def region(kb, *shape):
            n = 1
            for s in shape:
                n *= s
            a0 = int(kb * 256)
            assert a0 + n <= AK * 256, (kb, shape)
            v = arena[:, a0:a0 + n]
            if len(shape) == 2:
                return v.rearrange("p (a b) -> p a b", b=shape[1])
            if len(shape) == 3:
                return v.rearrange("p (a b c) -> p a b c", b=shape[1], c=shape[2])
            return v

        xT = region(0, KD, TOK)
        wqkv = region(24, KD, QKV)
        rows1 = region(72, 4, D)
        xm = region(88, D)
        xTs = region(92, KD, P)
        qTa = region(96, BC, TOK)
        qTc = region(108, BC, TOK)
        kTa = region(120, KV, TOK)
        kTc = region(126, KV, 8 * P)
        va = region(134, TILES, P)
        vc = region(137, 8, P)
        pq_a = region(141, BW)
        pkv = region(143, BW)
        pq_c = region(145, BW)
        rt = region(147, BW)
        rq_a = region(149, BW)
        rq_c = region(151, BW)
        rk = region(153, BW)
        wmod = [region(96 + 16 * b, KD, BW) for b in range(2)]
        modrow = region(141, 2, BW)[0:2]
        brow = region(145, 2, BW)[0:2]
        qz = [region(72 + 4 * b, HEADS, P) for b in range(2)]
        pr = [region(80 + 3 * b, TILES * P) for b in range(2)]
        pts = [region(86 + 3 * b, TILES, P) for b in range(2)]
        ysb = [region(92 + 2 * b, BW) for b in range(2)]
        yT = [region(24 + 12 * b, BC, TOK) for b in range(3)]
        wcv = [region(154 + 4 * b, KD, P) for b in range(4)]
        zb = region(72, 772)
        xbs = region(76, TOK)
        ycv = region(79, TOK)
        gbw = [region(60 + 6 * b, KD + BC, P) for b in range(2)]
        sg = [region(82 + 3 * b, TOK) for b in range(2)]
        mtmp = region(88, TOK)
        mT = region(96, KD, TOK)
        wout = region(120, KD, D)
        rows2 = region(154, 4, D)
        lt = region(72, D)

        wpq = region(0, KD, 2 * PH * P)
        ur = region(64, UR, D)
        vr = region(80, VR, D)
        prow = region(112, 3, D)
        ln2 = region(124, 2, D)
        keys = region(132, 2 * PH, P)
        hn = region(140, D)
        hT = region(144, KD, P)
        fx = region(148, D)
        dg = region(152, VR, P)
        q_sb = region(156, 2, P)
        qT_sb = region(157, 2, P)
        sc = region(158, 2, P)
        sc2 = region(159, 2, P)
        cand = region(160, TOPK, TOPK)
        cand2 = region(161, TOPK, TOPK)
        eq = region(162, 2 * TOPK, TOPK)
        gates = region(164, TILES * PH * TOPK)
        v16 = sb("v16", [P, 2, TOPK])
        i16 = sb("i16", [P, 2, TOPK], U32)
        i16f = sb("i16f", [P, 2, TOPK])
        top = sb("top", [P, TOPK])
        pos = sb("pos", [P, TOPK], U32)
        ab = sb("ab", [P, 2, TOPK], U32)
        abf = sb("abf", [P, 2, TOPK])
        sel = sb("sel", [P, 2, TOPK])
        idxf = sb("idxf", [P, TOPK])
        ntop = sb("ntop", [P, 1])
        te = sb("te", [P, TOPK])
        tsum = sb("tsum", [P, 2])
        idx = region(167, TILES * PH * TOPK).bitcast(U32)
        ist = [sb(f"ist{b}", [P, TOPK], U32) for b in range(2)]
        dots = sb("dots", [P, 2, GR])
        gl = sb("gl", [P, 2, GR])
        coef = sb("coef", [P, 2, GR])

        ps = stack.enter_context(nc.psum_tensor("ps", [P, 8 * BW], F32))

        def bank(b, lo=0, hi=BW):
            return ps[:, b * BW + lo:b * BW + hi]

        mods = nc.dram_tensor("mods", [LAYERS, 2, 6 * D], F32).ap()
        SH1, SC1, G1, SH2, SC2, G2 = range(6)

        def mod_row(l, kind, which):
            return mods[l, kind:kind + 1, which * D:(which + 1) * D].partition_broadcast(P)

        def row_of(t):
            return t.partition_broadcast(P)

        s = {n: sem(n) for n in (
            "x_in small_in ident_made consts_made wqkv_in c_in c_sig c_silu bmod_in0 bmod_in1 wmod_in0 wmod_in1 "
            "mod_mm mod_done mod_out0 mod_out1 rows1_in xm_done xt_mm xts_done xt_copied qa_mm kv_mm qc_mm qa_sb kv_sb "
            "qc_sb ss_done sd_done rqa_done rk_done rqc_done ta_mm tk_mm tc_mm qTa_done kT_done qTc_done "
            "v_chain pads_done qz_done s_mm nm_done p_done pt_mm pta_done ptb_done pv_mm es_in es_done y_done yt_mm yT_done "
            "wcv_in0 wcv_in1 wcv_in2 wcv_in3 cv_used xb_mm gc_mm gb_mm xbs_done cv_done yb_done "
            "gbw_in0 gbw_in1 g_mm b_mm sg_done m_evac mT_done wout_in rows2_in y_mm var_done std_done y_read x_mid "
            "wpq_in keys_in ln2_in prow_in g2_in hn_done ht_mm hT_done q_mm q_copied qT_mm qT_copied sc_mm sc_copied "
            "top_done exp_done idx_done gate_done dots_done gelu_done coef_done diag_done v_used pool_turn "
            "v_turn idx_staged f_read x_new x_out").split()}
        u_in = [sem(f"u_in{k}") for k in range(UR)]
        v_in = [sem(f"v_in{k}") for k in range(VR)]
        CREDIT = {"p_done": 2, "pta_done": 1, "ptb_done": 1, "pv_mm": 2, "y_done": 1, "yT_done": 1,
                  "m_evac": 2, "b_mm": 2, "dots_done": UR, "v_used": 2, "mod_done": 2, "mod_out0": 16, "mod_out1": 16,
                  "mod_mm": 2, "xts_done": 1, "xt_mm": 1, "xt_copied": 1, "qa_sb": 1, "kv_sb": 1, "qc_sb": 1,
                  "qa_mm": 1, "kv_mm": 1, "qc_mm": 1, "rqa_done": 1, "rk_done": 1, "rqc_done": 1,
                  "ta_mm": 1, "tk_mm": 1, "tc_mm": 1, "qTa_done": 1, "kT_done": 1, "qTc_done": 1,
                  "y_read": 2, "cv_done": 1, "hT_done": 1, "ht_mm": 1, "q_mm": 1, "q_copied": 1, "qT_mm": 1,
                  "qT_copied": 1, "sc_mm": 1, "sc_copied": 1, "top_done": 1, "idx_done": 1, "f_read": 1,
                  "idx_staged": 0, "x_new": 1, "hn_done": 1, "exp_done": 1, "yt_mm": 1, "gate_done": 1}
        OWNER = {
            "pe": "pv_mm b_mm v_used mod_mm xt_mm qa_mm kv_mm qc_mm ta_mm tk_mm tc_mm ht_mm q_mm qT_mm sc_mm yt_mm",
            "act": "p_done ptb_done yT_done xts_done qa_sb kv_sb qc_sb qTa_done kT_done qTc_done hT_done q_copied "
                   "qT_copied sc_copied exp_done",
            "dve": "pta_done y_done m_evac dots_done mod_done xt_copied rqa_done rk_done rqc_done y_read cv_done "
                   "top_done idx_done f_read x_new hn_done gate_done",
            "sp": "mod_out0 mod_out1"}

        def give_credits(eng, who):
            for n in OWNER[who].split():
                if CREDIT[n]:
                    eng.sem_inc(s[n], CREDIT[n])

        def need(eng, name, n):
            eng.wait_ge(s[name], n + CREDIT.get(name, 0))

        n_att = [HEADS * 0, 12]
        n_tiles = [0, TILES]
        width = [TOK, LAT * P]
        live = [TILES, LAT]

        block = stack.enter_context(nc.Block())

        @block.sync
        def _(sp):
            sp.dma_start(ccol[:], cc).then_inc(s["c_in"], 16)
            give_credits(sp, "sp")

            def modulation(l):
                with sp.Fori(0, 6) as r:
                    for b in range(2):
                        need(sp, "mod_mm", 12 * l + 2 * r + b - 1)
                        need(sp, "mod_done", 12 * l + 2 * r + b - 1)
                        sp.dma_start(wmod[b], w_mod[l, ds(2 * r + b, 1)].rearrange("o p k n -> p (o k) n")
                                     ).then_inc(s[f"wmod_in{b}"], 16)
                        sp.dma_start(brow[:, b, :], b_mod[l:l + 1, ds((2 * r + b) * BW, BW)].partition_broadcast(2)
                                     ).then_inc(s[f"bmod_in{b}"], 16)
                        if b == 1:
                            for c in range(2):
                                need(sp, "mod_done", 12 * l + 2 * r + c + 1)
                                sp.dma_start(mods[l, :, ds((2 * r + c) * BW, BW)], modrow[:, c, :]
                                             ).then_inc(s[f"mod_out{c}"], 16)
                for b in range(2):
                    need(sp, f"mod_out{b}", 16 * 6 * (l + 1))
                for kind in range(2):
                    for j, which in enumerate((SC1, SH1)):
                        sp.dma_start(rows1[:, 2 * kind + j, :], mod_row(l, kind, which)[:, 0, :]
                                     ).then_inc(s["rows1_in"], 16)

            def mixer(l):
                if l == 1:
                    need(sp, "x_new", TILES)
                sp.dma_start(wqkv, w_qkv[l]).then_inc(s["wqkv_in"], 16)
                if l == 0:
                    sp.dma_start(x_all[:, 0:LAT, :], x.rearrange("o (t p) d -> p (o t) d", p=P)).then_inc(s["x_in"], 16)
                    sp.dma_start(x_all[:, LAT:TILES, :], ctx.rearrange("o (t p) d -> p (o t) d", p=P)).then_inc(s["x_in"], 16)
                    for dst, src in ((ropec[:], rope_c), (ropes[:], rope_s), (convw[:], conv_w)):
                        sp.dma_start(dst, src).then_inc(s["small_in"], 16)
                    for dst, src in ((qn, q_norm), (kn, k_norm), (sinks, sink)):
                        for ll in range(LAYERS):
                            sp.dma_start(dst[:, ll, :], row_of(src[ll:ll + 1, :])[:, 0, :]).then_inc(s["small_in"], 16)
                modulation(l)
                need(sp, "yT_done", n_att[l] + 2 * live[l])
                for e in range(3 * BC):
                    if e >= 4:
                        sp.wait_ge(s["cv_used"], 3 * BC * l + e - 3)
                    sp.dma_start(wcv[e % 4], w_conv[l, e]).then_inc(s[f"wcv_in{e % 4}"], 16)
                sp.dma_start(wout, w_out[l]).then_inc(s["wout_in"], 16)
                with sp.Fori(0, 12) as r:
                    for b in range(2):
                        need(sp, "b_mm", 24 * l + 2 * r + b - 1)
                        sp.dma_start(gbw[b], w_gb[l, ds(2 * r + b, 1)].rearrange("o p k n -> p (o k) n")
                                     ).then_inc(s[f"gbw_in{b}"], 16)
                sp.wait_ge(s["cv_used"], 3 * BC * (l + 1))
                for j, src in enumerate((mod_row(l, 0, G1), mod_row(l, 1, G1), row_of(ln1_g[l:l + 1]), row_of(ln1_b[l:l + 1]))):
                    sp.dma_start(rows2[:, j, :], src[:, 0, :]).then_inc(s["rows2_in"], 16)

            def peer(l):
                n0 = n_tiles[l]
                sp.wait_ge(s["x_mid"], n0 + live[l])
                sp.dma_start(prow[:, 0, :], mod_row(l, 0, SC2)[:, 0, :]).then_inc(s["prow_in"], 16)
                sp.dma_start(prow[:, 1, :], mod_row(l, 0, SH2)[:, 0, :]).then_inc(s["prow_in"], 16)
                sp.dma_start(wpq, w_pq[l]).then_inc(s["wpq_in"], 16)
                sp.dma_start(keys, sub_keys[l]).then_inc(s["keys_in"], 16)
                for j, src in enumerate((ln2_g, ln2_b)):
                    sp.dma_start(ln2[:, j, :], row_of(src[l:l + 1])[:, 0, :]).then_inc(s["ln2_in"], 16)

                def g2_row(t):
                    need(sp, "x_new", n0 + t)
                    sp.dma_start(prow[:, 2, :], mods[l, ds(t // LAT, 1), G2 * D:(G2 + 1) * D].partition_broadcast(P)[:, 0, :]
                                 ).then_inc(s["g2_in"], 16)

                with sp.Fori(0, live[l] - 1) as t:
                    g2_row(t)
                    need(sp, "hn_done", n0 + t + 1)
                    for j, which in enumerate((SC2, SH2)):
                        sp.dma_start(prow[:, j, :], mods[l, ds((t + 1) // LAT, 1), which * D:(which + 1) * D].partition_broadcast(P)[:, 0, :]
                                     ).then_inc(s["prow_in"], 16)
                    if l == 1:
                        need(sp, "x_new", n0 + t + 1)
                        sp.dma_start(out[0, ds(t * P, P), :], x_all[:, ds(t, 1), :].rearrange("p o d -> p (o d)")
                                     ).then_inc(s["x_out"], 16)
                g2_row(live[l] - 1)

            for l in range(LAYERS):
                mixer(l)
                peer(l)
            need(sp, "x_new", n_tiles[1] + LAT)
            sp.dma_start(out[0, (LAT - 1) * P:LAT * P, :], x_all[:, LAT - 1, :]).then_inc(s["x_out"], 16)
            sp.wait_ge(s["x_out"], 16 * LAT)

        @block.gpsimd
        def _(pool):
            nc.gpsimd.memset(ident[:], 1.0).then_inc(s["ident_made"], 1)
            pool.wait_ge(s["ident_made"], 1)
            nc.gpsimd.affine_select(out=ident[:], in_=ident[:], compare_op=ALU.is_equal, fill=0.0, base=0,
                                    pattern=[[-1, P]], channel_multiplier=1).then_inc(s["ident_made"], 1)
            nc.gpsimd.memset(zeros[:], 0.0).then_inc(s["consts_made"], 1)
            nc.gpsimd.iota(iota16[:], [[1, TOPK]], base=0, channel_multiplier=0,
                           allow_small_or_imprecise_dtypes=True).then_inc(s["consts_made"], 1)
            nc.gpsimd.memset(mask[:], 0.0).then_inc(s["consts_made"], 1)
            pool.wait_ge(s["consts_made"], 3)
            for t in range(LAT):
                for side in range(2):
                    m = mask[:, t, side, :]
                    if (t, side) in ((0, 0), (LAT - 1, 1)):
                        nc.gpsimd.memset(m, NEG).then_inc(s["consts_made"], 1)
                    else:
                        sign = 1 if side == 0 else -1
                        nc.gpsimd.affine_select(out=m, in_=m, compare_op=ALU.is_ge, fill=NEG, base=0,
                                                pattern=[[sign, P]], channel_multiplier=-sign
                                                ).then_inc(s["consts_made"], 1)

            u_rows = u_tab.rearrange("l e d -> (l e) d")
            v_rows = v_tab.rearrange("l e d -> (l e) d")

            def head(i, i_idx, b):
                need(pool, "idx_done", i + 1)
                nc.gpsimd.tensor_copy(ist[b][:], idx[:, ds(i_idx * TOPK, TOPK)]).then_inc(s["idx_staged"], 1)
                pool.wait_ge(s["idx_staged"], i + 1)
                for q in range(GROUPS):
                    g = GROUPS * i + q
                    need(pool, "dots_done", UR * g)
                    pool.sem_inc(s["pool_turn"], 1)
                    for k in range(GR):
                        nc.gpsimd.indirect_dma_start(
                            ur[:, k, :], None, u_rows,
                            bass.IndirectOffsetOnAxis(ap=ist[b][:, q * GR + k:q * GR + k + 1], axis=0)
                        ).then_inc(u_in[k], 16)
                    need(pool, "v_used", g - 1)
                    pool.sem_inc(s["pool_turn"], 1)
                    for k in range(GR):
                        nc.gpsimd.indirect_dma_start(
                            vr[:, GR * (q % 2) + k, :], None, v_rows,
                            bass.IndirectOffsetOnAxis(ap=ist[b][:, q * GR + k:q * GR + k + 1], axis=0)
                        ).then_inc(v_in[GR * (q % 2) + k], 16)

            for l in range(LAYERS):
                i0 = PH * n_tiles[l]
                with pool.Fori(0, PH * live[l] // 2) as r:
                    for b in range(2):
                        head(i0 + 2 * r + b, 2 * r + b, b)

        @block.tensor
        def _(pe):
            give_credits(pe, "pe")
            pe.wait_ge(s["ident_made"], 2)
            pe.wait_ge(s["consts_made"], 3 + 2 * LAT)

            def mm(o, lhsT, rhs, first=True, last=True):
                return nc.tensor.matmul(o, lhsT, rhs, start=first, stop=last, skip_group_check=True)

            def modulation(l):
                if l == 0:
                    pe.wait_ge(s["c_silu"], 1)
                with pe.Fori(0, 6) as r:
                    for b in range(2):
                        pe.wait_ge(s[f"wmod_in{b}"], 16 * (6 * l + r + 1))
                        need(pe, "mod_done", 12 * l + 2 * r + b - 1)
                        for k in range(KD):
                            m = mm(bank(b)[0:2, :], csilu[:, k, :], wmod[b][:, k, :], k == 0, k == KD - 1)
                        m.then_inc(s["mod_mm"], 1)

            def project(l, lo, n, with_q):
                with pe.Fori(lo, lo + n) as t:
                    i = TILES * l + t
                    pe.wait_ge(s["xm_done"], i + 1)
                    need(pe, "xts_done", i)
                    for k in range(KD):
                        m = nc.tensor.transpose(bank(0, k * P, (k + 1) * P), xm[:, k * P:(k + 1) * P], ident[:])
                    m.then_inc(s["xt_mm"], 1)
                    need(pe, "xts_done", i + 1)
                    pe.wait_ge(s["wqkv_in"], 16 * (l + 1))
                    for b, name, copied in ((1, "kv_mm", "kv_sb"), (0, "qa_mm", "qa_sb"), (2, "qc_mm", "qc_sb")):
                        if b != 1 and not with_q:
                            continue
                        need(pe, copied, i)
                        for k in range(KD):
                            m = mm(bank(2 + b), xTs[:, k, :], wqkv[:, k, b * BW:(b + 1) * BW], k == 0, k == KD - 1)
                        m.then_inc(s[name], 1)
                    for src, done, b, name, copied in ((rk, "rk_done", 7, "tk_mm", "kT_done"), (rq_a, "rqa_done", 5, "ta_mm", "qTa_done"),
                                                       (rq_c, "rqc_done", 6, "tc_mm", "qTc_done")):
                        if b != 7 and not with_q:
                            continue
                        need(pe, done, i + 1)
                        need(pe, copied, i)
                        for k in range(BC):
                            m = nc.tensor.transpose(bank(b, k * P, (k + 1) * P), src[:, k * P:(k + 1) * P], ident[:])
                        m.then_inc(s[name], 1)

            def attend(u, t, branch, lat, yt_before):
                kT, v = (kTa, va) if branch == 0 else (kTc, vc)
                local = lat and branch == 1

                def scores(h):
                    hh = HEADS * u + h
                    o = 2 * (h % 2)
                    g = h // (HEADS // KV)
                    need(pe, "p_done", hh - 1)
                    q = qz[branch][:, h, :]
                    if branch == 0:
                        if lat:
                            mm(bank(o), q, kT[:, g, 0:BW])
                        m = mm(bank(o + 1, 0, 2 * P), q, kT[:, g, BW:TOK])
                    else:
                        if lat:
                            mm(bank(o, P, BW), q, kT[:, g, ds(t * P, 3 * P)])
                        m = mm(bank(o + 1, 0, 2 * P), q, kT[:, g, 6 * P:8 * P])
                    m.then_inc(s["s_mm"], 1)

                first = 0 if lat and branch == 0 else 1 if lat else 4

                def values(h):
                    hh = HEADS * u + h
                    g = h // (HEADS // KV)
                    need(pe, "p_done", hh + 1)
                    need(pe, "pta_done", hh)
                    need(pe, "ptb_done", hh)
                    for j in range(first, TILES):
                        m = nc.tensor.transpose(bank(4 + j // 4, (j % 4) * P, (j % 4 + 1) * P),
                                                pr[h % 2][:, j * P:(j + 1) * P], ident[:])
                    m.then_inc(s["pt_mm"], 1)
                    need(pe, "pta_done", hh + 1)
                    need(pe, "ptb_done", hh + 1)
                    if h == 0:
                        need(pe, "y_done", u)
                    for j in range(first, TILES):
                        if branch == 0:
                            vj = v[:, j, g * HD:(g + 1) * HD]
                        elif j < 4:
                            vj = v[:, ds(t + (j - 1), 1), g * HD:(g + 1) * HD].rearrange("p o d -> p (o d)")
                        else:
                            vj = v[:, j + 2, g * HD:(g + 1) * HD]
                        m = mm(bank(6, h * HD, (h + 1) * HD), pts[h % 2][:, j, :], vj, j == first, j == TILES - 1)
                    m.then_inc(s["pv_mm"], 1)

                pe.wait_ge(s["qz_done"], u + 1)
                for h in range(HEADS + 1):
                    if h < HEADS:
                        scores(h)
                    if h == 2 and yt_before:
                        turn_y(u - 1, 1 - branch)
                    if h >= 1:
                        values(h - 1)

            def turn_y(u, branch):
                need(pe, "y_done", u + 1)
                need(pe, "yT_done", u)
                for k in range(BC):
                    m = nc.tensor.transpose(bank(7, k * P, (k + 1) * P), ysb[branch][:, k * P:(k + 1) * P], ident[:])
                m.then_inc(s["yt_mm"], 1)

            def attention(l):
                for lo, n, lat in ((0, LAT, True), (LAT, CTX, False))[:2 - l]:
                    with pe.Fori(lo, lo + n) as t:
                        u = n_att[l] + 2 * t
                        attend(u, t, 0, lat, False)
                        attend(u + 1, t, 1, lat, True)
                        turn_y(u + 1, 1)

            def over_tokens(l, b, lhs, rhs, n):
                for k in range(n):
                    m = mm(bank(b), lhs(k), rhs[:, k, 0:LAT * P], k == 0, k == n - 1)
                if l == 0:
                    for k in range(n):
                        m = mm(bank(b + 1, 0, CTX * P), lhs(k), rhs[:, k, LAT * P:TOK], k == 0, k == n - 1)
                return m

            def convolution(l):
                for c in range(BC):
                    if c or l:
                        need(pe, "cv_done", BC * l + c)
                    for j, name in enumerate(("xb_mm", "gc_mm", "gb_mm")):
                        e = 3 * c + j
                        pe.wait_ge(s[f"wcv_in{e % 4}"], 16 * (3 * l + e // 4 + 1))
                        m = over_tokens(l, 2 * j, lambda k: wcv[e % 4][:, k, :], xT, KD)
                        m.then_inc(s[name], 1)
                        pe.wait_ge(s[name], BC * l + c + 1)
                        pe.sem_inc(s["cv_used"], 1)

            def merge(l):
                need(pe, "cv_done", BC * (l + 1))
                pe.wait_ge(s["yb_done"], BC * (l + 1))
                with pe.Fori(0, 4) as r:
                    for e6 in range(6):
                        e = 24 * l + 6 * r + e6
                        b, i = e6 % 2, e6 % 3
                        pe.wait_ge(s[f"gbw_in{b}"], 16 * (12 * l + 3 * r + e6 // 2 + 1))
                        need(pe, "m_evac", e - 1)
                        over_tokens(l, 4 * b, lambda k: gbw[b][:, k, :], xT, KD).then_inc(s["g_mm"], 1)
                        over_tokens(l, 4 * b + 2, lambda k: gbw[b][:, KD + k, :], yT[i], BC).then_inc(s["b_mm"], 1)

            def project_out(l):
                pe.wait_ge(s["mT_done"], 24 * (l + 1))
                pe.wait_ge(s["wout_in"], 16 * (l + 1))
                for t in range(live[l]):
                    need(pe, "y_read", n_tiles[l] + t - 1)
                    for half in range(2):
                        for k in range(KD):
                            m = mm(bank(2 * (t % 2) + half), mT[:, k, t * P:(t + 1) * P],
                                   wout[:, k, half * BW:(half + 1) * BW], k == 0, k == KD - 1)
                    m.then_inc(s["y_mm"], 1)

            def turn_h(n):
                need(pe, "hn_done", n + 1)
                need(pe, "hT_done", n)
                for k in range(KD):
                    m = nc.tensor.transpose(bank(4, k * P, (k + 1) * P), hn[:, k * P:(k + 1) * P], ident[:])
                m.then_inc(s["ht_mm"], 1)

            def head(i, h, gather, route):
                j = i + PH if gather else i

                def sum_group(q):
                    g = GROUPS * i + q
                    for k in range(GR):
                        slot = GR * (q % 2) + k
                        pe.wait_ge(v_in[slot], 16 * (2 * i + q // 2 + 1))
                        pe.wait_ge(s["diag_done"], GR * g + k + 1)
                        mm(bank(0), dg[:, slot, :], vr[:, slot, 0:BW], False, True)
                        m = mm(bank(1), dg[:, slot, :], vr[:, slot, BW:D], False, True)
                    m.then_inc(s["v_used"], 1)

                if route:
                    need(pe, "hT_done", (j // PH) + 1)
                    need(pe, "q_copied", j)
                    for k in range(KD):
                        m = mm(bank(6, 0, 2 * P), hT[:, k, :], wpq[:, k, ds(h * (2 * P), 2 * P)], k == 0, k == KD - 1)
                    m.then_inc(s["q_mm"], 1)
                if gather:
                    sum_group(0)
                if route:
                    need(pe, "q_copied", j + 1)
                    need(pe, "qT_copied", j)
                    for k in range(2):
                        m = nc.tensor.transpose(bank(6, (2 + k) * P, (3 + k) * P), q_sb[:, k, :], ident[:])
                    m.then_inc(s["qT_mm"], 1)
                if gather:
                    sum_group(1)
                if route:
                    need(pe, "qT_copied", j + 1)
                    need(pe, "sc_copied", j)
                    for k in range(2):
                        m = mm(bank(7, k * P, (k + 1) * P), qT_sb[:, k, :],
                               keys[:, ds(2 * h + k, 1), :].rearrange("p o n -> p (o n)"))
                    m.then_inc(s["sc_mm"], 1)
                if gather:
                    sum_group(2)
                    sum_group(3)

            def heads(n, gather, route):
                with pe.Fori(0, PH // 2) as r:
                    for b in range(2):
                        head(PH * n + 2 * r + b, 2 * r + b, gather, route)

            def clear_sum(n):
                need(pe, "f_read", n)
                for b in range(2):
                    mm(bank(b), zeros[:], wpq[:, 0, 0:BW], True, False)

            def peer(l):
                n0 = n_tiles[l]
                pe.wait_ge(s["wpq_in"], 16 * (l + 1))
                pe.wait_ge(s["keys_in"], 16 * (l + 1))
                turn_h(n0)
                heads(n0, False, True)
                with pe.Fori(0, live[l] - 1) as t:
                    clear_sum(n0 + t)
                    turn_h(n0 + t + 1)
                    heads(n0 + t, True, True)
                clear_sum(n0 + live[l] - 1)
                heads(n0 + live[l] - 1, True, False)

            for l in range(LAYERS):
                modulation(l)
                if l == 0:
                    project(l, 0, TILES, True)
                else:
                    project(l, 0, LAT, True)
                    project(l, LAT, CTX, False)
                attention(l)
                convolution(l)
                merge(l)
                project_out(l)
                peer(l)

        @block.scalar
        def _(act):
            give_credits(act, "act")

            def copy(o, i, name):
                nc.scalar.copy(o, i).then_inc(s[name], 1)

            act.wait_ge(s["c_in"], 16)
            nc.scalar.activation(csig[:], ccol[:], ACT.Sigmoid).then_inc(s["c_sig"], 1)

            def project(l, lo, n, with_q):
                with act.Fori(lo, lo + n) as t:
                    i = TILES * l + t
                    need(act, "xt_mm", i + 1)
                    need(act, "xt_copied", i)
                    need(act, "kv_mm", i)
                    if with_q:
                        need(act, "qa_mm", i)
                        need(act, "qc_mm", i)
                    copy(xTs.rearrange("p a b -> p (a b)"), ps[:, 0:D], "xts_done")
                    for src, dst, m, done, name in ((3, pkv, "kv_mm", "rk_done", "kv_sb"), (2, pq_a, "qa_mm", "rqa_done", "qa_sb"),
                                                    (4, pq_c, "qc_mm", "rqc_done", "qc_sb")):
                        if src != 3 and not with_q:
                            continue
                        need(act, m, i + 1)
                        need(act, done, i)
                        copy(dst, bank(src), name)
                    act.wait_ge(s["ss_done"], i + 1)
                    nc.scalar.activation(rstd[:, 0:10], ss[:, 0:10], ACT.Sqrt).then_inc(s["sd_done"], 1)
                    need(act, "tk_mm", i + 1)
                    col = lambda b: ds(b * P, P)
                    kv = bank(7).rearrange("p (g c) -> p g c", g=4)
                    nc.scalar.copy(kTa[:, :, col(t)], kv[:, 0:2, :])
                    copy(kTc[:, :, col(t + 1 + t // LAT)], kv[:, 2:4, :], "kT_done")
                    if with_q:
                        for b, dst, m, name in ((5, qTa, "ta_mm", "qTa_done"), (6, qTc, "tc_mm", "qTc_done")):
                            need(act, m, i + 1)
                            copy(dst[:, :, col(t)], bank(b).rearrange("p (g c) -> p g c", g=4), name)

            def attend(u, t, branch, lat, l, yt_before):
                first = 0 if lat and branch == 0 else 1 if lat else 4

                def exp(h):
                    hh = HEADS * u + h
                    o = 2 * BW * (h % 2)
                    act.wait_ge(s["nm_done"], hh + 1)
                    nc.scalar.activation(pr[h % 2][:, first * P:TOK], ps[:, o + first * P:o + TOK], ACT.Exp,
                                         bias=nm[:, h:h + 1], scale=SCALE, accum_out=sums[:, h:h + 1]
                                         ).then_inc(s["p_done"], 1)

                def evacuate(h):
                    hh = HEADS * u + h
                    act.wait_ge(s["pt_mm"], hh + 1)
                    need(act, "pv_mm", hh - 1)
                    copy(pts[h % 2][:, 4:6, :].rearrange("p a b -> p (a b)"), bank(5, 0, 2 * P), "ptb_done")

                for h in range(HEADS + 1):
                    if h < HEADS:
                        exp(h)
                    if h == 3 and yt_before:
                        evacuate_y(u - 1, t, 1 - branch)
                    if h >= 1:
                        evacuate(h - 1)
                if branch == 1:
                    act.wait_ge(s["es_in"], (u + 1) // 2)
                    nc.scalar.activation(es[:], es[:], ACT.Exp).then_inc(s["es_done"], 1)

            def evacuate_y(u, t, branch):
                need(act, "yt_mm", u + 1)
                copy(yT[2 * branch][:, :, ds(t * P, P)], bank(7).rearrange("p (a b) -> p a b", b=P), "yT_done")

            def attention(l):
                for lo, n, lat in ((0, LAT, True), (LAT, CTX, False))[:2 - l]:
                    with act.Fori(lo, lo + n) as t:
                        u = n_att[l] + 2 * t
                        attend(u, t, 0, lat, l, False)
                        attend(u + 1, t, 1, lat, l, True)
                        evacuate_y(u + 1, t, 1)

            def convolution(l):
                for c in range(BC):
                    act.wait_ge(s["xb_mm"], BC * l + c + 1)
                    need(act, "cv_done", BC * l + c)
                    copy(xbs[:, 0:width[l]], ps[:, 0:width[l]], "xbs_done")

            def merge(l):
                with act.Fori(0, 4) as r:
                    for e6 in range(6):
                        e = 24 * l + 6 * r + e6
                        b = e6 % 2
                        act.wait_ge(s["g_mm"], e + 1)
                        need(act, "m_evac", e - 1)
                        nc.scalar.activation(sg[b][:, 0:width[l]], ps[:, 4 * b * BW:4 * b * BW + width[l]],
                                             ACT.Sigmoid).then_inc(s["sg_done"], 1)

            def std(n):
                act.wait_ge(s["var_done"], n + 1)
                nc.scalar.activation(sd[:, 1:2], sd[:, 0:1], ACT.Sqrt).then_inc(s["std_done"], 1)

            def copy_hT(n):
                need(act, "ht_mm", n + 1)
                need(act, "q_mm", PH * n)
                copy(hT.rearrange("p a b -> p (a b)"), ps[:, 4 * BW:6 * BW], "hT_done")

            def head(i, gather, route):
                j = i + PH if gather else i

                def gelu(q):
                    g = GROUPS * i + q
                    need(act, "dots_done", GR * (g + 1))
                    nc.scalar.activation(gl[:, q % 2, :], dots[:, q % 2, :], ACT.Gelu).then_inc(s["gelu_done"], 1)

                def diagonals(q):
                    g = GROUPS * i + q
                    act.wait_ge(s["coef_done"], g + 1)
                    need(act, "v_used", g - 1)
                    for k in range(GR):
                        nc.scalar.activation(dg[:, GR * (q % 2) + k, :], ident[:], ACT.Copy,
                                             scale=coef[:, q % 2, k:k + 1]).then_inc(s["diag_done"], 1)

                if gather:
                    gelu(0)
                if route:
                    need(act, "q_mm", j + 1)
                    copy(q_sb.rearrange("p a b -> p (a b)"), bank(6, 0, 2 * P), "q_copied")
                if gather:
                    gelu(1)
                    diagonals(0)
                if route:
                    need(act, "qT_mm", j + 1)
                    need(act, "sc_mm", j)
                    copy(qT_sb.rearrange("p a b -> p (a b)"), bank(6, 2 * P, 4 * P), "qT_copied")
                if gather:
                    gelu(2)
                    diagonals(1)
                if route:
                    need(act, "sc_mm", j + 1)
                    need(act, "gate_done", j)
                    copy(sc.rearrange("p a b -> p (a b)"), bank(7, 0, 2 * P), "sc_copied")
                if gather:
                    gelu(3)
                    diagonals(2)
                    diagonals(3)
                if route:
                    need(act, "top_done", j + 1)
                    nc.scalar.activation(te[:], top[:], ACT.Exp, bias=ntop[:], accum_out=tsum[:, 0:1]
                                         ).then_inc(s["exp_done"], 1)

            def heads(n, gather, route):
                with act.Fori(0, PH // 2) as r:
                    for b in range(2):
                        head(PH * n + 2 * r + b, gather, route)

            def peer(l):
                n0 = n_tiles[l]
                norm0 = 2 * n0 + live[l]
                copy_hT(n0)
                heads(n0, False, True)
                with act.Fori(0, live[l] - 1) as t:
                    copy_hT(n0 + t + 1)
                    heads(n0 + t, True, True)
                    std(norm0 + t)
                heads(n0 + live[l] - 1, True, False)
                std(norm0 + live[l] - 1)

            for l in range(LAYERS):
                if l == 0:
                    project(l, 0, TILES, True)
                else:
                    project(l, 0, LAT, True)
                    project(l, LAT, CTX, False)
                attention(l)
                convolution(l)
                merge(l)
                with act.Fori(0, live[l]) as t:
                    std(2 * n_tiles[l] + t)
                peer(l)

        @block.vector
        def _(dve):
            v = nc.vector
            give_credits(dve, "dve")
            ch = Chain(dve, s["v_chain"])
            dve.wait_ge(s["c_sig"], 1)
            dve.wait_ge(s["consts_made"], 3 + 2 * LAT)
            v.tensor_tensor(csilu[:], csig[:], ccol[:], ALU.mult).then_inc(s["c_silu"], 1)

            def modulation(l):
                with dve.Fori(0, 6) as r:
                    for b in range(2):
                        e = 12 * l + 2 * r + b
                        need(dve, "mod_mm", e + 1)
                        dve.wait_ge(s[f"bmod_in{b}"], 16 * (6 * l + r + 1))
                        need(dve, f"mod_out{b}", 16 * (6 * l + r))
                        v.tensor_tensor(modrow[:, b, :], bank(b)[0:2, :], brow[:, b, :], ALU.add
                                        ).then_inc(s["mod_done"], 1)

            def rope(o, q, t, n, dup):
                q4 = q.rearrange("p (h f) -> p h f", f=HD)
                r4 = rt[:, 0:n * HD].rearrange("p (h f) -> p h f", f=HD)
                c = ropec[:, ds(t, 1), :].to_broadcast([P, n, HD])
                q5 = q.rearrange("p (h a s f) -> p h a s f", a=2, s=2, f=16)
                r5 = rt[:, 0:n * HD].rearrange("p (h a s f) -> p h a s f", a=2, s=2, f=16)
                for half in range(2):
                    sn = ropes[:, ds(t, 1), :].rearrange("p o (a s f) -> p o a s f", a=2, s=2)[:, :, :, half, :]
                    ch.inc(v.tensor_tensor(r5[:, :, :, half, :], q5[:, :, :, 1 - half, :],
                                           sn.to_broadcast([P, n, 2, 16]), ALU.mult))
                ch.wait()
                ch.inc(v.tensor_tensor(q4, q4, c, ALU.mult))
                ch.wait()
                return q4, r4

            def norm(q, n, at, g):
                q3 = q.rearrange("p (h f) -> p h f", f=HD)
                ch.inc(v.tensor_tensor(q3, q3, rstd[:, at:at + n].rearrange("p (h o) -> p h o", o=1).to_broadcast([P, n, HD]), ALU.mult))
                ch.wait()
                ch.inc(v.tensor_tensor(q3, q3, g.rearrange("p (o f) -> p o f", o=1).to_broadcast([P, n, HD]), ALU.mult))
                ch.wait()

            def squares(q, n, at):
                r = rt[:, 0:n * HD]
                ch.inc(v.tensor_tensor(r, q, q, ALU.mult))
                ch.wait()
                ch.inc(v.tensor_reduce(ss[:, at:at + n], r.rearrange("p (h f) -> p h f", f=HD), AX, ALU.add))
                ch.wait()

            def project(l, lo, n, with_q, per):
                with ch.loop(lo, n, per) as t:
                    i = TILES * l + t
                    need(dve, "xt_mm", i)
                    xt = x_all[:, ds(t, 1), :].rearrange("p o d -> p (o d)")
                    row = lambda j: rows1[:, ds(2 * (t // LAT) + j, 1), :].rearrange("p o d -> p (o d)")
                    ch.inc(v.scalar_tensor_tensor(out=xm, in0=row(0), scalar=1.0, in1=xt, op0=ALU.add, op1=ALU.mult))
                    ch.wait()
                    v.tensor_tensor(xm, xm, row(1), ALU.add).then_inc(s["xm_done"], 1)
                    need(dve, "xts_done", i + 1)
                    v.tensor_copy(xT[:, :, ds(t * P, P)], xTs).then_inc(s["xt_copied"], 1)
                    need(dve, "kv_sb", i + 1)
                    squares(pkv[:, 0:P], KV, HEADS)
                    if with_q:
                        need(dve, "qa_sb", i + 1)
                        squares(pq_a, HEADS, 0)
                    v.tensor_scalar(ss[:, 0:10], ss[:, 0:10], 1.0 / HD, EPS, ALU.mult, ALU.add).then_inc(s["ss_done"], 1)
                    ch.inc(v.tensor_copy(va[:, ds(t, 1), :].rearrange("p o d -> p (o d)"), pkv[:, P:2 * P]))
                    ch.inc(v.tensor_copy(vc[:, ds(t + 1 + t // LAT, 1), :].rearrange("p o d -> p (o d)"), pkv[:, 3 * P:4 * P]))
                    dve.wait_ge(s["sd_done"], i + 1)
                    ch.inc(v.reciprocal(rstd[:, 0:10], rstd[:, 0:10]))
                    ch.wait()
                    need(dve, "tk_mm", i)
                    norm(pkv[:, 0:P], KV, HEADS, kn[:, l, :])
                    twice = lambda o: o.rearrange("p (g r f) -> p g r f", r=2, f=HD)
                    for part in range(2):
                        q4, r4 = rope(rk, pkv[:, 2 * part * P:(2 * part + 1) * P], t, KV, 2)
                        for r in range(2):
                            last = v.tensor_tensor(twice(rk[:, 2 * part * P:2 * (part + 1) * P])[:, :, r, :], q4, r4, ALU.add)
                            if (part, r) == (1, 1):
                                last.then_inc(s["rk_done"], 1)
                            else:
                                ch.inc(last)
                        if part == 0:
                            ch.wait()
                    need(dve, "rk_done", i + 1)
                    if with_q:
                        need(dve, "ta_mm", i)
                        norm(pq_a, HEADS, 0, qn[:, l, :])
                        q4, r4 = rope(rq_a, pq_a, t, HEADS, 1)
                        v.tensor_tensor(rq_a.rearrange("p (h f) -> p h f", f=HD), q4, r4, ALU.add).then_inc(s["rqa_done"], 1)
                        need(dve, "rqa_done", i + 1)
                        need(dve, "qc_sb", i + 1)
                        need(dve, "tc_mm", i)
                        q4, r4 = rope(rq_c, pq_c, t, HEADS, 1)
                        v.tensor_tensor(rq_c.rearrange("p (h f) -> p h f", f=HD), q4, r4, ALU.add).then_inc(s["rqc_done"], 1)
                        need(dve, "rqc_done", i + 1)

            def attend(u, t, branch, lat, l):
                first = 0 if lat and branch == 0 else 1 if lat else 4
                qT = (qTa, qTc)[branch]
                for half in range(2):
                    rows = slice(64 * half, 64 * half + 64)
                    o = qz[branch][rows].rearrange("p (c two) n -> p c two n", two=2)[:, :, half, :]
                    m = v.tensor_copy(o, qT[rows, :, ds(t * P, P)])
                    if half == 0:
                        ch.inc(m)
                ch.wait()
                m.then_inc(s["qz_done"], 1)

                def maximum(h):
                    hh = HEADS * u + h
                    o = 2 * BW * (h % 2)
                    dve.wait_ge(s["s_mm"], hh + 1)
                    if lat and branch == 1:
                        edge = ps[:, o + P:o + P + 4 * P].rearrange("p (a b) -> p a b", a=2)[:, :, 0:P]
                        ch.inc(v.tensor_tensor(edge, edge, mask[:, ds(t, 1), :, :].rearrange("p o a b -> p (o a) b"), ALU.add))
                        ch.wait()
                    ch.inc(v.reduce_max(mx[:, h:h + 1], ps[:, o + first * P:o + TOK], AX))
                    ch.wait()
                    if branch == 1:
                        m = v.tensor_scalar(nm[:, h:h + 1], mx[:, h:h + 1], -SCALE, nsink[:, l, h:h + 1], ALU.mult, ALU.min)
                    else:
                        m = v.tensor_scalar(nm[:, h:h + 1], mx[:, h:h + 1], -SCALE, None, ALU.mult)
                    m.then_inc(s["nm_done"], 1)

                def evacuate(h):
                    hh = HEADS * u + h
                    if first < 4:
                        dve.wait_ge(s["pt_mm"], hh + 1)
                        need(dve, "pv_mm", hh - 1)
                        v.tensor_copy(pts[h % 2][:, first:4, :].rearrange("p a b -> p (a b)"), bank(4, first * P, BW)
                                      ).then_inc(s["pta_done"], 1)
                    else:
                        dve.sem_inc(s["pta_done"], 1)

                for h in range(HEADS + 1):
                    if h < HEADS:
                        maximum(h)
                    if h >= 1:
                        evacuate(h - 1)
                need(dve, "p_done", HEADS * (u + 1))
                if branch == 1:
                    v.tensor_tensor(es[:], nm[:], sinks[:, l, :], ALU.add).then_inc(s["es_in"], 1)
                    dve.wait_ge(s["es_done"], (u + 1) // 2)
                    ch.inc(v.tensor_tensor(sums[:], sums[:], es[:], ALU.add))
                    ch.wait()
                ch.inc(v.reciprocal(rec[:], sums[:]))
                ch.wait()
                need(dve, "pv_mm", HEADS * (u + 1))
                need(dve, "yt_mm", u - 1 if branch else u - 1)
                v.tensor_tensor(ysb[branch].rearrange("p (h f) -> p h f", f=HD), bank(6).rearrange("p (h f) -> p h f", f=HD),
                                rec[:].rearrange("p (h o) -> p h o", o=1).to_broadcast([P, HEADS, HD]), ALU.mult
                                ).then_inc(s["y_done"], 1)
                need(dve, "y_done", u + 1)

            def attention(l, pers):
                if l == 0:
                    dve.wait_ge(s["small_in"], 16 * 9)
                if l == 0:
                    ch.inc(v.tensor_scalar(nsink[:], sinks[:], -1.0, None, ALU.mult))
                for b in range(2):
                    ch.inc(v.memset(qz[b], 0.0))
                ch.wait()
                need(dve, "kT_done", TILES * (l + 1))
                need(dve, "qTa_done", TILES + LAT * l)
                need(dve, "qTc_done", TILES + LAT * l)
                for (lo, n, lat), per in zip(((0, LAT, True), (LAT, CTX, False))[:2 - l], pers):
                    with ch.loop(lo, n, per) as t:
                        u = n_att[l] + 2 * t
                        attend(u, t, 0, lat, l)
                        attend(u + 1, t, 1, lat, l)

            def convolution(l):
                w = width[l]
                ch.inc(v.memset(zb, 0.0))
                ch.wait()
                parts = [(1, 0, LAT * P), (515, LAT * P, CTX * P)][:2 - l]
                for c in range(BC):
                    dve.wait_ge(s["xbs_done"], BC * l + c + 1)
                    dve.wait_ge(s["gc_mm"], BC * l + c + 1)
                    for z0, x0, n in parts:
                        ch.inc(v.tensor_tensor(zb[:, z0:z0 + n], xbs[:, x0:x0 + n], ps[:, 2 * BW + x0:2 * BW + x0 + n], ALU.mult))
                    ch.wait()
                    for z0, x0, n in parts:
                        ch.inc(v.tensor_scalar(ycv[:, x0:x0 + n], zb[:, z0 - 1:z0 - 1 + n], convw[:, l, c, 0:1], None, ALU.mult))
                    ch.wait()
                    for tap in (1, 2):
                        for z0, x0, n in parts:
                            ch.inc(v.scalar_tensor_tensor(out=ycv[:, x0:x0 + n], in0=zb[:, z0 - 1 + tap:z0 - 1 + tap + n],
                                                          scalar=convw[:, l, c, tap:tap + 1], in1=ycv[:, x0:x0 + n],
                                                          op0=ALU.mult, op1=ALU.add))
                        ch.wait()
                    dve.wait_ge(s["gb_mm"], BC * l + c + 1)
                    v.tensor_tensor(yT[1][:, c, 0:w], ycv[:, 0:w], ps[:, 4 * BW:4 * BW + w], ALU.mult).then_inc(s["cv_done"], 1)
                    need(dve, "cv_done", BC * l + c + 1)
                    dve.sem_inc(s["yb_done"], 1)

            def merge(l, per):
                w = width[l]
                with ch.loop(0, 4, per) as r:
                    for e6 in range(6):
                        e = 24 * l + 6 * r + e6
                        b, i = e6 % 2, e6 % 3
                        dve.wait_ge(s["sg_done"], e + 1)
                        need(dve, "b_mm", e + 1)
                        o = mT[:, ds(2 * r + e6 // 3, 1), 0:w].rearrange("p o d -> p (o d)")
                        branch = ps[:, (4 * b + 2) * BW:(4 * b + 2) * BW + w]
                        if i == 0:
                            v.tensor_tensor(o, sg[b][:, 0:w], branch, ALU.mult).then_inc(s["m_evac"], 1)
                            need(dve, "m_evac", e + 1)
                            dve.sem_inc(s["mT_done"], 1)
                        else:
                            v.tensor_tensor(mtmp[:, 0:w], sg[b][:, 0:w], branch, ALU.mult).then_inc(s["m_evac"], 1)
                            need(dve, "m_evac", e + 1)
                            v.tensor_tensor(o, o, mtmp[:, 0:w], ALU.add).then_inc(s["mT_done"], 1)
                            dve.wait_ge(s["mT_done"], e + 1)

            def residual_norm(n, xt, y, gate, gamma, beta, tmp, read, done):
                v.tensor_tensor(tmp, y, gate, ALU.mult).then_inc(s[read[0]], 1)
                need(dve, *read)
                ch.inc(v.scalar_tensor_tensor(out=xt, in0=xt, scalar=ALPHA, in1=tmp, op0=ALU.mult, op1=ALU.add))
                ch.wait(s["v_turn"])
                for half in range(2):
                    ch.inc(v.bn_stats(stats[:, half, :], xt[:, half * BW:(half + 1) * BW]))
                ch.wait(s["v_turn"])
                ch.inc(v.bn_aggr(mv[:], stats[:].rearrange("p a b -> p (a b)")))
                ch.wait()
                v.tensor_scalar(sd[:, 0:1], mv[:, 1:2], 1.0, EPS, ALU.mult, ALU.add).then_inc(s["var_done"], 1)
                dve.wait_ge(s["std_done"], n + 1)
                ch.inc(v.reciprocal(rstd[:, 15:16], sd[:, 1:2]))
                ch.wait()
                ch.inc(v.tensor_scalar(xt, xt, mv[:, 0:1], rstd[:, 15:16], ALU.subtract, ALU.mult))
                ch.wait()
                ch.inc(v.tensor_tensor(xt, xt, gamma, ALU.mult))
                ch.wait()
                v.tensor_tensor(xt, xt, beta, ALU.add).then_inc(s[done[0]], 1)
                need(dve, *done)

            def out_norm(l, per):
                n0 = n_tiles[l]
                dve.wait_ge(s["rows2_in"], 64 * (l + 1))
                with ch.loop(0, live[l] // 2, per) as r:
                    for b in range(2):
                        t = 2 * r + b
                        dve.wait_ge(s["y_mm"], n0 + t + 1)
                        residual_norm(2 * n0 + t, x_all[:, ds(t, 1), :].rearrange("p o d -> p (o d)"),
                                      ps[:, 2 * b * BW:2 * (b + 1) * BW],
                                      rows2[:, ds(t // LAT, 1), :].rearrange("p o d -> p (o d)"), rows2[:, 2, :], rows2[:, 3, :],
                                      lt, ("y_read", n0 + t + 1), ("x_mid", n0 + t + 1))

            def next_h(n, t):
                dve.wait_ge(s["prow_in"], 32 * (n + 1))
                need(dve, "ht_mm", n)
                xt = x_all[:, ds(t, 1), :].rearrange("p o d -> p (o d)") if not isinstance(t, int) else x_all[:, t, :]
                ch.inc(v.scalar_tensor_tensor(out=hn, in0=prow[:, 0, :], scalar=1.0, in1=xt, op0=ALU.add, op1=ALU.mult))
                ch.wait()
                v.tensor_tensor(hn, hn, prow[:, 1, :], ALU.add).then_inc(s["hn_done"], 1)
                need(dve, "hn_done", n + 1)
                dve.sem_inc(s["v_turn"], 1)

            h_cur = ps[:, 2 * BW:4 * BW]

            def head(i, at, gather, route, l):
                j = i + PH if gather else i
                at_j = at + PH if gather else at

                def group_dots(q):
                    g = GROUPS * i + q
                    for k in range(GR):
                        dve.wait_ge(u_in[k], 16 * (g + 1))
                        v.tensor_tensor_reduce(ur[:, k, :], ur[:, k, :], h_cur, 1.0, 0.0, ALU.mult, ALU.add,
                                               dots[:, q % 2, k:k + 1]).then_inc(s["dots_done"], 1)

                def coefficients(q):
                    g = GROUPS * i + q
                    dve.wait_ge(s["gelu_done"], g + 1)
                    v.tensor_tensor(coef[:, q % 2, :], gl[:, q % 2, :], gates[:, ds(at * TOPK + q * GR, GR)], ALU.mult
                                    ).then_inc(s["coef_done"], 1)

                if gather:
                    for q in range(GROUPS):
                        group_dots(q)
                        if q:
                            coefficients(q - 1)
                if not route:
                    coefficients(GROUPS - 1)
                    return
                need(dve, "sc_copied", j + 1)
                dve.sem_inc(s["v_turn"], 1)
                for p in range(2):
                    ch.inc(v.max(v16[:, p, 0:8], sc[:, p, :]))
                ch.wait(s["v_turn"])
                for p in range(2):
                    ch.inc(v.max_index(i16[:, p, 0:8], v16[:, p, 0:8], sc[:, p, :]))
                    ch.inc(v.match_replace(sc2[:, p, :], v16[:, p, 0:8], sc[:, p, :], LOWEST))
                if gather:
                    coefficients(GROUPS - 1)
                ch.wait(s["v_turn"])
                for p in range(2):
                    ch.inc(v.max(v16[:, p, 8:16], sc2[:, p, :]))
                ch.wait(s["v_turn"])
                for p in range(2):
                    ch.inc(v.max_index(i16[:, p, 8:16], v16[:, p, 8:16], sc2[:, p, :]))
                wide = lambda a, b: a.to_broadcast([P, TOPK, TOPK])
                first = v16[:, 0, :].rearrange("p (a o) -> p a o", o=1).to_broadcast([P, TOPK, TOPK])
                second = v16[:, 1, :].rearrange("p (o a) -> p o a", o=1).to_broadcast([P, TOPK, TOPK])
                ch.inc(v.tensor_tensor(cand, first, second, ALU.add))
                ch.wait(s["v_turn"])
                flat = cand.rearrange("p a b -> p (a b)")
                flat2 = cand2.rearrange("p a b -> p (a b)")
                ch.inc(v.max(top[:, 0:8], flat))
                ch.inc(v.tensor_copy(i16f[:], i16[:]))
                ch.wait(s["v_turn"])
                ch.inc(v.max_index(pos[:, 0:8], top[:, 0:8], flat))
                ch.inc(v.match_replace(flat2, top[:, 0:8], flat, LOWEST))
                ch.inc(v.tensor_scalar(ntop[:], top[:, 0:1], -1.0, None, ALU.mult))
                ch.wait(s["v_turn"])
                v.max(top[:, 8:16], flat2).then_inc(s["top_done"], 1)
                need(dve, "top_done", j + 1)
                dve.sem_inc(s["v_turn"], 1)
                ch.inc(v.max_index(pos[:, 8:16], top[:, 8:16], flat2))
                ch.wait()
                ch.inc(v.tensor_scalar(ab[:, 0, :], pos[:], 4, None, ALU.logical_shift_right))
                ch.inc(v.tensor_scalar(ab[:, 1, :], pos[:], TOPK - 1, None, ALU.bitwise_and))
                ch.wait()
                ch.inc(v.tensor_copy(abf[:], ab[:]))
                ch.wait()
                ch.inc(v.tensor_tensor(eq, abf[:].rearrange("p a (k o) -> p (a k) o", o=1).to_broadcast([P, 2 * TOPK, TOPK]),
                                       iota16[:].rearrange("p (o k) -> p o k", o=1).to_broadcast([P, 2 * TOPK, TOPK]), ALU.is_equal))
                ch.wait()
                for p in range(2):
                    e = eq[:, p * TOPK:(p + 1) * TOPK, :]
                    ch.inc(v.tensor_tensor(e, e, i16f[:, p:p + 1, :].to_broadcast([P, TOPK, TOPK]), ALU.mult))
                ch.wait()
                ch.inc(v.tensor_reduce(sel[:].rearrange("p a k -> p (a k)"), eq, AX, ALU.add))
                ch.wait()
                ch.inc(v.scalar_tensor_tensor(out=idxf[:], in0=sel[:, 0, :], scalar=float(NK), in1=sel[:, 1, :],
                                              op0=ALU.mult, op1=ALU.add))
                ch.wait()
                v.tensor_scalar(idx[:, ds(at_j * TOPK, TOPK)], idxf[:], float(l * EXPERTS), None, ALU.add
                                ).then_inc(s["idx_done"], 1)
                need(dve, "exp_done", j + 1)
                ch.inc(v.reciprocal(tsum[:, 1:2], tsum[:, 0:1]))
                ch.wait()
                v.tensor_scalar(gates[:, ds(at_j * TOPK, TOPK)], te[:], tsum[:, 1:2], None, ALU.mult
                                ).then_inc(s["gate_done"], 1)
                need(dve, "gate_done", j + 1)

            def heads(n, t, gather, route, l):
                per = 2 * R_CHAIN if route else 0
                with ch.loop(0, PH // 2, per) as r:
                    for b in range(2):
                        head(PH * n + 2 * r + b, PH * t + 2 * r + b, gather, route, l)

            R_CHAIN = 26

            def tile_begins(n):
                ch.inc(v.tensor_copy(h_cur, hn))
                ch.wait()

            def tile_ends(n, t, l, norm0):
                need(dve, "v_used", GROUPS * PH * (n + 1))
                dve.wait_ge(s["g2_in"], 16 * (n + 1))
                dve.wait_ge(s["ln2_in"], 32 * (l + 1))
                xt = x_all[:, ds(t, 1), :].rearrange("p o d -> p (o d)") if not isinstance(t, int) else x_all[:, t, :]
                residual_norm(norm0 + t, xt, ps[:, 0:D], prow[:, 2, :], ln2[:, 0, :], ln2[:, 1, :], fx,
                              ("f_read", n + 1), ("x_new", n + 1))

            def peer(l, per):
                n0 = n_tiles[l]
                norm0 = 2 * n0 + live[l]
                next_h(n0, 0)
                heads(n0, 0, False, True, l)
                with ch.loop(0, live[l] - 1, per) as t:
                    tile_begins(n0 + t)
                    next_h(n0 + t + 1, t + 1)
                    heads(n0 + t, t, True, True, l)
                    tile_ends(n0 + t, t, l, norm0)
                t = live[l] - 1
                tile_begins(n0 + t)
                heads(n0 + t, t, True, False, l)
                tile_ends(n0 + t, t, l, norm0)

            for l in range(LAYERS):
                modulation(l)
                need(dve, "mod_mm", 12 * (l + 1))
                for b in (0, 5):
                    ch.inc(v.memset(kTc[:, :, b * P:(b + 1) * P], 0.0))
                    ch.inc(v.memset(vc[:, b, :], 0.0))
                if l == 0:
                    dve.wait_ge(s["x_in"], 32)
                    dve.wait_ge(s["small_in"], 16 * 9)
                ch.wait()
                dve.wait_ge(s["rows1_in"], 64 * (l + 1))
                if l == 0:
                    project(l, 0, TILES, True, 27)
                else:
                    project(l, 0, LAT, True, 27)
                    project(l, LAT, CTX, False, 17)
                attention(l, (29, 21))
                convolution(l)
                merge(l, 0)
                out_norm(l, 14)
                peer(l, 217)


def _rope_tables():
    import numpy as np
    quarter = HD // 4
    row = np.repeat(np.arange(LAT * P // 64), 64)
    col = np.tile(np.arange(64), LAT * P // 64)
    inv = np.power(np.float32(10000.0), -np.arange(quarter, dtype=np.float32) / np.float32(quarter)).astype(np.float32)
    ang = (np.stack([row, col], -1).astype(np.float32)[..., None] * inv).astype(np.float32)
    c, s = np.cos(ang), np.sin(ang)
    cos = np.ones((TILES * P, 2, 2, quarter), np.float32)
    sin = np.zeros((TILES * P, 2, 2, quarter), np.float32)
    cos[:LAT * P] = c[:, :, None, :]
    sin[:LAT * P, :, 0] = -s
    sin[:LAT * P, :, 1] = s
    place = lambda a: np.ascontiguousarray(a.reshape(TILES, P, HD).transpose(1, 0, 2))
    return place(cos), place(sin)


def kernel(x, c, ctx, c_ctx, w_mod, b_mod, w_in, q_norm, k_norm, conv_w, sink, w_branch, w_out, ln1_g, ln1_b,
           w_pq, sub_keys, u_tab, v_tab, ln2_g, ln2_b):
    import numpy as np
    import concourse.bacc as bacc
    from concourse.bass_utils import run_bass_kernel_spmd

    a = {n: np.asarray(v) for n, v in dict(
        x=x, ctx=ctx, b_mod=b_mod, q_norm=q_norm, k_norm=k_norm, sink=sink, ln1_g=ln1_g, ln1_b=ln1_b,
        u_tab=u_tab, v_tab=v_tab, ln2_g=ln2_g, ln2_b=ln2_b).items()}
    L = LAYERS
    w_in = np.asarray(w_in)
    rows_first = lambda w, k: w.reshape(L, k, P, -1).transpose(0, 2, 1, 3)
    cc = np.stack([np.asarray(c)[0], np.asarray(c_ctx)])
    a["cc"] = cc.reshape(2, KD, P).transpose(2, 1, 0)
    a["w_mod"] = np.asarray(w_mod).reshape(L, KD, P, 12, BW).transpose(0, 3, 2, 1, 4)
    kc = QKV - 2 * P
    a["w_qkv"] = rows_first(np.concatenate([w_in[..., 0:BW], w_in[..., BW:BW + 2 * P], w_in[..., kc:QKV],
                                            w_in[..., BW + 2 * P:kc]], -1), KD)
    cv = w_in[..., QKV:QKV + 3 * BW].reshape(L, KD, P, 3, BC, P)[:, :, :, [0, 2, 1]]
    a["w_conv"] = cv.transpose(0, 4, 3, 2, 1, 5).reshape(L, 3 * BC, P, KD, P)
    gate = w_in[..., QKV + 3 * BW:].reshape(L, KD, P, 3, KD, P).transpose(0, 4, 3, 2, 1, 5)
    branch = np.asarray(w_branch).reshape(L, 3, BC, P, KD, P).transpose(0, 4, 1, 3, 2, 5)
    a["w_gb"] = np.concatenate([gate, branch], 4).reshape(L, 3 * KD, P, KD + BC, P)
    a["w_out"] = rows_first(np.asarray(w_out), KD)
    a["w_pq"] = rows_first(np.asarray(w_pq), KD)
    a["sub_keys"] = np.asarray(sub_keys).reshape(L, 2 * PH, NK, P).transpose(0, 3, 1, 2)
    a["conv_w"] = np.asarray(conv_w).reshape(L, 3, BC, P).transpose(3, 0, 2, 1)
    a["rope_c"], a["rope_s"] = _rope_tables()

    nc = bacc.Bacc("TRN2", target_bir_lowering=False, num_devices=1)
    arrays, aps = {}, {}
    for n, v in a.items():
        arrays[f"in_{n}"] = np.ascontiguousarray(v)
        aps[n] = nc.dram_tensor(f"in_{n}", v.shape, mybir.dt.from_np(v.dtype), kind="ExternalInput").ap()
    out = nc.dram_tensor("out_0", (1, LAT * P, D), F32, kind="ExternalOutput").ap()
    hybrid_dit_peer(nc, out=out, **aps)
    r = run_bass_kernel_spmd(nc, [arrays], core_ids=[0])
    return r.results[0]["out_0"]
```

```python
from contextlib import ExitStack, contextmanager

import concourse.bass as bass
from concourse import mybir

P = 128
D = 1024
KD = D // P
LAYERS = 2
LAT, CTX = 4, 2
TILES = LAT + CTX
TOK = TILES * P
HD = 64
HEADS = 8
KV = 2
BW = HEADS * HD
BC = BW // P
QKV = 3 * BW
SCALE = HD ** -0.5
ALPHA = (2 * LAYERS) ** 0.25
EPS = 1e-6
NEG = -1e30
LOWEST = -3.4e38
MB = 512
MODS = 6 * D // MB

PH = 8
TOPK = 16
NK = 128
EXPERTS = NK * NK
UR, VR = 4, 8
GR = 4
GROUPS = TOPK // GR
LAG = 2

F32 = mybir.dt.float32
U32 = mybir.dt.uint32
ALU = mybir.AluOpType
ACT = mybir.ActivationFunctionType
AX = mybir.AxisListType.X
ds = bass.ds


class Chain:

    def __init__(self, eng, sem):
        self.eng, self.sem, self.base, self.k = eng, sem, 0, 0

    def inc(self, ins):
        ins.then_inc(self.sem, 1)
        self.k += 1

    def wait(self, alone=None):
        self.eng.wait_ge(self.sem, self.base + self.k)
        if alone is not None:
            self.eng.sem_inc(alone, 1)

    @contextmanager
    def loop(self, start, n, per):
        base, k = self.base, self.k
        with self.eng.Fori(start, start + n) as r:
            self.base, self.k = base + k + (r - start) * per, 0
            yield r
            assert self.k == per, ("increments of a round", self.k, "not", per)
        self.base, self.k = base, k + n * per


def hybrid_dit_peer(nc, x, ctx, cc, w_mod, b_mod, w_qkv, q_norm, k_norm, conv_w, sink, w_conv, w_gb,
                    w_out, ln1_g, ln1_b, w_pq, sub_keys, u_tab, v_tab, ln2_g, ln2_b, rope_c, rope_s,
                    out):
    with ExitStack() as stack:
        def sb(name, shape, dt=F32):
            return stack.enter_context(nc.sbuf_tensor(name, shape, dt))

        def sem(name):
            return stack.enter_context(nc.semaphore(name))

        x_all = sb("x_all", [P, TILES, D])
        ident = sb("ident", [P, P])
        zeros = sb("zeros", [P, P])
        iota16 = sb("iota16", [P, TOPK])
        ropec = sb("ropec", [P, TILES, HD])
        ropes = sb("ropes", [P, TILES, HD])
        mask = sb("mask", [P, LAT, 2, P])
        qn = sb("qn", [P, LAYERS, HD])
        kn = sb("kn", [P, LAYERS, HD])
        sinks = sb("sinks", [P, LAYERS, HEADS])
        nsink = sb("nsink", [P, LAYERS, HEADS])
        convw = sb("convw", [P, LAYERS, BC, 3])
        ccol = sb("ccol", [P, KD, 2])
        csig = sb("csig", [P, KD, 2])
        csilu = sb("csilu", [P, KD, 2])
        ss = sb("ss", [P, 16])
        rstd = sb("rstd", [P, 16])
        mx = sb("mx", [P, HEADS])
        nm = sb("nm", [P, HEADS])
        sums = sb("sums", [P, HEADS])
        es = sb("es", [P, HEADS])
        rec = sb("rec", [P, HEADS])
        stats = sb("stats", [P, 2, 6])
        mv = sb("mv", [P, 2])
        sd = sb("sd", [P, 2])
        AK = 170
        arena = sb("arena", [P, AK * 256])

        def region(kb, *shape):
            n = 1
            for s in shape:
                n *= s
            a0 = int(kb * 256)
            assert a0 + n <= AK * 256, (kb, shape)
            v = arena[:, a0:a0 + n]
            if len(shape) == 2:
                return v.rearrange("p (a b) -> p a b", b=shape[1])
            if len(shape) == 3:
                return v.rearrange("p (a b c) -> p a b c", b=shape[1], c=shape[2])
            return v

        xT = region(0, KD, TOK)
        wqkv = region(24, KD, QKV)
        rows1 = region(72, 4, D)
        xm = region(88, D)
        xTs = region(92, KD, P)
        qTa = region(96, BC, TOK)
        qTc = region(108, BC, TOK)
        kTa = region(120, KV, TOK)
        kTc = region(126, KV, 8 * P)
        va = region(134, TILES, P)
        vc = region(137, 8, P)
        pq_a = region(141, BW)
        pkv = region(143, BW)
        pq_c = region(145, BW)
        rt = region(147, BW)
        rq_a = region(149, BW)
        rq_c = region(151, BW)
        rk = region(153, BW)
        wmod = [[region(a0 + 16 * b, KD, MB) for b in range(2)] for a0 in (88, 0)]
        modrow = [region(a0, 2, MB)[0:2] for a0 in (145, 32)]
        brow = [region(a0, 2, MB)[0:2] for a0 in (141, 36)]
        qz = [region(72 + 4 * b, HEADS, P) for b in range(2)]
        pr = [region(80 + 3 * b, TILES * P) for b in range(2)]
        pts = [region(86 + 3 * b, TILES, P) for b in range(2)]
        ysb = [region(92 + 2 * b, BW) for b in range(2)]
        yT = [region(24 + 12 * b, BC, TOK) for b in range(3)]
        wcv = [region(154 + 4 * b, KD, P) for b in range(4)]
        zb = region(72, 772)
        xbs = region(76, TOK)
        ycv = region(79, TOK)
        gbw = [region(60 + 6 * b, KD + BC, P) for b in range(2)]
        sg = [region(82 + 3 * b, TOK) for b in range(2)]
        mtmp = region(88, TOK)
        mT = region(96, KD, TOK)
        wout = region(120, KD, D)
        rows2 = region(154, 4, D)
        lt = region(72, D)

        wpq = region(0, PH, KD * 2 * P)
        keys = region(64, 2 * PH, P)
        fx = region(72, D)
        prow = region(76, 3, D)
        ln2 = region(88, 2, D)
        ur = region(96, UR, D)
        vr = region(112, VR, D)
        hn = region(144, D)
        hT = region(148, KD, P)
        dg = region(152, VR, P)
        q_sb = region(156, 2, P)
        qT_sb = region(157, 2, P)
        sc = region(158, 2, P)
        sc2 = region(159, 2, P)
        cand = region(160, TOPK, TOPK)
        cand2 = region(161, TOPK, TOPK)
        eq = region(162, 2 * TOPK, TOPK)
        gates = region(164, PH * TOPK)
        v16 = sb("v16", [P, 2, TOPK])
        i16 = sb("i16", [P, 2, TOPK], U32)
        i16f = sb("i16f", [P, 2, TOPK])
        top = sb("top", [P, TOPK])
        pos = sb("pos", [P, TOPK], U32)
        ab = sb("ab", [P, 2, TOPK], U32)
        abf = sb("abf", [P, 2, TOPK])
        sel = sb("sel", [P, 2, TOPK])
        idxf = sb("idxf", [P, TOPK])
        ntop = sb("ntop", [P, 1])
        te = sb("te", [P, TOPK])
        tsum = sb("tsum", [P, 2])
        idx = region(164.5, PH * TOPK).bitcast(U32)
        ist = [sb(f"ist{b}", [P, TOPK], U32) for b in range(2)]
        dots = sb("dots", [P, 2, GR])
        gl = sb("gl", [P, 2, GR])
        coef = sb("coef", [P, 2, GR])

        ps = stack.enter_context(nc.psum_tensor("ps", [P, 8 * BW], F32))

        def bank(b, lo=0, hi=BW):
            return ps[:, b * BW + lo:b * BW + hi]

        mods = nc.dram_tensor("mods", [LAYERS, 2, 6 * D], F32).ap()
        SH1, SC1, G1, SH2, SC2, G2 = range(6)

        def mod_row(l, kind, which):
            return mods[l, kind:kind + 1, which * D:(which + 1) * D].partition_broadcast(P)

        def row_of(t):
            return t.partition_broadcast(P)

        s = {n: sem(n) for n in (
            "x_in small_in ident_made consts_made wqkv_in c_in c_sig c_silu bmod_in0 bmod_in1 wmod_in0 wmod_in1 "
            "mod_mm mod_done mod_out0 mod_out1 rows1_in xm_done xt_mm xts_done xt_copied qa_mm kv_mm qc_mm qa_sb kv_sb "
            "qc_sb ss_done sd_done rqa_done rk_done rqc_done ta_mm tk_mm tc_mm qTa_done kT_done qTc_done "
            "v_chain pads_done qz_done s_mm nm_done p_done pt_mm pta_done ptb_done pv_mm es_in es_done y_done yt_mm yT_done "
            "wcv_in0 wcv_in1 wcv_in2 wcv_in3 cv_used xb_mm gc_mm gb_mm xbs_done cv_done yb_done "
            "gbw_in0 gbw_in1 g_mm b_mm sg_done m_evac mT_done wout_in rows2_in y_mm var_done std_done y_read x_mid "
            "wpq_in keys_in ln2_in prow_in g2_in hn_done ht_mm hT_done q_mm q_copied qT_mm qT_copied sc_mm sc_copied "
            "top_done exp_done idx_done gate_done dots_done gelu_done coef_done diag_done v_used pool_turn "
            "v_turn idx_staged f_read x_new x_out").split()}
        u_in = [sem(f"u_in{k}") for k in range(UR)]
        v_in = [sem(f"v_in{k}") for k in range(VR)]
        CREDIT = {"p_done": 2, "pta_done": 1, "ptb_done": 1, "pv_mm": 2, "y_done": 1, "yT_done": 1,
                  "m_evac": 2, "b_mm": 2, "dots_done": UR, "v_used": VR, "mod_done": 2, "mod_out0": 16, "mod_out1": 16,
                  "mod_mm": 2, "xts_done": 1, "xt_mm": 1, "xt_copied": 1, "qa_sb": 1, "kv_sb": 1, "qc_sb": 1,
                  "qa_mm": 1, "kv_mm": 1, "qc_mm": 1, "rqa_done": 1, "rk_done": 1, "rqc_done": 1,
                  "ta_mm": 1, "tk_mm": 1, "tc_mm": 1, "qTa_done": 1, "kT_done": 1, "qTc_done": 1,
                  "y_read": 2, "cv_done": 1, "hT_done": 1, "ht_mm": 1, "q_mm": 1, "q_copied": 1, "qT_mm": 1,
                  "qT_copied": 1, "sc_mm": 1, "sc_copied": 1, "top_done": 1, "idx_done": 1, "f_read": 1,
                  "idx_staged": 0, "x_new": 1, "hn_done": 1, "exp_done": 1, "yt_mm": 1, "gate_done": 1}
        OWNER = {
            "pe": "pv_mm b_mm v_used mod_mm xt_mm qa_mm kv_mm qc_mm ta_mm tk_mm tc_mm ht_mm q_mm qT_mm sc_mm yt_mm",
            "act": "p_done ptb_done yT_done xts_done qa_sb kv_sb qc_sb qTa_done kT_done qTc_done hT_done q_copied "
                   "qT_copied sc_copied exp_done",
            "dve": "pta_done y_done m_evac dots_done mod_done xt_copied rqa_done rk_done rqc_done y_read cv_done "
                   "top_done idx_done f_read x_new hn_done gate_done",
            "sp": "mod_out0 mod_out1"}

        def give_credits(eng, who):
            for n in OWNER[who].split():
                if CREDIT[n]:
                    eng.sem_inc(s[n], CREDIT[n])

        def need(eng, name, n):
            eng.wait_ge(s[name], n + CREDIT.get(name, 0))

        MOD_HEADS = 5
        n_att = [HEADS * 0, 12]
        n_tiles = [0, TILES]
        width = [TOK, LAT * P]
        live = [TILES, LAT]

        block = stack.enter_context(nc.Block())

        @block.sync
        def _(sp):
            sp.dma_start(ccol[:], cc).then_inc(s["c_in"], 16)
            give_credits(sp, "sp")

            def modulation(l):
                def load(e, b):
                    need(sp, "mod_mm", MODS * l + e - 1)
                    need(sp, "mod_done", MODS * l + e - 1)
                    sp.dma_start(wmod[l][b], w_mod[l, ds(e, 1)].rearrange("o p k n -> p (o k) n")
                                 ).then_inc(s[f"wmod_in{b}"], 16)
                    sp.dma_start(brow[l][:, b, :], b_mod[l:l + 1, ds(e * MB, MB)].partition_broadcast(2)[:, 0, :]
                                 ).then_inc(s[f"bmod_in{b}"], 16)

                def store(e, b):
                    need(sp, "mod_done", MODS * l + e + 1)
                    sp.dma_start(mods[l, :, ds(e * MB, MB)], modrow[l][:, b, :]).then_inc(s[f"mod_out{b}"], 16)

                for b in range(2):
                    load(b, b)
                with sp.Fori(1, MODS // 2) as r:
                    for b in range(2):
                        load(2 * r + b, b)
                        store(2 * r + (b - 2), b)
                for b in range(2):
                    store(MODS - 2 + b, b)
                for b in range(2):
                    need(sp, f"mod_out{b}", 8 * MODS * (l + 1))

            def mod_rows(l):
                for kind in range(2):
                    for j, which in enumerate((SC1, SH1)):
                        sp.dma_start(rows1[:, 2 * kind + j, :], mod_row(l, kind, which)[:, 0, :]
                                     ).then_inc(s["rows1_in"], 16)

            def mixer(l):
                if l == 1:
                    need(sp, "q_mm", PH * (TILES - 1) + MOD_HEADS)
                    modulation(l)
                    need(sp, "sc_mm", PH * TILES)
                    sp.dma_start(wqkv, w_qkv[l]).then_inc(s["wqkv_in"], 16)
                    need(sp, "x_new", TILES)
                    mod_rows(l)
                else:
                    sp.dma_start(x_all[:, 0:LAT, :], x.rearrange("o (t p) d -> p (o t) d", p=P)).then_inc(s["x_in"], 16)
                    sp.dma_start(x_all[:, LAT:TILES, :], ctx.rearrange("o (t p) d -> p (o t) d", p=P)).then_inc(s["x_in"], 16)
                    for dst, src in ((ropec[:], rope_c), (ropes[:], rope_s), (convw[:], conv_w)):
                        sp.dma_start(dst, src).then_inc(s["small_in"], 16)
                    for dst, src in ((qn, q_norm), (kn, k_norm), (sinks, sink)):
                        for ll in range(LAYERS):
                            sp.dma_start(dst[:, ll, :], row_of(src[ll:ll + 1, :])[:, 0, :]).then_inc(s["small_in"], 16)
                    modulation(l)
                    mod_rows(l)
                    sp.dma_start(wqkv, w_qkv[l]).then_inc(s["wqkv_in"], 16)
                need(sp, "yT_done", n_att[l] + 2 * live[l])
                for e in range(3 * BC):
                    if e >= 4:
                        sp.wait_ge(s["cv_used"], 3 * BC * l + e - 3)
                    sp.dma_start(wcv[e % 4], w_conv[l, e]).then_inc(s[f"wcv_in{e % 4}"], 16)
                sp.dma_start(wout, w_out[l]).then_inc(s["wout_in"], 16)
                with sp.Fori(0, 12) as r:
                    for b in range(2):
                        need(sp, "b_mm", 24 * l + 2 * r + b - 1)
                        sp.dma_start(gbw[b], w_gb[l, ds(2 * r + b, 1)].rearrange("o p k n -> p (o k) n")
                                     ).then_inc(s[f"gbw_in{b}"], 16)
                sp.wait_ge(s["cv_used"], 3 * BC * (l + 1))
                for j, src in enumerate((mod_row(l, 0, G1), mod_row(l, 1, G1), row_of(ln1_g[l:l + 1]), row_of(ln1_b[l:l + 1]))):
                    sp.dma_start(rows2[:, j, :], src[:, 0, :]).then_inc(s["rows2_in"], 16)

            def peer(l):
                n0 = n_tiles[l]
                sp.wait_ge(s["mT_done"], 24 * (l + 1))
                sp.dma_start(prow[:, 0, :], mod_row(l, 0, SC2)[:, 0, :]).then_inc(s["prow_in"], 16)
                sp.dma_start(prow[:, 1, :], mod_row(l, 0, SH2)[:, 0, :]).then_inc(s["prow_in"], 16)
                sp.dma_start(wpq, w_pq[l]).then_inc(s["wpq_in"], 16)
                sp.dma_start(keys, sub_keys[l]).then_inc(s["keys_in"], 16)
                for j, src in enumerate((ln2_g, ln2_b)):
                    sp.dma_start(ln2[:, j, :], row_of(src[l:l + 1])[:, 0, :]).then_inc(s["ln2_in"], 16)

                def next_rows(t):
                    need(sp, "hn_done", n0 + t)
                    for j, which in enumerate((SC2, SH2)):
                        sp.dma_start(prow[:, j, :], mods[l, ds(t // LAT, 1), which * D:(which + 1) * D].partition_broadcast(P)[:, 0, :]
                                     ).then_inc(s["prow_in"], 16)

                def g2_row(t):
                    need(sp, "f_read", n0 + t)
                    sp.dma_start(prow[:, 2, :], mods[l, ds(t // LAT, 1), G2 * D:(G2 + 1) * D].partition_broadcast(P)[:, 0, :]
                                 ).then_inc(s["g2_in"], 16)

                def store(t):
                    need(sp, "x_new", n0 + t + 1)
                    sp.dma_start(out[0, ds(t * P, P), :], x_all[:, ds(t, 1), :].rearrange("p o d -> p (o d)")
                                 ).then_inc(s["x_out"], 16)

                next_rows(1)
                g2_row(0)
                with sp.Fori(1, live[l] - 1) as t:
                    next_rows(t + 1)
                    g2_row(t)
                    if l == 1:
                        store(t - 1)
                g2_row(live[l] - 1)
                if l == 1:
                    store(LAT - 2)

            for l in range(LAYERS):
                mixer(l)
                peer(l)
            need(sp, "x_new", n_tiles[1] + LAT)
            sp.dma_start(out[0, (LAT - 1) * P:LAT * P, :], x_all[:, LAT - 1, :]).then_inc(s["x_out"], 16)
            sp.wait_ge(s["x_out"], 16 * LAT)

        @block.gpsimd
        def _(pool):
            nc.gpsimd.memset(ident[:], 1.0).then_inc(s["ident_made"], 1)
            pool.wait_ge(s["ident_made"], 1)
            nc.gpsimd.affine_select(out=ident[:], in_=ident[:], compare_op=ALU.is_equal, fill=0.0, base=0,
                                    pattern=[[-1, P]], channel_multiplier=1).then_inc(s["ident_made"], 1)
            nc.gpsimd.memset(zeros[:], 0.0).then_inc(s["consts_made"], 1)
            nc.gpsimd.iota(iota16[:], [[1, TOPK]], base=0, channel_multiplier=0,
                           allow_small_or_imprecise_dtypes=True).then_inc(s["consts_made"], 1)
            nc.gpsimd.memset(mask[:], 0.0).then_inc(s["consts_made"], 1)
            pool.wait_ge(s["consts_made"], 3)
            for t in range(LAT):
                for side in range(2):
                    m = mask[:, t, side, :]
                    if (t, side) in ((0, 0), (LAT - 1, 1)):
                        nc.gpsimd.memset(m, NEG).then_inc(s["consts_made"], 1)
                    else:
                        sign = 1 if side == 0 else -1
                        nc.gpsimd.affine_select(out=m, in_=m, compare_op=ALU.is_ge, fill=NEG, base=0,
                                                pattern=[[sign, P]], channel_multiplier=-sign
                                                ).then_inc(s["consts_made"], 1)

            u_rows = u_tab.rearrange("l e d -> (l e) d")
            v_rows = v_tab.rearrange("l e d -> (l e) d")

            def head(i, i_idx, b):
                need(pool, "idx_done", i + 1)
                nc.gpsimd.tensor_copy(ist[b][:], idx[:, ds(i_idx * TOPK, TOPK)]).then_inc(s["idx_staged"], 1)
                pool.wait_ge(s["idx_staged"], i + 1)
                for q in range(GROUPS):
                    g = GROUPS * i + q
                    for k in range(GR):
                        need(pool, "dots_done", UR * (g - 1) + k + 1)
                        pool.sem_inc(s["pool_turn"], 1)
                        nc.gpsimd.indirect_dma_start(
                            ur[:, k, :], None, u_rows,
                            bass.IndirectOffsetOnAxis(ap=ist[b][:, q * GR + k:q * GR + k + 1], axis=0)
                        ).then_inc(u_in[k], 16)
                    for k in range(GR):
                        need(pool, "v_used", GR * (g - 2) + k + 1)
                        pool.sem_inc(s["pool_turn"], 1)
                        nc.gpsimd.indirect_dma_start(
                            vr[:, GR * (q % 2) + k, :], None, v_rows,
                            bass.IndirectOffsetOnAxis(ap=ist[b][:, q * GR + k:q * GR + k + 1], axis=0)
                        ).then_inc(v_in[GR * (q % 2) + k], 16)

            for l in range(LAYERS):
                i0 = PH * n_tiles[l]
                with pool.Fori(0, live[l]) as t:
                    with pool.Fori(0, PH // 2) as r:
                        for b in range(2):
                            head(i0 + PH * t + 2 * r + b, 2 * r + b, b)

        @block.tensor
        def _(pe):
            give_credits(pe, "pe")
            pe.wait_ge(s["ident_made"], 2)
            pe.wait_ge(s["consts_made"], 3 + 2 * LAT)

            def mm(o, lhsT, rhs, first=True, last=True):
                return nc.tensor.matmul(o, lhsT, rhs, start=first, stop=last, skip_group_check=True)

            def mod_block(l, r, b):
                pe.wait_ge(s[f"wmod_in{b}"], 16 * (MODS // 2 * l + r + 1))
                need(pe, "mod_done", MODS * l + 2 * r + b - 1)
                for k in range(KD):
                    m = mm(bank(4 + b)[0:2, 0:MB], csilu[:, k, :], wmod[l][b][:, k, :], k == 0, k == KD - 1)
                m.then_inc(s["mod_mm"], 1)

            def modulation(l):
                pe.wait_ge(s["c_silu"], 1)
                with pe.Fori(0, MODS // 2) as r:
                    for b in range(2):
                        mod_block(l, r, b)

            def project(l, lo, n, with_q):
                with pe.Fori(lo, lo + n) as t:
                    i = TILES * l + t
                    pe.wait_ge(s["xm_done"], i + 1)
                    need(pe, "xts_done", i)
                    for k in range(KD):
                        m = nc.tensor.transpose(bank(0, k * P, (k + 1) * P), xm[:, k * P:(k + 1) * P], ident[:])
                    m.then_inc(s["xt_mm"], 1)
                    need(pe, "xts_done", i + 1)
                    pe.wait_ge(s["wqkv_in"], 16 * (l + 1))
                    for b, name, copied in ((1, "kv_mm", "kv_sb"), (0, "qa_mm", "qa_sb"), (2, "qc_mm", "qc_sb")):
                        if b != 1 and not with_q:
                            continue
                        need(pe, copied, i)
                        for k in range(KD):
                            m = mm(bank(2 + b), xTs[:, k, :], wqkv[:, k, b * BW:(b + 1) * BW], k == 0, k == KD - 1)
                        m.then_inc(s[name], 1)
                    for src, done, b, name, copied in ((rk, "rk_done", 7, "tk_mm", "kT_done"), (rq_a, "rqa_done", 5, "ta_mm", "qTa_done"),
                                                       (rq_c, "rqc_done", 6, "tc_mm", "qTc_done")):
                        if b != 7 and not with_q:
                            continue
                        need(pe, done, i + 1)
                        need(pe, copied, i)
                        for k in range(BC):
                            m = nc.tensor.transpose(bank(b, k * P, (k + 1) * P), src[:, k * P:(k + 1) * P], ident[:])
                        m.then_inc(s[name], 1)

            def attend(u, t, branch, lat, yt_before):
                kT, v = (kTa, va) if branch == 0 else (kTc, vc)
                local = lat and branch == 1

                def scores(h):
                    hh = HEADS * u + h
                    o = 2 * (h % 2)
                    g = h // (HEADS // KV)
                    need(pe, "p_done", hh - 1)
                    q = qz[branch][:, h, :]
                    if branch == 0:
                        if lat:
                            mm(bank(o), q, kT[:, g, 0:BW])
                        m = mm(bank(o + 1, 0, 2 * P), q, kT[:, g, BW:TOK])
                    else:
                        if lat:
                            mm(bank(o, P, BW), q, kT[:, g, ds(t * P, 3 * P)])
                        m = mm(bank(o + 1, 0, 2 * P), q, kT[:, g, 6 * P:8 * P])
                    m.then_inc(s["s_mm"], 1)

                first = 0 if lat and branch == 0 else 1 if lat else 4

                def turn_p(h):
                    hh = HEADS * u + h
                    need(pe, "p_done", hh + 1)
                    need(pe, "pta_done", hh)
                    need(pe, "ptb_done", hh)
                    for j in range(first, TILES):
                        m = nc.tensor.transpose(bank(4 + j // 4, (j % 4) * P, (j % 4 + 1) * P),
                                                pr[h % 2][:, j * P:(j + 1) * P], ident[:])
                    m.then_inc(s["pt_mm"], 1)

                def values(h):
                    hh = HEADS * u + h
                    g = h // (HEADS // KV)
                    need(pe, "pta_done", hh + 1)
                    need(pe, "ptb_done", hh + 1)
                    if h == 0:
                        need(pe, "y_done", u)
                    for j in range(first, TILES):
                        if branch == 0:
                            vj = v[:, j, g * HD:(g + 1) * HD]
                        elif j < 4:
                            vj = v[:, ds(t + (j - 1), 1), g * HD:(g + 1) * HD].rearrange("p o d -> p (o d)")
                        else:
                            vj = v[:, j + 2, g * HD:(g + 1) * HD]
                        m = mm(bank(6, h * HD, (h + 1) * HD), pts[h % 2][:, j, :], vj, j == first, j == TILES - 1)
                    m.then_inc(s["pv_mm"], 1)

                pe.wait_ge(s["qz_done"], u + 1)
                for h in range(HEADS + 2):
                    if h < HEADS:
                        scores(h)
                    if h == 2 and yt_before:
                        turn_y(u - 1, 1 - branch)
                    if h >= 2:
                        values(h - 2)
                    if 1 <= h <= HEADS:
                        turn_p(h - 1)

            def turn_y(u, branch):
                need(pe, "y_done", u + 1)
                need(pe, "yT_done", u)
                for k in range(BC):
                    m = nc.tensor.transpose(bank(7, k * P, (k + 1) * P), ysb[branch][:, k * P:(k + 1) * P], ident[:])
                m.then_inc(s["yt_mm"], 1)

            def attention(l):
                for lo, n, lat in ((0, LAT, True), (LAT, CTX, False))[:2 - l]:
                    with pe.Fori(lo, lo + n) as t:
                        u = n_att[l] + 2 * t
                        attend(u, t, 0, lat, False)
                        attend(u + 1, t, 1, lat, True)
                        turn_y(u + 1, 1)

            def over_tokens(l, b, lhs, rhs, n):
                for k in range(n):
                    m = mm(bank(b), lhs(k), rhs[:, k, 0:LAT * P], k == 0, k == n - 1)
                if l == 0:
                    for k in range(n):
                        m = mm(bank(b + 1, 0, CTX * P), lhs(k), rhs[:, k, LAT * P:TOK], k == 0, k == n - 1)
                return m

            def convolution(l):
                for c in range(BC):
                    if c or l:
                        need(pe, "cv_done", BC * l + c)
                    for j, name in enumerate(("xb_mm", "gc_mm", "gb_mm")):
                        e = 3 * c + j
                        pe.wait_ge(s[f"wcv_in{e % 4}"], 16 * (3 * l + e // 4 + 1))
                        m = over_tokens(l, 2 * j, lambda k: wcv[e % 4][:, k, :], xT, KD)
                        m.then_inc(s[name], 1)
                        pe.wait_ge(s[name], BC * l + c + 1)
                        pe.sem_inc(s["cv_used"], 1)

            def merge(l):
                need(pe, "cv_done", BC * (l + 1))
                pe.wait_ge(s["yb_done"], BC * (l + 1))
                with pe.Fori(0, 4) as r:
                    for e6 in range(6):
                        e = 24 * l + 6 * r + e6
                        b, i = e6 % 2, e6 % 3
                        pe.wait_ge(s[f"gbw_in{b}"], 16 * (12 * l + 3 * r + e6 // 2 + 1))
                        need(pe, "m_evac", e - 1)
                        over_tokens(l, 4 * b, lambda k: gbw[b][:, k, :], xT, KD).then_inc(s["g_mm"], 1)
                        over_tokens(l, 4 * b + 2, lambda k: gbw[b][:, KD + k, :], yT[i], BC).then_inc(s["b_mm"], 1)

            def project_out(l):
                pe.wait_ge(s["mT_done"], 24 * (l + 1))
                pe.wait_ge(s["wout_in"], 16 * (l + 1))
                for t in range(live[l]):
                    need(pe, "y_read", n_tiles[l] + t - 1)
                    for half in range(2):
                        for k in range(KD):
                            m = mm(bank(2 * (t % 2) + half), mT[:, k, t * P:(t + 1) * P],
                                   wout[:, k, half * BW:(half + 1) * BW], k == 0, k == KD - 1)
                    m.then_inc(s["y_mm"], 1)

            def turn_h(n):
                need(pe, "hn_done", n + 1)
                need(pe, "hT_done", n)
                for k in range(KD):
                    m = nc.tensor.transpose(bank(4, k * P, (k + 1) * P), hn[:, k * P:(k + 1) * P], ident[:])
                m.then_inc(s["ht_mm"], 1)

            def head(i, h, h_j, n_j, gather, route, clears=None, turns=False, mod=None):
                j = i + LAG if gather else i

                def sum_group(q):
                    g = GROUPS * i + q
                    for k in range(GR):
                        slot = GR * (q % 2) + k
                        pe.wait_ge(v_in[slot], 16 * (2 * i + q // 2 + 1))
                        pe.wait_ge(s["diag_done"], GR * g + k + 1)
                        mm(bank(0), dg[:, slot, :], vr[:, slot, 0:BW], False, True)
                        mm(bank(1), dg[:, slot, :], vr[:, slot, BW:D], False, True).then_inc(s["v_used"], 1)

                if route:
                    if turns:
                        turn_h(n_j)
                    need(pe, "hT_done", n_j + 1)
                    need(pe, "q_copied", j)
                    for k in range(KD):
                        w = wpq[:, ds(h_j, 1), k * 2 * P:(k + 1) * 2 * P].rearrange("p o n -> p (o n)")
                        m = mm(bank(6, 0, 2 * P), hT[:, k, :], w, k == 0, k == KD - 1)
                    m.then_inc(s["q_mm"], 1)
                    need(pe, "q_copied", j + 1)
                    need(pe, "qT_copied", j)
                    for k in range(2):
                        m = nc.tensor.transpose(bank(6, (2 + k) * P, (3 + k) * P), q_sb[:, k, :], ident[:])
                    m.then_inc(s["qT_mm"], 1)
                    need(pe, "qT_copied", j + 1)
                    need(pe, "sc_copied", j)
                    for k in range(2):
                        m = mm(bank(7, k * P, (k + 1) * P), qT_sb[:, k, :],
                               keys[:, ds(2 * h_j + k, 1), :].rearrange("p o n -> p (o n)"))
                    m.then_inc(s["sc_mm"], 1)
                if gather:
                    if clears is not None:
                        clear_sum(clears)
                    for q in range(GROUPS):
                        if mod is not None and q > 0:
                            r, part = mod
                            m = 3 * part + q - 1
                            mod_block(1, 3 * r + m // 2, m % 2)
                        sum_group(q)

            def tile(n, last=False, mod=False):
                for h in range(2):
                    head(PH * n + h, h, h + LAG, n, True, True, n if h == 0 else None)
                with pe.Fori(1, PH // 2 - 1) as r:
                    for b in range(2):
                        h = 2 * r + b
                        head(PH * n + h, h, h + LAG, n, True, True, mod=(r - 1, b) if mod else None)
                for h in range(PH - 2, PH):
                    head(PH * n + h, h, h + LAG - PH, n + 1, True, not last, turns=not last and h == PH - 2)

            def clear_sum(n):
                need(pe, "f_read", n)
                for b in range(2):
                    mm(bank(b), zeros[:], mask[:, 0:2, :, :].rearrange("p a b c -> p (a b c)"), True, False)

            def peer(l):
                n0 = n_tiles[l]
                pe.wait_ge(s["wpq_in"], 16 * (l + 1))
                pe.wait_ge(s["keys_in"], 16 * (l + 1))
                for h in range(LAG):
                    head(PH * n0 + h, h, h, n0, False, True, turns=h == 0)
                with pe.Fori(0, live[l] - 1) as t:
                    tile(n0 + t)
                tile(n0 + live[l] - 1, True, l == 0)

            modulation(0)
            for l in range(LAYERS):
                if l == 0:
                    project(l, 0, TILES, True)
                else:
                    project(l, 0, LAT, True)
                    project(l, LAT, CTX, False)
                attention(l)
                convolution(l)
                merge(l)
                project_out(l)
                peer(l)

        @block.scalar
        def _(act):
            give_credits(act, "act")

            def copy(o, i, name):
                nc.scalar.copy(o, i).then_inc(s[name], 1)

            act.wait_ge(s["c_in"], 16)
            nc.scalar.activation(csig[:], ccol[:], ACT.Sigmoid).then_inc(s["c_sig"], 1)

            def project(l, lo, n, with_q):
                with act.Fori(lo, lo + n) as t:
                    i = TILES * l + t
                    need(act, "xt_mm", i + 1)
                    need(act, "xt_copied", i)
                    need(act, "kv_mm", i)
                    if with_q:
                        need(act, "qa_mm", i)
                        need(act, "qc_mm", i)
                    copy(xTs.rearrange("p a b -> p (a b)"), ps[:, 0:D], "xts_done")
                    for src, dst, m, done, name in ((3, pkv, "kv_mm", "rk_done", "kv_sb"), (2, pq_a, "qa_mm", "rqa_done", "qa_sb"),
                                                    (4, pq_c, "qc_mm", "rqc_done", "qc_sb")):
                        if src != 3 and not with_q:
                            continue
                        need(act, m, i + 1)
                        need(act, done, i)
                        copy(dst, bank(src), name)
                    act.wait_ge(s["ss_done"], i + 1)
                    nc.scalar.activation(rstd[:, 0:10], ss[:, 0:10], ACT.Sqrt).then_inc(s["sd_done"], 1)
                    need(act, "tk_mm", i + 1)
                    col = lambda b: ds(b * P, P)
                    kv = bank(7).rearrange("p (g c) -> p g c", g=4)
                    nc.scalar.copy(kTa[:, :, col(t)], kv[:, 0:2, :])
                    copy(kTc[:, :, col(t + 1 + t // LAT)], kv[:, 2:4, :], "kT_done")
                    if with_q:
                        for b, dst, m, name in ((5, qTa, "ta_mm", "qTa_done"), (6, qTc, "tc_mm", "qTc_done")):
                            need(act, m, i + 1)
                            copy(dst[:, :, col(t)], bank(b).rearrange("p (g c) -> p g c", g=4), name)

            def attend(u, t, branch, lat, l, yt_before):
                first = 0 if lat and branch == 0 else 1 if lat else 4

                def exp(h):
                    hh = HEADS * u + h
                    o = 2 * BW * (h % 2)
                    act.wait_ge(s["nm_done"], hh + 1)
                    nc.scalar.activation(pr[h % 2][:, first * P:TOK], ps[:, o + first * P:o + TOK], ACT.Exp,
                                         bias=nm[:, h:h + 1], scale=SCALE, accum_out=sums[:, h:h + 1]
                                         ).then_inc(s["p_done"], 1)

                def evacuate(h):
                    hh = HEADS * u + h
                    act.wait_ge(s["pt_mm"], hh + 1)
                    need(act, "pv_mm", hh - 1)
                    copy(pts[h % 2][:, 4:6, :].rearrange("p a b -> p (a b)"), bank(5, 0, 2 * P), "ptb_done")

                for h in range(HEADS + 1):
                    if h < HEADS:
                        exp(h)
                    if h == 3 and yt_before:
                        evacuate_y(u - 1, t, 1 - branch)
                    if h >= 1:
                        evacuate(h - 1)
                if branch == 1:
                    act.wait_ge(s["es_in"], (u + 1) // 2)
                    nc.scalar.activation(es[:], es[:], ACT.Exp).then_inc(s["es_done"], 1)

            def evacuate_y(u, t, branch):
                need(act, "yt_mm", u + 1)
                copy(yT[2 * branch][:, :, ds(t * P, P)], bank(7).rearrange("p (a b) -> p a b", b=P), "yT_done")

            def attention(l):
                for lo, n, lat in ((0, LAT, True), (LAT, CTX, False))[:2 - l]:
                    with act.Fori(lo, lo + n) as t:
                        u = n_att[l] + 2 * t
                        attend(u, t, 0, lat, l, False)
                        attend(u + 1, t, 1, lat, l, True)
                        evacuate_y(u + 1, t, 1)

            def convolution(l):
                for c in range(BC):
                    act.wait_ge(s["xb_mm"], BC * l + c + 1)
                    need(act, "cv_done", BC * l + c)
                    copy(xbs[:, 0:width[l]], ps[:, 0:width[l]], "xbs_done")

            def merge(l):
                with act.Fori(0, 4) as r:
                    for e6 in range(6):
                        e = 24 * l + 6 * r + e6
                        b = e6 % 2
                        act.wait_ge(s["g_mm"], e + 1)
                        need(act, "m_evac", e - 1)
                        nc.scalar.activation(sg[b][:, 0:width[l]], ps[:, 4 * b * BW:4 * b * BW + width[l]],
                                             ACT.Sigmoid).then_inc(s["sg_done"], 1)

            def std(n):
                act.wait_ge(s["var_done"], n + 1)
                nc.scalar.activation(sd[:, 1:2], sd[:, 0:1], ACT.Sqrt).then_inc(s["std_done"], 1)

            def copy_hT(n):
                need(act, "ht_mm", n + 1)
                need(act, "q_mm", PH * n)
                copy(hT.rearrange("p a b -> p (a b)"), ps[:, 4 * BW:6 * BW], "hT_done")

            def head(i, gather, route, turns=None, norm=None):
                j = i + LAG if gather else i

                def gelu(q):
                    g = GROUPS * i + q
                    need(act, "dots_done", GR * (g + 1))
                    nc.scalar.activation(gl[:, q % 2, :], dots[:, q % 2, :], ACT.Gelu).then_inc(s["gelu_done"], 1)

                def diagonals(q):
                    g = GROUPS * i + q
                    act.wait_ge(s["coef_done"], g + 1)
                    need(act, "v_used", GR * (g - 1))
                    for k in range(GR):
                        nc.scalar.activation(dg[:, GR * (q % 2) + k, :], ident[:], ACT.Copy,
                                             scale=coef[:, q % 2, k:k + 1]).then_inc(s["diag_done"], 1)

                if gather:
                    gelu(0)
                    diagonals(0)
                if route:
                    if turns is not None:
                        copy_hT(turns)
                    need(act, "q_mm", j + 1)
                    copy(q_sb.rearrange("p a b -> p (a b)"), bank(6, 0, 2 * P), "q_copied")
                    need(act, "qT_mm", j + 1)
                    need(act, "sc_mm", j)
                    copy(qT_sb.rearrange("p a b -> p (a b)"), bank(6, 2 * P, 4 * P), "qT_copied")
                    need(act, "sc_mm", j + 1)
                    need(act, "top_done", j)
                    copy(sc.rearrange("p a b -> p (a b)"), bank(7, 0, 2 * P), "sc_copied")
                if gather:
                    gelu(1)
                    if norm is not None:
                        std(norm)
                    diagonals(1)
                    gelu(2)
                    diagonals(2)
                if route:
                    need(act, "top_done", j + 1)
                    nc.scalar.activation(te[:], top[:], ACT.Exp, bias=ntop[:], accum_out=tsum[:, 0:1]
                                         ).then_inc(s["exp_done"], 1)
                if gather:
                    gelu(3)
                    diagonals(3)

            def tile(n, norm=None, last=False):
                for h in range(2):
                    head(PH * n + h, True, True, None, norm if h == 0 else None)
                with act.Fori(1, PH // 2 - 1) as r:
                    for b in range(2):
                        head(PH * n + 2 * r + b, True, True)
                for h in range(PH - 2, PH):
                    head(PH * n + h, True, not last, n + 1 if not last and h == PH - 2 else None)

            def peer(l):
                n0 = n_tiles[l]
                norm0 = 2 * n0 + live[l]
                for h in range(LAG):
                    head(PH * n0 + h, False, True, n0 if h == 0 else None)
                tile(n0)
                with act.Fori(1, live[l] - 1) as t:
                    tile(n0 + t, norm0 + t - 1)
                tile(n0 + live[l] - 1, norm0 + live[l] - 2, True)
                std(norm0 + live[l] - 1)

            for l in range(LAYERS):
                if l == 0:
                    project(l, 0, TILES, True)
                else:
                    project(l, 0, LAT, True)
                    project(l, LAT, CTX, False)
                attention(l)
                convolution(l)
                merge(l)
                with act.Fori(0, live[l]) as t:
                    std(2 * n_tiles[l] + t)
                peer(l)

        @block.vector
        def _(dve):
            v = nc.vector
            give_credits(dve, "dve")
            ch = Chain(dve, s["v_chain"])
            dve.wait_ge(s["c_sig"], 1)
            dve.wait_ge(s["consts_made"], 3 + 2 * LAT)
            v.tensor_tensor(csilu[:], csig[:], ccol[:], ALU.mult).then_inc(s["c_silu"], 1)

            def mod_block(l, r, b):
                need(dve, "mod_mm", MODS * l + 2 * r + b + 1)
                dve.wait_ge(s[f"bmod_in{b}"], 16 * (MODS // 2 * l + r + 1))
                need(dve, f"mod_out{b}", 16 * (MODS // 2 * l + r))
                v.tensor_tensor(modrow[l][:, b, :], bank(4 + b)[0:2, 0:MB], brow[l][:, b, :], ALU.add
                                ).then_inc(s["mod_done"], 1)

            def rope(o, q, t, n, dup):
                q4 = q.rearrange("p (h f) -> p h f", f=HD)
                r4 = rt[:, 0:n * HD].rearrange("p (h f) -> p h f", f=HD)
                c = ropec[:, ds(t, 1), :].to_broadcast([P, n, HD])
                q5 = q.rearrange("p (h a s f) -> p h a s f", a=2, s=2, f=16)
                r5 = rt[:, 0:n * HD].rearrange("p (h a s f) -> p h a s f", a=2, s=2, f=16)
                for half in range(2):
                    sn = ropes[:, ds(t, 1), :].rearrange("p o (a s f) -> p o a s f", a=2, s=2)[:, :, :, half, :]
                    ch.inc(v.tensor_tensor(r5[:, :, :, half, :], q5[:, :, :, 1 - half, :],
                                           sn.to_broadcast([P, n, 2, 16]), ALU.mult))
                ch.wait()
                ch.inc(v.tensor_tensor(q4, q4, c, ALU.mult))
                ch.wait()
                return q4, r4

            def norm(q, n, at, g):
                q3 = q.rearrange("p (h f) -> p h f", f=HD)
                ch.inc(v.tensor_tensor(q3, q3, rstd[:, at:at + n].rearrange("p (h o) -> p h o", o=1).to_broadcast([P, n, HD]), ALU.mult))
                ch.wait()
                ch.inc(v.tensor_tensor(q3, q3, g.rearrange("p (o f) -> p o f", o=1).to_broadcast([P, n, HD]), ALU.mult))
                ch.wait()

            def squares(q, n, at):
                r = rt[:, 0:n * HD]
                ch.inc(v.tensor_tensor(r, q, q, ALU.mult))
                ch.wait()
                ch.inc(v.tensor_reduce(ss[:, at:at + n], r.rearrange("p (h f) -> p h f", f=HD), AX, ALU.add))
                ch.wait()

            def project(l, lo, n, with_q, per):
                with ch.loop(lo, n, per) as t:
                    i = TILES * l + t
                    need(dve, "xt_mm", i)
                    xt = x_all[:, ds(t, 1), :].rearrange("p o d -> p (o d)")
                    row = lambda j: rows1[:, ds(2 * (t // LAT) + j, 1), :].rearrange("p o d -> p (o d)")
                    ch.inc(v.scalar_tensor_tensor(out=xm, in0=row(0), scalar=1.0, in1=xt, op0=ALU.add, op1=ALU.mult))
                    ch.wait()
                    v.tensor_tensor(xm, xm, row(1), ALU.add).then_inc(s["xm_done"], 1)
                    need(dve, "xts_done", i + 1)
                    v.tensor_copy(xT[:, :, ds(t * P, P)], xTs).then_inc(s["xt_copied"], 1)
                    need(dve, "kv_sb", i + 1)
                    squares(pkv[:, 0:P], KV, HEADS)
                    if with_q:
                        need(dve, "qa_sb", i + 1)
                        squares(pq_a, HEADS, 0)
                    v.tensor_scalar(ss[:, 0:10], ss[:, 0:10], 1.0 / HD, EPS, ALU.mult, ALU.add).then_inc(s["ss_done"], 1)
                    ch.inc(v.tensor_copy(va[:, ds(t, 1), :].rearrange("p o d -> p (o d)"), pkv[:, P:2 * P]))
                    ch.inc(v.tensor_copy(vc[:, ds(t + 1 + t // LAT, 1), :].rearrange("p o d -> p (o d)"), pkv[:, 3 * P:4 * P]))
                    dve.wait_ge(s["sd_done"], i + 1)
                    ch.inc(v.reciprocal(rstd[:, 0:10], rstd[:, 0:10]))
                    ch.wait()
                    need(dve, "tk_mm", i)
                    norm(pkv[:, 0:P], KV, HEADS, kn[:, l, :])
                    twice = lambda o: o.rearrange("p (g r f) -> p g r f", r=2, f=HD)
                    for part in range(2):
                        q4, r4 = rope(rk, pkv[:, 2 * part * P:(2 * part + 1) * P], t, KV, 2)
                        for r in range(2):
                            last = v.tensor_tensor(twice(rk[:, 2 * part * P:2 * (part + 1) * P])[:, :, r, :], q4, r4, ALU.add)
                            if (part, r) == (1, 1):
                                last.then_inc(s["rk_done"], 1)
                            else:
                                ch.inc(last)
                        if part == 0:
                            ch.wait()
                    need(dve, "rk_done", i + 1)
                    if with_q:
                        need(dve, "ta_mm", i)
                        norm(pq_a, HEADS, 0, qn[:, l, :])
                        q4, r4 = rope(rq_a, pq_a, t, HEADS, 1)
                        v.tensor_tensor(rq_a.rearrange("p (h f) -> p h f", f=HD), q4, r4, ALU.add).then_inc(s["rqa_done"], 1)
                        need(dve, "rqa_done", i + 1)
                        need(dve, "qc_sb", i + 1)
                        need(dve, "tc_mm", i)
                        q4, r4 = rope(rq_c, pq_c, t, HEADS, 1)
                        v.tensor_tensor(rq_c.rearrange("p (h f) -> p h f", f=HD), q4, r4, ALU.add).then_inc(s["rqc_done"], 1)
                        need(dve, "rqc_done", i + 1)

            def attend(u, t, branch, lat, l):
                first = 0 if lat and branch == 0 else 1 if lat else 4
                qT = (qTa, qTc)[branch]
                for half in range(2):
                    rows = slice(64 * half, 64 * half + 64)
                    o = qz[branch][rows].rearrange("p (c two) n -> p c two n", two=2)[:, :, half, :]
                    m = v.tensor_copy(o, qT[rows, :, ds(t * P, P)])
                    if half == 0:
                        ch.inc(m)
                ch.wait()
                m.then_inc(s["qz_done"], 1)

                def maximum(h):
                    hh = HEADS * u + h
                    o = 2 * BW * (h % 2)
                    dve.wait_ge(s["s_mm"], hh + 1)
                    if lat and branch == 1:
                        edge = ps[:, o + P:o + P + 4 * P].rearrange("p (a b) -> p a b", a=2)[:, :, 0:P]
                        ch.inc(v.tensor_tensor(edge, edge, mask[:, ds(t, 1), :, :].rearrange("p o a b -> p (o a) b"), ALU.add))
                        ch.wait()
                    ch.inc(v.reduce_max(mx[:, h:h + 1], ps[:, o + first * P:o + TOK], AX))
                    ch.wait()
                    if branch == 1:
                        m = v.tensor_scalar(nm[:, h:h + 1], mx[:, h:h + 1], -SCALE, nsink[:, l, h:h + 1], ALU.mult, ALU.min)
                    else:
                        m = v.tensor_scalar(nm[:, h:h + 1], mx[:, h:h + 1], -SCALE, None, ALU.mult)
                    m.then_inc(s["nm_done"], 1)

                def evacuate(h):
                    hh = HEADS * u + h
                    if first < 4:
                        dve.wait_ge(s["pt_mm"], hh + 1)
                        need(dve, "pv_mm", hh - 1)
                        v.tensor_copy(pts[h % 2][:, first:4, :].rearrange("p a b -> p (a b)"), bank(4, first * P, BW)
                                      ).then_inc(s["pta_done"], 1)
                    else:
                        dve.sem_inc(s["pta_done"], 1)

                for h in range(HEADS + 1):
                    if h < HEADS:
                        maximum(h)
                    if h >= 1:
                        evacuate(h - 1)
                need(dve, "p_done", HEADS * (u + 1))
                if branch == 1:
                    v.tensor_tensor(es[:], nm[:], sinks[:, l, :], ALU.add).then_inc(s["es_in"], 1)
                    dve.wait_ge(s["es_done"], (u + 1) // 2)
                    ch.inc(v.tensor_tensor(sums[:], sums[:], es[:], ALU.add))
                    ch.wait()
                ch.inc(v.reciprocal(rec[:], sums[:]))
                ch.wait()
                need(dve, "pv_mm", HEADS * (u + 1))
                need(dve, "yt_mm", u - 1 if branch else u - 1)
                v.tensor_tensor(ysb[branch].rearrange("p (h f) -> p h f", f=HD), bank(6).rearrange("p (h f) -> p h f", f=HD),
                                rec[:].rearrange("p (h o) -> p h o", o=1).to_broadcast([P, HEADS, HD]), ALU.mult
                                ).then_inc(s["y_done"], 1)
                need(dve, "y_done", u + 1)

            def attention(l, pers):
                if l == 0:
                    dve.wait_ge(s["small_in"], 16 * 9)
                if l == 0:
                    ch.inc(v.tensor_scalar(nsink[:], sinks[:], -1.0, None, ALU.mult))
                for b in range(2):
                    ch.inc(v.memset(qz[b], 0.0))
                ch.wait()
                need(dve, "kT_done", TILES * (l + 1))
                need(dve, "qTa_done", TILES + LAT * l)
                need(dve, "qTc_done", TILES + LAT * l)
                for (lo, n, lat), per in zip(((0, LAT, True), (LAT, CTX, False))[:2 - l], pers):
                    with ch.loop(lo, n, per) as t:
                        u = n_att[l] + 2 * t
                        attend(u, t, 0, lat, l)
                        attend(u + 1, t, 1, lat, l)

            def convolution(l):
                w = width[l]
                ch.inc(v.memset(zb, 0.0))
                ch.wait()
                parts = [(1, 0, LAT * P), (515, LAT * P, CTX * P)][:2 - l]
                for c in range(BC):
                    dve.wait_ge(s["xbs_done"], BC * l + c + 1)
                    dve.wait_ge(s["gc_mm"], BC * l + c + 1)
                    for z0, x0, n in parts:
                        ch.inc(v.tensor_tensor(zb[:, z0:z0 + n], xbs[:, x0:x0 + n], ps[:, 2 * BW + x0:2 * BW + x0 + n], ALU.mult))
                    ch.wait()
                    for z0, x0, n in parts:
                        ch.inc(v.tensor_scalar(ycv[:, x0:x0 + n], zb[:, z0 - 1:z0 - 1 + n], convw[:, l, c, 0:1], None, ALU.mult))
                    ch.wait()
                    for tap in (1, 2):
                        for z0, x0, n in parts:
                            ch.inc(v.scalar_tensor_tensor(out=ycv[:, x0:x0 + n], in0=zb[:, z0 - 1 + tap:z0 - 1 + tap + n],
                                                          scalar=convw[:, l, c, tap:tap + 1], in1=ycv[:, x0:x0 + n],
                                                          op0=ALU.mult, op1=ALU.add))
                        ch.wait()
                    dve.wait_ge(s["gb_mm"], BC * l + c + 1)
                    v.tensor_tensor(yT[1][:, c, 0:w], ycv[:, 0:w], ps[:, 4 * BW:4 * BW + w], ALU.mult).then_inc(s["cv_done"], 1)
                    need(dve, "cv_done", BC * l + c + 1)
                    dve.sem_inc(s["yb_done"], 1)

            def merge(l, per):
                w = width[l]
                with ch.loop(0, 4, per) as r:
                    for e6 in range(6):
                        e = 24 * l + 6 * r + e6
                        b, i = e6 % 2, e6 % 3
                        dve.wait_ge(s["sg_done"], e + 1)
                        need(dve, "b_mm", e + 1)
                        o = mT[:, ds(2 * r + e6 // 3, 1), 0:w].rearrange("p o d -> p (o d)")
                        branch = ps[:, (4 * b + 2) * BW:(4 * b + 2) * BW + w]
                        if i == 0:
                            v.tensor_tensor(o, sg[b][:, 0:w], branch, ALU.mult).then_inc(s["m_evac"], 1)
                            need(dve, "m_evac", e + 1)
                            dve.sem_inc(s["mT_done"], 1)
                        else:
                            v.tensor_tensor(mtmp[:, 0:w], sg[b][:, 0:w], branch, ALU.mult).then_inc(s["m_evac"], 1)
                            need(dve, "m_evac", e + 1)
                            v.tensor_tensor(o, o, mtmp[:, 0:w], ALU.add).then_inc(s["mT_done"], 1)
                            dve.wait_ge(s["mT_done"], e + 1)

            def norm_read(y, gate, tmp, name, count):
                v.tensor_tensor(tmp, y, gate, ALU.mult).then_inc(s[name], 1)
                need(dve, name, count)

            def norm_stats(xt, tmp):
                ch.inc(v.scalar_tensor_tensor(out=xt, in0=xt, scalar=ALPHA, in1=tmp, op0=ALU.mult, op1=ALU.add))
                ch.wait(s["v_turn"])
                for half in range(2):
                    ch.inc(v.bn_stats(stats[:, half, :], xt[:, half * BW:(half + 1) * BW]))
                ch.wait(s["v_turn"])
                ch.inc(v.bn_aggr(mv[:], stats[:].rearrange("p a b -> p (a b)")))
                ch.wait()
                v.tensor_scalar(sd[:, 0:1], mv[:, 1:2], 1.0, EPS, ALU.mult, ALU.add).then_inc(s["var_done"], 1)

            def norm_apply(n, xt, gamma, beta, name, count):
                dve.wait_ge(s["std_done"], n + 1)
                ch.inc(v.reciprocal(rstd[:, 15:16], sd[:, 1:2]))
                ch.wait()
                ch.inc(v.tensor_scalar(xt, xt, mv[:, 0:1], rstd[:, 15:16], ALU.subtract, ALU.mult))
                ch.wait()
                ch.inc(v.tensor_tensor(xt, xt, gamma, ALU.mult))
                ch.wait()
                v.tensor_tensor(xt, xt, beta, ALU.add).then_inc(s[name], 1)
                need(dve, name, count)

            def out_norm(l, per):
                n0 = n_tiles[l]
                dve.wait_ge(s["rows2_in"], 64 * (l + 1))
                with ch.loop(0, live[l] // 2, per) as r:
                    for b in range(2):
                        t = 2 * r + b
                        dve.wait_ge(s["y_mm"], n0 + t + 1)
                        xt = x_all[:, ds(t, 1), :].rearrange("p o d -> p (o d)")
                        norm_read(ps[:, 2 * b * BW:2 * (b + 1) * BW],
                                  rows2[:, ds(t // LAT, 1), :].rearrange("p o d -> p (o d)"), lt, "y_read", n0 + t + 1)
                        norm_stats(xt, lt)
                        norm_apply(2 * n0 + t, xt, rows2[:, 2, :], rows2[:, 3, :], "x_mid", n0 + t + 1)

            def next_h(n, t):
                dve.wait_ge(s["prow_in"], 32 * (n + 1))
                need(dve, "ht_mm", n)
                xt = tile_of(t)
                ch.inc(v.scalar_tensor_tensor(out=hn, in0=prow[:, 0, :], scalar=1.0, in1=xt, op0=ALU.add, op1=ALU.mult))
                ch.wait()
                v.tensor_tensor(hn, hn, prow[:, 1, :], ALU.add).then_inc(s["hn_done"], 1)
                need(dve, "hn_done", n + 1)
                dve.sem_inc(s["v_turn"], 1)

            h_cur = ps[:, 2 * BW:4 * BW]

            def head(i, at, at_j, gather, route, l, begins=None, norm=None, turns=None, mod=None):
                j = i + LAG if gather else i

                def mod_part(m):
                    if mod is not None:
                        r, part = mod
                        mod_block(1, 3 * r + (3 * part + m) // 2, (3 * part + m) % 2)

                def group_dots(q):
                    g = GROUPS * i + q
                    for k in range(GR):
                        dve.wait_ge(u_in[k], 16 * (g + 1))
                        v.tensor_tensor_reduce(ur[:, k, :], ur[:, k, :], h_cur, 1.0, 0.0, ALU.mult, ALU.add,
                                               dots[:, q % 2, k:k + 1]).then_inc(s["dots_done"], 1)

                def coefficients(q):
                    g = GROUPS * i + q
                    dve.wait_ge(s["gelu_done"], g + 1)
                    v.tensor_tensor(coef[:, q % 2, :], gl[:, q % 2, :], gates[:, ds(at * TOPK + q * GR, GR)], ALU.mult
                                    ).then_inc(s["coef_done"], 1)

                if gather:
                    group_dots(0)
                    coefficients(0)
                    if norm is not None:
                        n, t = begins
                        ends_read(n - 1, l)
                    if turns is not None:
                        next_h(*turns)
                    group_dots(1)
                    if norm is not None:
                        norm_stats(tile_of(t - 1), fx)
                if route:
                    highest_of_keys(j, gather)
                if gather:
                    coefficients(1)
                    group_dots(2)
                    if norm is not None:
                        norm_apply(norm, tile_of(t - 1), ln2[:, 0, :], ln2[:, 1, :], "x_new", n)
                    mod_part(0)
                if route:
                    highest_of_sums(j)
                if gather:
                    coefficients(2)
                    group_dots(3)
                    mod_part(1)
                    if not route:
                        coefficients(3)
                if route:
                    experts(j, at_j, l, (lambda: coefficients(3)) if gather else None)
                mod_part(2)

            def highest_of_keys(j, gather):
                need(dve, "sc_copied", j + 1)
                dve.sem_inc(s["v_turn"], 1)
                for p in range(2):
                    ch.inc(v.max(v16[:, p, 0:8], sc[:, p, :]))
                ch.wait(s["v_turn"])
                for p in range(2):
                    ch.inc(v.max_index(i16[:, p, 0:8], v16[:, p, 0:8], sc[:, p, :]))
                    ch.inc(v.match_replace(sc2[:, p, :], v16[:, p, 0:8], sc[:, p, :], LOWEST))
                ch.wait(s["v_turn"])
                for p in range(2):
                    ch.inc(v.max(v16[:, p, 8:16], sc2[:, p, :]))
                ch.wait(s["v_turn"])
                for p in range(2):
                    ch.inc(v.max_index(i16[:, p, 8:16], v16[:, p, 8:16], sc2[:, p, :]))
                ch.wait()

            def highest_of_sums(j):
                wide = lambda a, b: a.to_broadcast([P, TOPK, TOPK])
                first = v16[:, 0, :].rearrange("p (a o) -> p a o", o=1).to_broadcast([P, TOPK, TOPK])
                second = v16[:, 1, :].rearrange("p (o a) -> p o a", o=1).to_broadcast([P, TOPK, TOPK])
                ch.inc(v.tensor_tensor(cand, first, second, ALU.add))
                ch.wait(s["v_turn"])
                flat = cand.rearrange("p a b -> p (a b)")
                flat2 = cand2.rearrange("p a b -> p (a b)")
                ch.inc(v.max(top[:, 0:8], flat))
                ch.inc(v.tensor_copy(i16f[:], i16[:]))
                ch.wait(s["v_turn"])
                ch.inc(v.max_index(pos[:, 0:8], top[:, 0:8], flat))
                ch.inc(v.match_replace(flat2, top[:, 0:8], flat, LOWEST))
                ch.inc(v.tensor_scalar(ntop[:], top[:, 0:1], -1.0, None, ALU.mult))
                ch.wait(s["v_turn"])
                v.max(top[:, 8:16], flat2).then_inc(s["top_done"], 1)
                need(dve, "top_done", j + 1)
                dve.sem_inc(s["v_turn"], 1)

            def experts(j, at_j, l, between):
                flat2 = cand2.rearrange("p a b -> p (a b)")
                ch.inc(v.max_index(pos[:, 8:16], top[:, 8:16], flat2))
                ch.wait()
                ch.inc(v.tensor_scalar(ab[:, 0, :], pos[:], 4, None, ALU.logical_shift_right))
                ch.inc(v.tensor_scalar(ab[:, 1, :], pos[:], TOPK - 1, None, ALU.bitwise_and))
                ch.wait()
                ch.inc(v.tensor_copy(abf[:], ab[:]))
                if between is not None:
                    between()
                ch.wait()
                ch.inc(v.tensor_tensor(eq, abf[:].rearrange("p a (k o) -> p (a k) o", o=1).to_broadcast([P, 2 * TOPK, TOPK]),
                                       iota16[:].rearrange("p (o k) -> p o k", o=1).to_broadcast([P, 2 * TOPK, TOPK]), ALU.is_equal))
                ch.wait()
                for p in range(2):
                    e = eq[:, p * TOPK:(p + 1) * TOPK, :]
                    ch.inc(v.tensor_tensor(e, e, i16f[:, p:p + 1, :].to_broadcast([P, TOPK, TOPK]), ALU.mult))
                ch.wait()
                ch.inc(v.tensor_reduce(sel[:].rearrange("p a k -> p (a k)"), eq, AX, ALU.add))
                ch.wait()
                ch.inc(v.scalar_tensor_tensor(out=idxf[:], in0=sel[:, 0, :], scalar=float(NK), in1=sel[:, 1, :],
                                              op0=ALU.mult, op1=ALU.add))
                ch.wait()
                v.tensor_scalar(idx[:, ds(at_j * TOPK, TOPK)], idxf[:], float(l * EXPERTS), None, ALU.add
                                ).then_inc(s["idx_done"], 1)
                need(dve, "exp_done", j + 1)
                ch.inc(v.reciprocal(tsum[:, 1:2], tsum[:, 0:1]))
                ch.wait()
                v.tensor_scalar(gates[:, ds(at_j * TOPK, TOPK)], te[:], tsum[:, 1:2], None, ALU.mult
                                ).then_inc(s["gate_done"], 1)
                need(dve, "gate_done", j + 1)

            def tile(n, t, l, norm=None, last=False, mod=False):
                tile_begins()
                for h in range(2):
                    head(PH * n + h, h, h + LAG, True, True, l, *(((n, t), norm) if h == 0 else ()))
                dve.sem_inc(s["v_turn"], 1)
                with ch.loop(1, PH // 2 - 2, 2 * R_CHAIN) as r:
                    for b in range(2):
                        h = 2 * r + b
                        head(PH * n + h, h, h + LAG, True, True, l, mod=(r - 1, b) if mod else None)
                for h in range(PH - 2, PH):
                    head(PH * n + h, h, h + LAG - PH, True, not last, l,
                         turns=(n + 1, t + 1) if not last and h == PH - 2 else None)

            R_CHAIN = 26

            def tile_of(t):
                return x_all[:, ds(t, 1), :].rearrange("p o d -> p (o d)")

            def tile_begins():
                ch.inc(v.tensor_copy(h_cur, hn))
                ch.wait()

            def ends_read(n, l):
                need(dve, "v_used", TOPK * PH * (n + 1))
                dve.wait_ge(s["g2_in"], 16 * (n + 1))
                norm_read(ps[:, 0:D], prow[:, 2, :], fx, "f_read", n + 1)

            def peer(l, per):
                n0 = n_tiles[l]
                norm0 = 2 * n0 + live[l]
                dve.wait_ge(s["ln2_in"], 32 * (l + 1))
                next_h(n0, 0)
                for h in range(LAG):
                    head(PH * n0 + h, h, h, False, True, l)
                tile(n0, 0, l)
                with ch.loop(1, live[l] - 2, per) as t:
                    tile(n0 + t, t, l, norm0 + t - 1)
                t = live[l] - 1
                tile(n0 + t, t, l, norm0 + t - 1, True, l == 0)
                ends_read(n0 + t, l)
                norm_stats(tile_of(t), fx)
                norm_apply(norm0 + t, tile_of(t), ln2[:, 0, :], ln2[:, 1, :], "x_new", n0 + t + 1)

            for l in range(LAYERS):
                if l == 0:
                    with dve.Fori(0, MODS // 2) as r:
                        for b in range(2):
                            mod_block(l, r, b)
                for b in (0, 5):
                    ch.inc(v.memset(kTc[:, :, b * P:(b + 1) * P], 0.0))
                    ch.inc(v.memset(vc[:, b, :], 0.0))
                if l == 0:
                    dve.wait_ge(s["x_in"], 32)
                    dve.wait_ge(s["small_in"], 16 * 9)
                ch.wait()
                need(dve, "mod_mm", MODS * (l + 1))
                dve.wait_ge(s["rows1_in"], 64 * (l + 1))
                if l == 0:
                    project(l, 0, TILES, True, 27)
                else:
                    project(l, 0, LAT, True, 27)
                    project(l, LAT, CTX, False, 17)
                attention(l, (29, 21))
                convolution(l)
                merge(l, 0)
                out_norm(l, 14)
                peer(l, 217)


def _rope_tables():
    import numpy as np
    quarter = HD // 4
    row = np.repeat(np.arange(LAT * P // 64), 64)
    col = np.tile(np.arange(64), LAT * P // 64)
    inv = np.power(np.float32(10000.0), -np.arange(quarter, dtype=np.float32) / np.float32(quarter)).astype(np.float32)
    ang = (np.stack([row, col], -1).astype(np.float32)[..., None] * inv).astype(np.float32)
    c, s = np.cos(ang), np.sin(ang)
    cos = np.ones((TILES * P, 2, 2, quarter), np.float32)
    sin = np.zeros((TILES * P, 2, 2, quarter), np.float32)
    cos[:LAT * P] = c[:, :, None, :]
    sin[:LAT * P, :, 0] = -s
    sin[:LAT * P, :, 1] = s
    place = lambda a: np.ascontiguousarray(a.reshape(TILES, P, HD).transpose(1, 0, 2))
    return place(cos), place(sin)


def kernel(x, c, ctx, c_ctx, w_mod, b_mod, w_in, q_norm, k_norm, conv_w, sink, w_branch, w_out, ln1_g, ln1_b,
           w_pq, sub_keys, u_tab, v_tab, ln2_g, ln2_b):
    import numpy as np
    import concourse.bacc as bacc
    from concourse.bass_utils import run_bass_kernel_spmd

    a = {n: np.asarray(v) for n, v in dict(
        x=x, ctx=ctx, b_mod=b_mod, q_norm=q_norm, k_norm=k_norm, sink=sink, ln1_g=ln1_g, ln1_b=ln1_b,
        u_tab=u_tab, v_tab=v_tab, ln2_g=ln2_g, ln2_b=ln2_b).items()}
    L = LAYERS
    w_in = np.asarray(w_in)
    rows_first = lambda w, k: w.reshape(L, k, P, -1).transpose(0, 2, 1, 3)
    cc = np.stack([np.asarray(c)[0], np.asarray(c_ctx)])
    a["cc"] = cc.reshape(2, KD, P).transpose(2, 1, 0)
    a["w_mod"] = np.asarray(w_mod).reshape(L, KD, P, MODS, MB).transpose(0, 3, 2, 1, 4)
    kc = QKV - 2 * P
    a["w_qkv"] = rows_first(np.concatenate([w_in[..., 0:BW], w_in[..., BW:BW + 2 * P], w_in[..., kc:QKV],
                                            w_in[..., BW + 2 * P:kc]], -1), KD)
    cv = w_in[..., QKV:QKV + 3 * BW].reshape(L, KD, P, 3, BC, P)[:, :, :, [0, 2, 1]]
    a["w_conv"] = cv.transpose(0, 4, 3, 2, 1, 5).reshape(L, 3 * BC, P, KD, P)
    gate = w_in[..., QKV + 3 * BW:].reshape(L, KD, P, 3, KD, P).transpose(0, 4, 3, 2, 1, 5)
    branch = np.asarray(w_branch).reshape(L, 3, BC, P, KD, P).transpose(0, 4, 1, 3, 2, 5)
    a["w_gb"] = np.concatenate([gate, branch], 4).reshape(L, 3 * KD, P, KD + BC, P)
    a["w_out"] = rows_first(np.asarray(w_out), KD)
    a["w_pq"] = np.asarray(w_pq).reshape(L, KD, P, PH, 2 * P).transpose(0, 2, 3, 1, 4).reshape(L, P, PH, KD * 2 * P)
    a["sub_keys"] = np.asarray(sub_keys).reshape(L, 2 * PH, NK, P).transpose(0, 3, 1, 2)
    a["conv_w"] = np.asarray(conv_w).reshape(L, 3, BC, P).transpose(3, 0, 2, 1)
    a["rope_c"], a["rope_s"] = _rope_tables()

    nc = bacc.Bacc("TRN2", target_bir_lowering=False, num_devices=1)
    arrays, aps = {}, {}
    for n, v in a.items():
        arrays[f"in_{n}"] = np.ascontiguousarray(v)
        aps[n] = nc.dram_tensor(f"in_{n}", v.shape, mybir.dt.from_np(v.dtype), kind="ExternalInput").ap()
    out = nc.dram_tensor("out_0", (1, LAT * P, D), F32, kind="ExternalOutput").ap()
    hybrid_dit_peer(nc, out=out, **aps)
    r = run_bass_kernel_spmd(nc, [arrays], core_ids=[0])
    return r.results[0]["out_0"]
```

```python
from contextlib import ExitStack, contextmanager

import concourse.bass as bass
from concourse import mybir

P = 128
D = 1024
KD = D // P
LAYERS = 2
LAT, CTX = 4, 2
TILES = LAT + CTX
TOK = TILES * P
HD = 64
HEADS = 8
KV = 2
BW = HEADS * HD
BC = BW // P
QKV = 3 * BW
SCALE = HD ** -0.5
ALPHA = (2 * LAYERS) ** 0.25
EPS = 1e-6
NEG = -1e30
LOWEST = -3.4e38
MB = 512
MODS = 6 * D // MB

PH = 8
TOPK = 16
NK = 128
EXPERTS = NK * NK
UR, VR = 4, 8
GR = 4
GROUPS = TOPK // GR
LAG = 2

F32 = mybir.dt.float32
U32 = mybir.dt.uint32
ALU = mybir.AluOpType
ACT = mybir.ActivationFunctionType
AX = mybir.AxisListType.X
ds = bass.ds


class Chain:

    def __init__(self, eng, sem):
        self.eng, self.sem, self.base, self.k = eng, sem, 0, 0

    def inc(self, ins):
        ins.then_inc(self.sem, 1)
        self.k += 1

    def wait(self, alone=None):
        self.eng.wait_ge(self.sem, self.base + self.k)
        if alone is not None:
            self.eng.sem_inc(alone, 1)

    @contextmanager
    def loop(self, start, n, per):
        base, k = self.base, self.k
        with self.eng.Fori(start, start + n) as r:
            self.base, self.k = base + k + (r - start) * per, 0
            yield r
            assert self.k == per, ("increments of a round", self.k, "not", per)
        self.base, self.k = base, k + n * per


def hybrid_dit_peer(nc, x, ctx, cc, w_mod, b_mod, w_qkv, q_norm, k_norm, conv_w, sink, w_conv, w_gb,
                    w_out, ln1_g, ln1_b, w_pq, sub_keys, u_tab, v_tab, ln2_g, ln2_b, rope_c, rope_s,
                    out):
    with ExitStack() as stack:
        def sb(name, shape, dt=F32):
            return stack.enter_context(nc.sbuf_tensor(name, shape, dt))

        def sem(name):
            return stack.enter_context(nc.semaphore(name))

        x_all = sb("x_all", [P, TILES, D])
        ident = sb("ident", [P, P])
        zeros = sb("zeros", [P, P])
        iota16 = sb("iota16", [P, TOPK])
        ropec = sb("ropec", [P, TILES, HD])
        ropes = sb("ropes", [P, TILES, HD])
        mask = sb("mask", [P, LAT, 2, P])
        qn = sb("qn", [P, LAYERS, HD])
        kn = sb("kn", [P, LAYERS, HD])
        sinks = sb("sinks", [P, LAYERS, HEADS])
        nsink = sb("nsink", [P, LAYERS, HEADS])
        convw = sb("convw", [P, LAYERS, BC, 3])
        ccol = sb("ccol", [P, KD, 2])
        csig = sb("csig", [P, KD, 2])
        csilu = sb("csilu", [P, KD, 2])
        ss = sb("ss", [P, 16])
        rstd = sb("rstd", [P, 16])
        mx = sb("mx", [P, HEADS])
        nm = sb("nm", [P, HEADS])
        sums = sb("sums", [P, HEADS])
        es = sb("es", [P, HEADS])
        rec = sb("rec", [P, HEADS])
        stats = sb("stats", [P, 2, 6])
        mv = sb("mv", [P, 2])
        sd = sb("sd", [P, 2])
        AK = 170
        arena = sb("arena", [P, AK * 256])

        def region(kb, *shape):
            n = 1
            for s in shape:
                n *= s
            a0 = int(kb * 256)
            assert a0 + n <= AK * 256, (kb, shape)
            v = arena[:, a0:a0 + n]
            if len(shape) == 2:
                return v.rearrange("p (a b) -> p a b", b=shape[1])
            if len(shape) == 3:
                return v.rearrange("p (a b c) -> p a b c", b=shape[1], c=shape[2])
            return v

        xT = region(0, KD, TOK)
        wqkv = region(24, KD, QKV)
        rows1 = region(72, 4, D)
        xm = region(88, D)
        xTs = region(92, KD, P)
        qTa = region(96, BC, TOK)
        qTc = region(108, BC, TOK)
        kTa = region(120, KV, TOK)
        kTc = region(126, KV, 8 * P)
        va = region(134, TILES, P)
        vc = region(137, 8, P)
        pq_a = region(141, BW)
        pkv = region(143, BW)
        pq_c = region(145, BW)
        rt = region(147, BW)
        rq_a = region(149, BW)
        rq_c = region(151, BW)
        rk = region(153, BW)
        wmod = [[region(a0 + 16 * b, KD, MB) for b in range(2)] for a0 in (96, 0)]
        modrow = [region(a0, 2, MB)[0:2] for a0 in (158, 32)]
        brow = [region(a0, 2, MB)[0:2] for a0 in (162, 36)]
        qz = [region(72 + 4 * b, HEADS, P) for b in range(2)]
        pr = [region(80 + 3 * b, TILES * P) for b in range(2)]
        pts = [region(86 + 3 * b, TILES, P) for b in range(2)]
        ysb = [region(92 + 2 * b, BW) for b in range(2)]
        yT = [region(24 + 12 * b, BC, TOK) for b in range(3)]
        wcv = [region(158 + 4 * b, KD, P) for b in range(3)]
        zb = region(141, 772)
        xbs = region(145, TOK)
        ycv = region(148, TOK)
        cw = sb("cw", [P, 3])
        gbw = [region(60 + 6 * b, KD + BC, P) for b in range(2)]
        sg = [region(82 + 3 * b, TOK) for b in range(2)]
        mtmp = region(88, TOK)
        mT = region(96, KD, TOK)
        wout = region(120, KD, D)
        rows2 = region(154, 4, D)
        lt = region(72, D)

        wpq = region(0, PH, KD * 2 * P)
        keys = region(64, 2 * PH, P)
        fx = region(72, D)
        prow = region(76, 3, D)
        ln2 = region(88, 2, D)
        ur = region(96, UR, D)
        vr = region(112, VR, D)
        hn = region(144, D)
        hT = region(148, KD, P)
        dg = region(152, VR, P)
        q_sb = region(156, 2, P)
        qT_sb = region(157, 2, P)
        sc = region(158, 2, P)
        sc2 = region(159, 2, P)
        cand = region(160, TOPK, TOPK)
        cand2 = region(161, TOPK, TOPK)
        eq = region(162, 2 * TOPK, TOPK)
        gates = region(164, PH * TOPK)
        v16 = sb("v16", [P, 2, TOPK])
        i16 = sb("i16", [P, 2, TOPK], U32)
        i16f = sb("i16f", [P, 2, TOPK])
        top = sb("top", [P, TOPK])
        pos = sb("pos", [P, TOPK], U32)
        ab = sb("ab", [P, 2, TOPK], U32)
        abf = sb("abf", [P, 2, TOPK])
        sel = sb("sel", [P, 2, TOPK])
        idxf = sb("idxf", [P, TOPK])
        ntop = sb("ntop", [P, 1])
        te = sb("te", [P, TOPK])
        tsum = sb("tsum", [P, 2])
        idx = region(164.5, PH * TOPK).bitcast(U32)
        ist = [sb(f"ist{b}", [P, TOPK], U32) for b in range(2)]
        dots = sb("dots", [P, 2, GR])
        gl = sb("gl", [P, 2, GR])
        coef = sb("coef", [P, 2, GR])

        ps = stack.enter_context(nc.psum_tensor("ps", [P, 8 * BW], F32))

        def bank(b, lo=0, hi=BW):
            return ps[:, b * BW + lo:b * BW + hi]

        mods = nc.dram_tensor("mods", [LAYERS, 2, 6 * D], F32).ap()
        SH1, SC1, G1, SH2, SC2, G2 = range(6)

        def mod_row(l, kind, which):
            return mods[l, kind:kind + 1, which * D:(which + 1) * D].partition_broadcast(P)

        def row_of(t):
            return t.partition_broadcast(P)

        s = {n: sem(n) for n in (
            "x_in small_in ident_made consts_made wqkv_in c_in c_sig c_silu bmod_in0 bmod_in1 wmod_in0 wmod_in1 "
            "mod_mm mod_done mod_out0 mod_out1 rows1_in xm_done xt_mm xts_done xt_copied qa_mm kv_mm qc_mm qa_sb kv_sb "
            "qc_sb ss_done sd_done rqa_done rk_done rqc_done ta_mm tk_mm tc_mm qTa_done kT_done qTc_done "
            "v_chain qz_done s_mm nm_done p_done pt_mm pta_done ptb_done pv_mm es_in es_done y_done yt_mm yT_done "
            "wcv_in0 wcv_in1 wcv_in2 xb_mm gc_mm gb_mm xbs_done zb_done yb_done "
            "gbw_in0 gbw_in1 g_mm b_mm sg_done m_evac mT_done wout_in rows2_in y_mm var_done std_done y_read x_mid "
            "wpq_in keys_in ln2_in prow_in g2_in hn_done ht_mm hT_done q_mm q_copied qT_mm qT_copied sc_mm sc_copied "
            "top_done exp_done idx_done gate_done dots_done gelu_done coef_done diag_done v_used pool_turn "
            "v_turn idx_staged f_read x_new x_out").split()}
        u_in = [sem(f"u_in{k}") for k in range(UR)]
        v_in = [sem(f"v_in{k}") for k in range(VR)]
        CREDIT = {"p_done": 2, "pta_done": 1, "ptb_done": 1, "pv_mm": 2, "y_done": 1, "yT_done": 1,
                  "m_evac": 2, "b_mm": 2, "dots_done": UR, "v_used": VR, "mod_done": 2, "mod_out0": 16, "mod_out1": 16,
                  "mod_mm": 2, "xts_done": 1, "xt_mm": 1, "xt_copied": 1, "qa_sb": 1, "kv_sb": 1, "qc_sb": 1,
                  "qa_mm": 1, "kv_mm": 1, "qc_mm": 1, "rqa_done": 1, "rk_done": 1, "rqc_done": 1,
                  "ta_mm": 1, "tk_mm": 1, "tc_mm": 1, "qTa_done": 1, "kT_done": 1, "qTc_done": 1,
                  "y_read": 2, "yb_done": 1, "hT_done": 1, "ht_mm": 1, "q_mm": 1, "q_copied": 1, "qT_mm": 1,
                  "qT_copied": 1, "sc_mm": 1, "sc_copied": 1, "top_done": 1, "idx_done": 1, "f_read": 1,
                  "idx_staged": 0, "x_new": 1, "hn_done": 1, "exp_done": 1, "yt_mm": 1, "gate_done": 1}
        OWNER = {
            "pe": "pv_mm b_mm v_used mod_mm xt_mm qa_mm kv_mm qc_mm ta_mm tk_mm tc_mm ht_mm q_mm qT_mm sc_mm yt_mm",
            "act": "p_done ptb_done yT_done xts_done qa_sb kv_sb qc_sb qTa_done kT_done qTc_done hT_done q_copied "
                   "qT_copied sc_copied exp_done",
            "dve": "pta_done y_done m_evac dots_done mod_done xt_copied rqa_done rk_done rqc_done y_read yb_done "
                   "top_done idx_done f_read x_new hn_done gate_done",
            "sp": "mod_out0 mod_out1"}

        def give_credits(eng, who):
            for n in OWNER[who].split():
                if CREDIT[n]:
                    eng.sem_inc(s[n], CREDIT[n])

        def need(eng, name, n):
            eng.wait_ge(s[name], n + CREDIT.get(name, 0))

        assert LAT == BC
        CV = ("xb_mm", "gc_mm", "gb_mm")
        CV_READ = ("xbs_done", "zb_done", "yb_done")
        CV_SLOTS = 5
        LAST_SLOT = 2 * HEADS - 1
        cv_parts = [2, 1]
        cv_before = [0, 2 * BC]

        def cv_step(l, slot):
            if slot == 2 * CV_SLOTS:
                return None
            kind, i = divmod(slot - (slot > 2 * CV_SLOTS), CV_SLOTS)
            return (kind, *(((0, 0, 3), (0, 3, 6), (0, 6, 8), (1, 0, 4), (1, 4, 8)),
                            ((0, 0, 2), (0, 2, 4), (0, 4, 6), (0, 6, 7), (0, 7, 8)))[l][i])

        MOD_HEADS = 5
        n_att = [HEADS * 0, 12]
        n_tiles = [0, TILES]
        width = [TOK, LAT * P]
        live = [TILES, LAT]

        block = stack.enter_context(nc.Block())

        @block.sync
        def _(sp):
            sp.dma_start(ccol[:], cc).then_inc(s["c_in"], 16)
            give_credits(sp, "sp")

            def first_loads():
                sp.dma_start(x_all[:, 0:LAT, :], x.rearrange("o (t p) d -> p (o t) d", p=P)).then_inc(s["x_in"], 16)
                sp.dma_start(x_all[:, LAT:TILES, :], ctx.rearrange("o (t p) d -> p (o t) d", p=P)).then_inc(s["x_in"], 16)
                for dst, src in ((ropec[:], rope_c), (ropes[:], rope_s), (convw[:], conv_w)):
                    sp.dma_start(dst, src).then_inc(s["small_in"], 16)
                for dst, src in ((qn, q_norm), (kn, k_norm), (sinks, sink)):
                    for ll in range(LAYERS):
                        sp.dma_start(dst[:, ll, :], row_of(src[ll:ll + 1, :])[:, 0, :]).then_inc(s["small_in"], 16)

            def modulation(l):
                def load(e, b):
                    need(sp, "mod_mm", MODS * l + e - 1)
                    need(sp, "mod_done", MODS * l + e - 1)
                    sp.dma_start(wmod[l][b], w_mod[l, ds(e, 1)].rearrange("o p k n -> p (o k) n")
                                 ).then_inc(s[f"wmod_in{b}"], 16)
                    sp.dma_start(brow[l][:, b, :], b_mod[l:l + 1, ds(e * MB, MB)].partition_broadcast(2)[:, 0, :]
                                 ).then_inc(s[f"bmod_in{b}"], 16)

                def store(e, b):
                    need(sp, "mod_done", MODS * l + e + 1)
                    sp.dma_start(mods[l, :, ds(e * MB, MB)], modrow[l][:, b, :]).then_inc(s[f"mod_out{b}"], 16)

                def rounds(lo, hi):
                    with sp.Fori(lo, hi) as r:
                        for b in range(2):
                            load(2 * r + b, b)
                            store(2 * r + (b - 2), b)

                for b in range(2):
                    load(b, b)
                if l == 0:
                    early = max(SH1, SC1) * D // MB + D // MB
                    rounds(1, early // 2 + 1)
                    for b in range(2):
                        need(sp, f"mod_out{b}", 8 * early)
                    mod_rows(l)
                    first_loads()
                    rounds(early // 2 + 1, MODS // 2)
                    sp.dma_start(wqkv, w_qkv[l]).then_inc(s["wqkv_in"], 16)
                else:
                    rounds(1, MODS // 2)
                for b in range(2):
                    store(MODS - 2 + b, b)
                for b in range(2):
                    need(sp, f"mod_out{b}", 8 * MODS * (l + 1))

            def mod_rows(l):
                for kind in range(2):
                    for j, which in enumerate((SC1, SH1)):
                        sp.dma_start(rows1[:, 2 * kind + j, :], mod_row(l, kind, which)[:, 0, :]
                                     ).then_inc(s["rows1_in"], 16)

            def mixer(l):
                if l == 1:
                    need(sp, "q_mm", PH * (TILES - 1) + MOD_HEADS)
                    modulation(l)
                    need(sp, "sc_mm", PH * TILES)
                    sp.dma_start(wqkv, w_qkv[l]).then_inc(s["wqkv_in"], 16)
                    need(sp, "x_new", TILES)
                    mod_rows(l)
                else:
                    modulation(l)
                for c in range(BC):
                    for j in range(3):
                        if c:
                            sp.wait_ge(s[CV[j]], cv_before[l] + cv_parts[l] * c)
                        sp.dma_start(wcv[j], w_conv[l, 3 * c + j]).then_inc(s[f"wcv_in{j}"], 16)
                with sp.Fori(0, 12) as r:
                    for b in range(2):
                        need(sp, "b_mm", 24 * l + 2 * r + b - 1)
                        sp.dma_start(gbw[b], w_gb[l, ds(2 * r + b, 1)].rearrange("o p k n -> p (o k) n")
                                     ).then_inc(s[f"gbw_in{b}"], 16)
                need(sp, "yT_done", n_att[l] + 2 * live[l])
                sp.dma_start(wout, w_out[l]).then_inc(s["wout_in"], 16)
                for j, src in enumerate((mod_row(l, 0, G1), mod_row(l, 1, G1), row_of(ln1_g[l:l + 1]), row_of(ln1_b[l:l + 1]))):
                    sp.dma_start(rows2[:, j, :], src[:, 0, :]).then_inc(s["rows2_in"], 16)

            def peer(l):
                n0 = n_tiles[l]
                sp.wait_ge(s["mT_done"], 24 * (l + 1))
                sp.dma_start(prow[:, 0, :], mod_row(l, 0, SC2)[:, 0, :]).then_inc(s["prow_in"], 16)
                sp.dma_start(prow[:, 1, :], mod_row(l, 0, SH2)[:, 0, :]).then_inc(s["prow_in"], 16)
                sp.dma_start(wpq, w_pq[l]).then_inc(s["wpq_in"], 16)
                sp.dma_start(keys, sub_keys[l]).then_inc(s["keys_in"], 16)
                for j, src in enumerate((ln2_g, ln2_b)):
                    sp.dma_start(ln2[:, j, :], row_of(src[l:l + 1])[:, 0, :]).then_inc(s["ln2_in"], 16)

                def next_rows(t):
                    need(sp, "hn_done", n0 + t)
                    for j, which in enumerate((SC2, SH2)):
                        sp.dma_start(prow[:, j, :], mods[l, ds(t // LAT, 1), which * D:(which + 1) * D].partition_broadcast(P)[:, 0, :]
                                     ).then_inc(s["prow_in"], 16)

                def g2_row(t):
                    need(sp, "f_read", n0 + t)
                    sp.dma_start(prow[:, 2, :], mods[l, ds(t // LAT, 1), G2 * D:(G2 + 1) * D].partition_broadcast(P)[:, 0, :]
                                 ).then_inc(s["g2_in"], 16)

                def store(t):
                    need(sp, "x_new", n0 + t + 1)
                    sp.dma_start(out[0, ds(t * P, P), :], x_all[:, ds(t, 1), :].rearrange("p o d -> p (o d)")
                                 ).then_inc(s["x_out"], 16)

                next_rows(1)
                g2_row(0)
                with sp.Fori(1, live[l] - 1) as t:
                    next_rows(t + 1)
                    g2_row(t)
                    if l == 1:
                        store(t - 1)
                g2_row(live[l] - 1)
                if l == 1:
                    store(LAT - 2)

            for l in range(LAYERS):
                mixer(l)
                peer(l)
            need(sp, "x_new", n_tiles[1] + LAT)
            sp.dma_start(out[0, (LAT - 1) * P:LAT * P, :], x_all[:, LAT - 1, :]).then_inc(s["x_out"], 16)
            sp.wait_ge(s["x_out"], 16 * LAT)

        @block.gpsimd
        def _(pool):
            nc.gpsimd.memset(ident[:], 1.0).then_inc(s["ident_made"], 1)
            pool.wait_ge(s["ident_made"], 1)
            nc.gpsimd.affine_select(out=ident[:], in_=ident[:], compare_op=ALU.is_equal, fill=0.0, base=0,
                                    pattern=[[-1, P]], channel_multiplier=1).then_inc(s["ident_made"], 1)
            nc.gpsimd.memset(zeros[:], 0.0).then_inc(s["consts_made"], 1)
            nc.gpsimd.iota(iota16[:], [[1, TOPK]], base=0, channel_multiplier=0,
                           allow_small_or_imprecise_dtypes=True).then_inc(s["consts_made"], 1)
            nc.gpsimd.memset(mask[:], 0.0).then_inc(s["consts_made"], 1)
            pool.wait_ge(s["consts_made"], 3)
            for t in range(LAT):
                for side in range(2):
                    m = mask[:, t, side, :]
                    if (t, side) in ((0, 0), (LAT - 1, 1)):
                        nc.gpsimd.memset(m, NEG).then_inc(s["consts_made"], 1)
                    else:
                        sign = 1 if side == 0 else -1
                        nc.gpsimd.affine_select(out=m, in_=m, compare_op=ALU.is_ge, fill=NEG, base=0,
                                                pattern=[[sign, P]], channel_multiplier=-sign
                                                ).then_inc(s["consts_made"], 1)

            u_rows = u_tab.rearrange("l e d -> (l e) d")
            v_rows = v_tab.rearrange("l e d -> (l e) d")

            def head(i, i_idx, b):
                need(pool, "idx_done", i + 1)
                nc.gpsimd.tensor_copy(ist[b][:], idx[:, ds(i_idx * TOPK, TOPK)]).then_inc(s["idx_staged"], 1)
                pool.wait_ge(s["idx_staged"], i + 1)
                for q in range(GROUPS):
                    g = GROUPS * i + q
                    for k in range(GR):
                        need(pool, "dots_done", UR * (g - 1) + k + 1)
                        pool.sem_inc(s["pool_turn"], 1)
                        nc.gpsimd.indirect_dma_start(
                            ur[:, k, :], None, u_rows,
                            bass.IndirectOffsetOnAxis(ap=ist[b][:, q * GR + k:q * GR + k + 1], axis=0)
                        ).then_inc(u_in[k], 16)
                    for k in range(GR):
                        need(pool, "v_used", GR * (g - 2) + k + 1)
                        pool.sem_inc(s["pool_turn"], 1)
                        nc.gpsimd.indirect_dma_start(
                            vr[:, GR * (q % 2) + k, :], None, v_rows,
                            bass.IndirectOffsetOnAxis(ap=ist[b][:, q * GR + k:q * GR + k + 1], axis=0)
                        ).then_inc(v_in[GR * (q % 2) + k], 16)

            for l in range(LAYERS):
                i0 = PH * n_tiles[l]
                with pool.Fori(0, live[l]) as t:
                    with pool.Fori(0, PH // 2) as r:
                        for b in range(2):
                            head(i0 + PH * t + 2 * r + b, 2 * r + b, b)

        @block.tensor
        def _(pe):
            give_credits(pe, "pe")
            pe.wait_ge(s["ident_made"], 2)
            pe.wait_ge(s["consts_made"], 3 + 2 * LAT)

            def mm(o, lhsT, rhs, first=True, last=True):
                return nc.tensor.matmul(o, lhsT, rhs, start=first, stop=last, skip_group_check=True)

            def mod_block(l, r, b):
                pe.wait_ge(s[f"wmod_in{b}"], 16 * (MODS // 2 * l + r + 1))
                need(pe, "mod_done", MODS * l + 2 * r + b - 1)
                for k in range(KD):
                    m = mm(bank(4 + b)[0:2, 0:MB], csilu[:, k, :], wmod[l][b][:, k, :], k == 0, k == KD - 1)
                m.then_inc(s["mod_mm"], 1)

            def modulation(l):
                pe.wait_ge(s["c_silu"], 1)
                with pe.Fori(0, MODS // 2) as r:
                    for b in range(2):
                        mod_block(l, r, b)

            def turn_x(l, t):
                i = TILES * l + t
                pe.wait_ge(s["xm_done"], i + 1)
                need(pe, "xts_done", i)
                for k in range(KD):
                    m = nc.tensor.transpose(bank(0, k * P, (k + 1) * P), xm[:, k * P:(k + 1) * P], ident[:])
                m.then_inc(s["xt_mm"], 1)

            def turn_qk(l, t, src, done, b, name, copied):
                i = TILES * l + t
                need(pe, done, i + 1)
                need(pe, copied, i)
                for k in range(BC):
                    m = nc.tensor.transpose(bank(b, k * P, (k + 1) * P), src[:, k * P:(k + 1) * P], ident[:])
                m.then_inc(s[name], 1)

            def turn_q(l, t):
                turn_qk(l, t, rq_a, "rqa_done", 5, "ta_mm", "qTa_done")
                turn_qk(l, t, rq_c, "rqc_done", 6, "tc_mm", "qTc_done")

            def project_tile(l, t, with_q, q_before, x_after):
                i = TILES * l + t

                def product(b, name, copied):
                    need(pe, copied, i)
                    for k in range(KD):
                        m = mm(bank(2 + b), xTs[:, k, :], wqkv[:, k, b * BW:(b + 1) * BW], k == 0, k == KD - 1)
                    m.then_inc(s[name], 1)

                need(pe, "xts_done", i + 1)
                product(1, "kv_mm", "kv_sb")
                if q_before:
                    turn_q(l, t - 1)
                if x_after:
                    turn_x(l, t + 1)
                if with_q:
                    product(0, "qa_mm", "qa_sb")
                    product(2, "qc_mm", "qc_sb")
                turn_qk(l, t, rk, "rk_done", 7, "tk_mm", "kT_done")

            def project(l):
                turn_x(l, 0)
                pe.wait_ge(s["wqkv_in"], 16 * (l + 1))
                project_tile(l, 0, True, False, True)
                with pe.Fori(1, live[l] - (l == 0)) as t:
                    project_tile(l, t, True, True, True)
                if l == 0:
                    project_tile(l, TILES - 1, True, True, False)
                    turn_q(l, TILES - 1)
                else:
                    project_tile(l, LAT, False, True, True)
                    project_tile(l, LAT + 1, False, False, False)

            def attend(l, u, t, branch, lat, yt_before):
                kT, v = (kTa, va) if branch == 0 else (kTc, vc)
                local = lat and branch == 1

                def scores(h):
                    hh = HEADS * u + h
                    o = 2 * (h % 2)
                    g = h // (HEADS // KV)
                    need(pe, "p_done", hh - 1)
                    q = qz[branch][:, h, :]
                    if branch == 0:
                        if lat:
                            mm(bank(o), q, kT[:, g, 0:BW])
                        m = mm(bank(o + 1, 0, 2 * P), q, kT[:, g, BW:TOK])
                    else:
                        if lat:
                            mm(bank(o, P, BW), q, kT[:, g, ds(t * P, 3 * P)])
                        m = mm(bank(o + 1, 0, 2 * P), q, kT[:, g, 6 * P:8 * P])
                    m.then_inc(s["s_mm"], 1)

                first = 0 if lat and branch == 0 else 1 if lat else 4

                def turn_p(h):
                    hh = HEADS * u + h
                    need(pe, "p_done", hh + 1)
                    if h == 0:
                        need(pe, "yT_done", u)
                    need(pe, "pta_done", hh)
                    need(pe, "ptb_done", hh)
                    for j in range(first, TILES):
                        m = nc.tensor.transpose(bank(4 + j // 4, (j % 4) * P, (j % 4 + 1) * P),
                                                pr[h % 2][:, j * P:(j + 1) * P], ident[:])
                    m.then_inc(s["pt_mm"], 1)

                def values(h):
                    hh = HEADS * u + h
                    g = h // (HEADS // KV)
                    need(pe, "pta_done", hh + 1)
                    need(pe, "ptb_done", hh + 1)
                    if h == 0:
                        need(pe, "y_done", u)
                    for j in range(first, TILES):
                        if branch == 0:
                            vj = v[:, j, g * HD:(g + 1) * HD]
                        elif j < 4:
                            vj = v[:, ds(t + (j - 1), 1), g * HD:(g + 1) * HD].rearrange("p o d -> p (o d)")
                        else:
                            vj = v[:, j + 2, g * HD:(g + 1) * HD]
                        m = mm(bank(6, h * HD, (h + 1) * HD), pts[h % 2][:, j, :], vj, j == first, j == TILES - 1)
                    m.then_inc(s["pv_mm"], 1)

                if lat:
                    convolve(l, t, HEADS * branch)
                pe.wait_ge(s["qz_done"], u + 1)
                for h in range(HEADS + 2):
                    if h < HEADS:
                        scores(h)
                    if h == 0 and yt_before:
                        turn_y(u - 1, 1 - branch)
                    if lat and 0 < h < HEADS and HEADS * branch + h < LAST_SLOT:
                        convolve(l, t, HEADS * branch + h)
                    if h >= 2:
                        values(h - 2)
                    if 1 <= h <= HEADS:
                        turn_p(h - 1)
                if lat and branch == 1:
                    convolve(l, t, LAST_SLOT)

            def turn_y(u, branch):
                need(pe, "y_done", u + 1)
                need(pe, "yT_done", u)
                for k in range(BC):
                    m = nc.tensor.transpose(bank(4, k * P, (k + 1) * P), ysb[branch][:, k * P:(k + 1) * P], ident[:])
                m.then_inc(s["yt_mm"], 1)

            def convolve(l, c, slot):
                step = cv_step(l, slot)
                if step is None:
                    return
                kind, part, k0, k1 = step
                if k0 == 0:
                    if kind == 0 and part == 0:
                        need(pe, "yb_done", cv_before[l] + cv_parts[l] * c)
                    elif part == 0:
                        need(pe, CV_READ[kind - 1], cv_before[l] + cv_parts[l] * (c + 1))
                    else:
                        need(pe, CV_READ[kind], cv_before[l] + cv_parts[l] * c + 1)
                    pe.wait_ge(s[f"wcv_in{kind}"], 16 * (BC * l + c + 1))
                at = (slice(0, LAT * P), slice(LAT * P, TOK))[part]
                for k in range(k0, k1):
                    m = mm(bank(7, 0, at.stop - at.start), wcv[kind][:, k, :], xT[:, k, at], k == 0, k == KD - 1)
                if k1 == KD:
                    m.then_inc(s[CV[kind]], 1)

            def attention(l):
                need(pe, "kT_done", TILES * (l + 1))
                for lo, n, lat in ((0, LAT, True), (LAT, CTX, False))[:2 - l]:
                    with pe.Fori(lo, lo + n) as t:
                        u = n_att[l] + 2 * t
                        attend(l, u, t, 0, lat, False)
                        attend(l, u + 1, t, 1, lat, True)
                        turn_y(u + 1, 1)

            def over_tokens(l, b, lhs, rhs, n):
                for k in range(n):
                    m = mm(bank(b), lhs(k), rhs[:, k, 0:LAT * P], k == 0, k == n - 1)
                if l == 0:
                    for k in range(n):
                        m = mm(bank(b + 1, 0, CTX * P), lhs(k), rhs[:, k, LAT * P:TOK], k == 0, k == n - 1)
                return m

            def merge(l):
                need(pe, "yb_done", cv_before[l] + cv_parts[l] * BC)
                need(pe, "yT_done", n_att[l] + 2 * live[l])
                with pe.Fori(0, 4) as r:
                    for e6 in range(6):
                        e = 24 * l + 6 * r + e6
                        b, i = e6 % 2, e6 % 3
                        pe.wait_ge(s[f"gbw_in{b}"], 16 * (12 * l + 3 * r + e6 // 2 + 1))
                        need(pe, "m_evac", e - 1)
                        over_tokens(l, 4 * b, lambda k: gbw[b][:, k, :], xT, KD).then_inc(s["g_mm"], 1)
                        over_tokens(l, 4 * b + 2, lambda k: gbw[b][:, KD + k, :], yT[i], BC).then_inc(s["b_mm"], 1)

            def project_out(l):
                pe.wait_ge(s["mT_done"], 24 * (l + 1))
                pe.wait_ge(s["wout_in"], 16 * (l + 1))
                for t in range(live[l]):
                    need(pe, "y_read", n_tiles[l] + t - 1)
                    for half in range(2):
                        for k in range(KD):
                            m = mm(bank(2 * (t % 2) + half), mT[:, k, t * P:(t + 1) * P],
                                   wout[:, k, half * BW:(half + 1) * BW], k == 0, k == KD - 1)
                    m.then_inc(s["y_mm"], 1)

            def turn_h(n):
                need(pe, "hn_done", n + 1)
                need(pe, "hT_done", n)
                for k in range(KD):
                    m = nc.tensor.transpose(bank(4, k * P, (k + 1) * P), hn[:, k * P:(k + 1) * P], ident[:])
                m.then_inc(s["ht_mm"], 1)

            def head(i, h, h_j, n_j, gather, route, clears=None, turns=False, mod=None):
                j = i + LAG if gather else i

                def sum_group(q):
                    g = GROUPS * i + q
                    for k in range(GR):
                        slot = GR * (q % 2) + k
                        pe.wait_ge(v_in[slot], 16 * (2 * i + q // 2 + 1))
                        pe.wait_ge(s["diag_done"], GR * g + k + 1)
                        mm(bank(0), dg[:, slot, :], vr[:, slot, 0:BW], False, True)
                        mm(bank(1), dg[:, slot, :], vr[:, slot, BW:D], False, True).then_inc(s["v_used"], 1)

                if route:
                    if turns:
                        turn_h(n_j)
                    need(pe, "hT_done", n_j + 1)
                    need(pe, "q_copied", j)
                    for k in range(KD):
                        w = wpq[:, ds(h_j, 1), k * 2 * P:(k + 1) * 2 * P].rearrange("p o n -> p (o n)")
                        m = mm(bank(6, 0, 2 * P), hT[:, k, :], w, k == 0, k == KD - 1)
                    m.then_inc(s["q_mm"], 1)
                    need(pe, "q_copied", j + 1)
                    need(pe, "qT_copied", j)
                    for k in range(2):
                        m = nc.tensor.transpose(bank(6, (2 + k) * P, (3 + k) * P), q_sb[:, k, :], ident[:])
                    m.then_inc(s["qT_mm"], 1)
                    need(pe, "qT_copied", j + 1)
                    need(pe, "sc_copied", j)
                    for k in range(2):
                        m = mm(bank(7, k * P, (k + 1) * P), qT_sb[:, k, :],
                               keys[:, ds(2 * h_j + k, 1), :].rearrange("p o n -> p (o n)"))
                    m.then_inc(s["sc_mm"], 1)
                if gather:
                    if clears is not None:
                        clear_sum(clears)
                    for q in range(GROUPS):
                        if mod is not None and q > 0:
                            r, part = mod
                            m = 3 * part + q - 1
                            mod_block(1, 3 * r + m // 2, m % 2)
                        sum_group(q)

            def tile(n, last=False, mod=False):
                for h in range(2):
                    head(PH * n + h, h, h + LAG, n, True, True, n if h == 0 else None)
                with pe.Fori(1, PH // 2 - 1) as r:
                    for b in range(2):
                        h = 2 * r + b
                        head(PH * n + h, h, h + LAG, n, True, True, mod=(r - 1, b) if mod else None)
                for h in range(PH - 2, PH):
                    head(PH * n + h, h, h + LAG - PH, n + 1, True, not last, turns=not last and h == PH - 2)

            def clear_sum(n):
                need(pe, "f_read", n)
                for b in range(2):
                    mm(bank(b), zeros[:], mask[:, 0:2, :, :].rearrange("p a b c -> p (a b c)"), True, False)

            def peer(l):
                n0 = n_tiles[l]
                pe.wait_ge(s["wpq_in"], 16 * (l + 1))
                pe.wait_ge(s["keys_in"], 16 * (l + 1))
                for h in range(LAG):
                    head(PH * n0 + h, h, h, n0, False, True, turns=h == 0)
                with pe.Fori(0, live[l] - 1) as t:
                    tile(n0 + t)
                tile(n0 + live[l] - 1, True, l == 0)

            modulation(0)
            for l in range(LAYERS):
                project(l)
                attention(l)
                merge(l)
                project_out(l)
                peer(l)

        @block.scalar
        def _(act):
            give_credits(act, "act")

            def copy(o, i, name):
                nc.scalar.copy(o, i).then_inc(s[name], 1)

            act.wait_ge(s["c_in"], 16)
            nc.scalar.activation(csig[:], ccol[:], ACT.Sigmoid).then_inc(s["c_sig"], 1)

            def copy_x(l, t):
                i = TILES * l + t
                need(act, "xt_mm", i + 1)
                need(act, "xt_copied", i)
                need(act, "kv_mm", i)
                q = TILES + LAT if isinstance(t, int) and l == 1 and t > LAT else i
                need(act, "qa_mm", q)
                need(act, "qc_mm", q)
                copy(xTs.rearrange("p a b -> p (a b)"), ps[:, 0:D], "xts_done")

            def copy_q(l, t):
                i = TILES * l + t
                for b, dst, m, name in ((5, qTa, "ta_mm", "qTa_done"), (6, qTc, "tc_mm", "qTc_done")):
                    need(act, m, i + 1)
                    copy(dst[:, :, ds(t * P, P)], bank(b).rearrange("p (g c) -> p g c", g=4), name)

            def project_tile(l, t, with_q, q_before, x_after):
                i = TILES * l + t

                def evacuate(src, dst, m, done, name):
                    need(act, m, i + 1)
                    need(act, done, i)
                    copy(dst, bank(src), name)

                evacuate(3, pkv, "kv_mm", "rk_done", "kv_sb")
                if q_before:
                    copy_q(l, t - 1)
                if with_q:
                    evacuate(2, pq_a, "qa_mm", "rqa_done", "qa_sb")
                act.wait_ge(s["ss_done"], i + 1)
                nc.scalar.activation(rstd[:, 0:10], ss[:, 0:10], ACT.Sqrt).then_inc(s["sd_done"], 1)
                if with_q:
                    evacuate(4, pq_c, "qc_mm", "rqc_done", "qc_sb")
                if x_after:
                    copy_x(l, t + 1)
                need(act, "tk_mm", i + 1)
                kv = bank(7).rearrange("p (g c) -> p g c", g=4)
                nc.scalar.copy(kTa[:, :, ds(t * P, P)], kv[:, 0:2, :])
                copy(kTc[:, :, ds((t + 1 + t // LAT) * P, P)], kv[:, 2:4, :], "kT_done")

            def project(l):
                copy_x(l, 0)
                project_tile(l, 0, True, False, True)
                with act.Fori(1, live[l] - (l == 0)) as t:
                    project_tile(l, t, True, True, True)
                if l == 0:
                    project_tile(l, TILES - 1, True, True, False)
                    copy_q(l, TILES - 1)
                else:
                    project_tile(l, LAT, False, True, True)
                    project_tile(l, LAT + 1, False, False, False)

            def attend(u, t, branch, lat, l, yt_before):
                first = 0 if lat and branch == 0 else 1 if lat else 4

                def exp(h):
                    hh = HEADS * u + h
                    o = 2 * BW * (h % 2)
                    act.wait_ge(s["nm_done"], hh + 1)
                    nc.scalar.activation(pr[h % 2][:, first * P:TOK], ps[:, o + first * P:o + TOK], ACT.Exp,
                                         bias=nm[:, h:h + 1], scale=SCALE, accum_out=sums[:, h:h + 1]
                                         ).then_inc(s["p_done"], 1)

                def evacuate(h):
                    hh = HEADS * u + h
                    act.wait_ge(s["pt_mm"], hh + 1)
                    need(act, "pv_mm", hh - 1)
                    copy(pts[h % 2][:, 4:6, :].rearrange("p a b -> p (a b)"), bank(5, 0, 2 * P), "ptb_done")

                for h in range(HEADS + 1):
                    if h < HEADS:
                        exp(h)
                    if h == 0 and yt_before:
                        evacuate_y(u - 1, t, 1 - branch)
                    if lat and h < HEADS:
                        convolve(l, t, HEADS * branch + h)
                    if h >= 1:
                        evacuate(h - 1)
                if branch == 1:
                    act.wait_ge(s["es_in"], (u + 1) // 2)
                    nc.scalar.activation(es[:], es[:], ACT.Exp).then_inc(s["es_done"], 1)

            def evacuate_y(u, t, branch):
                need(act, "yt_mm", u + 1)
                copy(yT[2 * branch][:, :, ds(t * P, P)], bank(4).rearrange("p (a b) -> p a b", b=P), "yT_done")

            def convolve(l, c, slot):
                kind, part, _, k1 = cv_step(l, slot) or (3, 0, 0, 0)
                if kind == 0 and k1 == KD:
                    need(act, "xb_mm", cv_before[l] + cv_parts[l] * c + part + 1)
                    at = (slice(0, LAT * P), slice(LAT * P, TOK))[part]
                    copy(xbs[:, at], bank(7, 0, at.stop - at.start), "xbs_done")

            def attention(l):
                for lo, n, lat in ((0, LAT, True), (LAT, CTX, False))[:2 - l]:
                    with act.Fori(lo, lo + n) as t:
                        u = n_att[l] + 2 * t
                        attend(u, t, 0, lat, l, False)
                        attend(u + 1, t, 1, lat, l, True)
                        evacuate_y(u + 1, t, 1)

            def merge(l):
                with act.Fori(0, 4) as r:
                    for e6 in range(6):
                        e = 24 * l + 6 * r + e6
                        b = e6 % 2
                        act.wait_ge(s["g_mm"], e + 1)
                        need(act, "m_evac", e - 1)
                        nc.scalar.activation(sg[b][:, 0:width[l]], ps[:, 4 * b * BW:4 * b * BW + width[l]],
                                             ACT.Sigmoid).then_inc(s["sg_done"], 1)

            def std(n):
                act.wait_ge(s["var_done"], n + 1)
                nc.scalar.activation(sd[:, 1:2], sd[:, 0:1], ACT.Sqrt).then_inc(s["std_done"], 1)

            def copy_hT(n):
                need(act, "ht_mm", n + 1)
                need(act, "q_mm", PH * n)
                copy(hT.rearrange("p a b -> p (a b)"), ps[:, 4 * BW:6 * BW], "hT_done")

            def head(i, gather, route, turns=None, norm=None):
                j = i + LAG if gather else i

                def gelu(q):
                    g = GROUPS * i + q
                    need(act, "dots_done", GR * (g + 1))
                    nc.scalar.activation(gl[:, q % 2, :], dots[:, q % 2, :], ACT.Gelu).then_inc(s["gelu_done"], 1)

                def diagonals(q):
                    g = GROUPS * i + q
                    act.wait_ge(s["coef_done"], g + 1)
                    need(act, "v_used", GR * (g - 1))
                    for k in range(GR):
                        nc.scalar.activation(dg[:, GR * (q % 2) + k, :], ident[:], ACT.Copy,
                                             scale=coef[:, q % 2, k:k + 1]).then_inc(s["diag_done"], 1)

                if gather:
                    gelu(0)
                    diagonals(0)
                if route:
                    if turns is not None:
                        copy_hT(turns)
                    need(act, "q_mm", j + 1)
                    copy(q_sb.rearrange("p a b -> p (a b)"), bank(6, 0, 2 * P), "q_copied")
                    need(act, "qT_mm", j + 1)
                    need(act, "sc_mm", j)
                    copy(qT_sb.rearrange("p a b -> p (a b)"), bank(6, 2 * P, 4 * P), "qT_copied")
                    need(act, "sc_mm", j + 1)
                    need(act, "top_done", j)
                    copy(sc.rearrange("p a b -> p (a b)"), bank(7, 0, 2 * P), "sc_copied")
                if gather:
                    gelu(1)
                    if norm is not None:
                        std(norm)
                    diagonals(1)
                    gelu(2)
                    diagonals(2)
                if route:
                    need(act, "top_done", j + 1)
                    nc.scalar.activation(te[:], top[:], ACT.Exp, bias=ntop[:], accum_out=tsum[:, 0:1]
                                         ).then_inc(s["exp_done"], 1)
                if gather:
                    gelu(3)
                    diagonals(3)

            def tile(n, norm=None, last=False):
                for h in range(2):
                    head(PH * n + h, True, True, None, norm if h == 0 else None)
                with act.Fori(1, PH // 2 - 1) as r:
                    for b in range(2):
                        head(PH * n + 2 * r + b, True, True)
                for h in range(PH - 2, PH):
                    head(PH * n + h, True, not last, n + 1 if not last and h == PH - 2 else None)

            def peer(l):
                n0 = n_tiles[l]
                norm0 = 2 * n0 + live[l]
                for h in range(LAG):
                    head(PH * n0 + h, False, True, n0 if h == 0 else None)
                tile(n0)
                with act.Fori(1, live[l] - 1) as t:
                    tile(n0 + t, norm0 + t - 1)
                tile(n0 + live[l] - 1, norm0 + live[l] - 2, True)
                std(norm0 + live[l] - 1)

            for l in range(LAYERS):
                project(l)
                attention(l)
                merge(l)
                with act.Fori(0, live[l]) as t:
                    std(2 * n_tiles[l] + t)
                peer(l)

        @block.vector
        def _(dve):
            v = nc.vector
            give_credits(dve, "dve")
            ch = Chain(dve, s["v_chain"])
            dve.wait_ge(s["c_sig"], 1)
            dve.wait_ge(s["consts_made"], 3 + 2 * LAT)
            v.tensor_tensor(csilu[:], csig[:], ccol[:], ALU.mult).then_inc(s["c_silu"], 1)

            def mod_block(l, r, b):
                need(dve, "mod_mm", MODS * l + 2 * r + b + 1)
                dve.wait_ge(s[f"bmod_in{b}"], 16 * (MODS // 2 * l + r + 1))
                need(dve, f"mod_out{b}", 16 * (MODS // 2 * l + r))
                v.tensor_tensor(modrow[l][:, b, :], bank(4 + b)[0:2, 0:MB], brow[l][:, b, :], ALU.add
                                ).then_inc(s["mod_done"], 1)

            def rope(o, q, t, n, dup):
                q4 = q.rearrange("p (h f) -> p h f", f=HD)
                r4 = rt[:, 0:n * HD].rearrange("p (h f) -> p h f", f=HD)
                c = ropec[:, ds(t, 1), :].to_broadcast([P, n, HD])
                q5 = q.rearrange("p (h a s f) -> p h a s f", a=2, s=2, f=16)
                r5 = rt[:, 0:n * HD].rearrange("p (h a s f) -> p h a s f", a=2, s=2, f=16)
                for half in range(2):
                    sn = ropes[:, ds(t, 1), :].rearrange("p o (a s f) -> p o a s f", a=2, s=2)[:, :, :, half, :]
                    ch.inc(v.tensor_tensor(r5[:, :, :, half, :], q5[:, :, :, 1 - half, :],
                                           sn.to_broadcast([P, n, 2, 16]), ALU.mult))
                ch.wait()
                ch.inc(v.tensor_tensor(q4, q4, c, ALU.mult))
                ch.wait()
                return q4, r4

            def norm(q, n, at, g):
                q3 = q.rearrange("p (h f) -> p h f", f=HD)
                ch.inc(v.tensor_tensor(q3, q3, rstd[:, at:at + n].rearrange("p (h o) -> p h o", o=1).to_broadcast([P, n, HD]), ALU.mult))
                ch.wait()
                ch.inc(v.tensor_tensor(q3, q3, g.rearrange("p (o f) -> p o f", o=1).to_broadcast([P, n, HD]), ALU.mult))
                ch.wait()

            def squares(q, n, at):
                r = rt[:, 0:n * HD]
                ch.inc(v.tensor_tensor(r, q, q, ALU.mult))
                ch.wait()
                ch.inc(v.tensor_reduce(ss[:, at:at + n], r.rearrange("p (h f) -> p h f", f=HD), AX, ALU.add))
                ch.wait()

            def modulate(l, t):
                need(dve, "xt_mm", TILES * l + t)
                xt = x_all[:, ds(t, 1), :].rearrange("p o d -> p (o d)")
                row = lambda j: rows1[:, ds(2 * (t // LAT) + j, 1), :].rearrange("p o d -> p (o d)")
                ch.inc(v.scalar_tensor_tensor(out=xm, in0=row(0), scalar=1.0, in1=xt, op0=ALU.add, op1=ALU.mult))
                ch.wait()
                v.tensor_tensor(xm, xm, row(1), ALU.add).then_inc(s["xm_done"], 1)

            def project_tile(l, t, with_q, x_after):
                i = TILES * l + t
                need(dve, "xts_done", i + 1)
                v.tensor_copy(xT[:, :, ds(t * P, P)], xTs).then_inc(s["xt_copied"], 1)
                if x_after:
                    modulate(l, t + 1)
                need(dve, "kv_sb", i + 1)
                squares(pkv[:, 0:P], KV, HEADS)
                if with_q:
                    need(dve, "qa_sb", i + 1)
                    squares(pq_a, HEADS, 0)
                v.tensor_scalar(ss[:, 0:10], ss[:, 0:10], 1.0 / HD, EPS, ALU.mult, ALU.add).then_inc(s["ss_done"], 1)
                ch.inc(v.tensor_copy(va[:, ds(t, 1), :].rearrange("p o d -> p (o d)"), pkv[:, P:2 * P]))
                ch.inc(v.tensor_copy(vc[:, ds(t + 1 + t // LAT, 1), :].rearrange("p o d -> p (o d)"), pkv[:, 3 * P:4 * P]))
                dve.wait_ge(s["sd_done"], i + 1)
                ch.inc(v.reciprocal(rstd[:, 0:10], rstd[:, 0:10]))
                ch.wait()
                need(dve, "tk_mm", i)
                norm(pkv[:, 0:P], KV, HEADS, kn[:, l, :])
                twice = lambda o: o.rearrange("p (g r f) -> p g r f", r=2, f=HD)
                for part in range(2):
                    q4, r4 = rope(rk, pkv[:, 2 * part * P:(2 * part + 1) * P], t, KV, 2)
                    for r in range(2):
                        last = v.tensor_tensor(twice(rk[:, 2 * part * P:2 * (part + 1) * P])[:, :, r, :], q4, r4, ALU.add)
                        if (part, r) == (1, 1):
                            last.then_inc(s["rk_done"], 1)
                        else:
                            ch.inc(last)
                    if part == 0:
                        ch.wait()
                need(dve, "rk_done", i + 1)
                if with_q:
                    need(dve, "ta_mm", i)
                    norm(pq_a, HEADS, 0, qn[:, l, :])
                    q4, r4 = rope(rq_a, pq_a, t, HEADS, 1)
                    v.tensor_tensor(rq_a.rearrange("p (h f) -> p h f", f=HD), q4, r4, ALU.add).then_inc(s["rqa_done"], 1)
                    need(dve, "rqa_done", i + 1)
                    need(dve, "qc_sb", i + 1)
                    need(dve, "tc_mm", i)
                    q4, r4 = rope(rq_c, pq_c, t, HEADS, 1)
                    v.tensor_tensor(rq_c.rearrange("p (h f) -> p h f", f=HD), q4, r4, ALU.add).then_inc(s["rqc_done"], 1)
                    need(dve, "rqc_done", i + 1)

            def project(l):
                modulate(l, 0)
                project_tile(l, 0, True, True)
                n = live[l] - (l == 0)
                with ch.loop(1, n - 1, PROJECT_CHAIN) as t:
                    project_tile(l, t, True, True)
                if l == 0:
                    project_tile(l, TILES - 1, True, False)
                else:
                    project_tile(l, LAT, False, True)
                    project_tile(l, LAT + 1, False, False)

            PROJECT_CHAIN = 27

            def attend(u, t, branch, lat, l):
                first = 0 if lat and branch == 0 else 1 if lat else 4
                def spread_q(branch):
                    qT = (qTa, qTc)[branch]
                    for half in range(2):
                        rows = slice(64 * half, 64 * half + 64)
                        o = qz[branch][rows].rearrange("p (c two) n -> p c two n", two=2)[:, :, half, :]
                        m = v.tensor_copy(o, qT[rows, :, ds(t * P, P)])
                        if half == 0:
                            ch.inc(m)
                            ch.wait()
                    m.then_inc(s["qz_done"], 1)

                if branch == 0:
                    spread_q(0)

                def maximum(h):
                    hh = HEADS * u + h
                    o = 2 * BW * (h % 2)
                    dve.wait_ge(s["s_mm"], hh + 1)
                    if lat and branch == 1:
                        edge = ps[:, o + P:o + P + 4 * P].rearrange("p (a b) -> p a b", a=2)[:, :, 0:P]
                        ch.inc(v.tensor_tensor(edge, edge, mask[:, ds(t, 1), :, :].rearrange("p o a b -> p (o a) b"), ALU.add))
                        ch.wait()
                    ch.inc(v.reduce_max(mx[:, h:h + 1], ps[:, o + first * P:o + TOK], AX))
                    ch.wait()
                    if branch == 1:
                        m = v.tensor_scalar(nm[:, h:h + 1], mx[:, h:h + 1], -SCALE, nsink[:, l, h:h + 1], ALU.mult, ALU.min)
                    else:
                        m = v.tensor_scalar(nm[:, h:h + 1], mx[:, h:h + 1], -SCALE, None, ALU.mult)
                    m.then_inc(s["nm_done"], 1)

                def evacuate(h):
                    hh = HEADS * u + h
                    if first < 4:
                        dve.wait_ge(s["pt_mm"], hh + 1)
                        need(dve, "pv_mm", hh - 1)
                        v.tensor_copy(pts[h % 2][:, first:4, :].rearrange("p a b -> p (a b)"), bank(4, first * P, BW)
                                      ).then_inc(s["pta_done"], 1)
                    else:
                        dve.sem_inc(s["pta_done"], 1)

                for h in range(HEADS + 1):
                    if h < HEADS:
                        maximum(h)
                        if branch == 0 and h == HEADS // 2:
                            spread_q(1)
                        if lat and HEADS * branch + h < LAST_SLOT:
                            convolve(l, t, HEADS * branch + h)
                    if h >= 1:
                        evacuate(h - 1)
                need(dve, "p_done", HEADS * (u + 1))
                if branch == 1:
                    v.tensor_tensor(es[:], nm[:], sinks[:, l, :], ALU.add).then_inc(s["es_in"], 1)
                    dve.wait_ge(s["es_done"], (u + 1) // 2)
                    ch.inc(v.tensor_tensor(sums[:], sums[:], es[:], ALU.add))
                    ch.wait()
                ch.inc(v.reciprocal(rec[:], sums[:]))
                ch.wait()
                need(dve, "pv_mm", HEADS * (u + 1))
                need(dve, "yt_mm", u - 1 if branch else u - 1)
                v.tensor_tensor(ysb[branch].rearrange("p (h f) -> p h f", f=HD), bank(6).rearrange("p (h f) -> p h f", f=HD),
                                rec[:].rearrange("p (h o) -> p h o", o=1).to_broadcast([P, HEADS, HD]), ALU.mult
                                ).then_inc(s["y_done"], 1)
                need(dve, "y_done", u + 1)
                if lat and branch == 1:
                    convolve(l, t, LAST_SLOT)

            ATTENTION_CHAIN = ((36, 21), (33,))

            def attention(l, pers):
                if l == 0:
                    dve.wait_ge(s["small_in"], 16 * 9)
                if l == 0:
                    ch.inc(v.tensor_scalar(nsink[:], sinks[:], -1.0, None, ALU.mult))
                for b in range(2):
                    ch.inc(v.memset(qz[b], 0.0))
                ch.inc(v.memset(zb, 0.0))
                ch.wait()
                need(dve, "kT_done", TILES * (l + 1))
                need(dve, "qTa_done", TILES + LAT * l)
                need(dve, "qTc_done", TILES + LAT * l)
                for (lo, n, lat), per in zip(((0, LAT, True), (LAT, CTX, False))[:2 - l], pers):
                    with ch.loop(lo, n, per) as t:
                        u = n_att[l] + 2 * t
                        attend(u, t, 0, lat, l)
                        attend(u + 1, t, 1, lat, l)

            def convolve(l, c, slot):
                if slot == 0:
                    ch.inc(v.tensor_copy(cw[:], convw[:, l, ds(c, 1), :].rearrange("p o k -> p (o k)")))
                at = (slice(0, LAT * P), slice(LAT * P, TOK))
                z0 = (1, 515)
                n = (LAT * P, CTX * P)

                def tap(part, j):
                    ch.wait()
                    z = zb[:, z0[part] - 1 + j:z0[part] - 1 + j + n[part]]
                    o = ycv[:, at[part]]
                    if j == 0:
                        ch.inc(v.tensor_scalar(o, z, cw[:, 0:1], None, ALU.mult))
                    else:
                        ch.inc(v.scalar_tensor_tensor(out=o, in0=z, scalar=cw[:, j:j + 1], in1=o, op0=ALU.mult, op1=ALU.add))

                for part in range(cv_parts[l]):
                    start = 3 * CV_SLOTS - 6 if l or part else CV_SLOTS + 2
                    if 0 <= slot - start - 1 < 3:
                        if slot - start - 1 == 0:
                            need(dve, "zb_done", cv_before[l] + cv_parts[l] * c + part + 1)
                        tap(part, slot - start - 1)
                kind, part, _, k1 = cv_step(l, slot) or (3, 0, 0, 0)
                if k1 == KD and kind in (1, 2):
                    done = cv_before[l] + cv_parts[l] * c + part + 1
                    need(dve, CV[kind], done)
                    y = bank(7, 0, n[part])
                    if kind == 1:
                        need(dve, "xbs_done", done)
                        v.tensor_tensor(zb[:, z0[part]:z0[part] + n[part]], xbs[:, at[part]], y, ALU.mult
                                        ).then_inc(s["zb_done"], 1)
                    else:
                        ch.wait()
                        v.tensor_tensor(yT[1][:, ds(c, 1), at[part]].rearrange("p o n -> p (o n)"), ycv[:, at[part]], y, ALU.mult
                                        ).then_inc(s["yb_done"], 1)

            def merge(l, per):
                w = width[l]
                with ch.loop(0, 4, per) as r:
                    for e6 in range(6):
                        e = 24 * l + 6 * r + e6
                        b, i = e6 % 2, e6 % 3
                        dve.wait_ge(s["sg_done"], e + 1)
                        need(dve, "b_mm", e + 1)
                        o = mT[:, ds(2 * r + e6 // 3, 1), 0:w].rearrange("p o d -> p (o d)")
                        branch = ps[:, (4 * b + 2) * BW:(4 * b + 2) * BW + w]
                        if i == 0:
                            v.tensor_tensor(o, sg[b][:, 0:w], branch, ALU.mult).then_inc(s["m_evac"], 1)
                            need(dve, "m_evac", e + 1)
                            dve.sem_inc(s["mT_done"], 1)
                        else:
                            v.tensor_tensor(mtmp[:, 0:w], sg[b][:, 0:w], branch, ALU.mult).then_inc(s["m_evac"], 1)
                            need(dve, "m_evac", e + 1)
                            v.tensor_tensor(o, o, mtmp[:, 0:w], ALU.add).then_inc(s["mT_done"], 1)
                            dve.wait_ge(s["mT_done"], e + 1)

            def norm_read(y, gate, tmp, name, count):
                v.tensor_tensor(tmp, y, gate, ALU.mult).then_inc(s[name], 1)
                need(dve, name, count)

            def norm_stats(xt, tmp):
                ch.inc(v.scalar_tensor_tensor(out=xt, in0=xt, scalar=ALPHA, in1=tmp, op0=ALU.mult, op1=ALU.add))
                ch.wait(s["v_turn"])
                for half in range(2):
                    ch.inc(v.bn_stats(stats[:, half, :], xt[:, half * BW:(half + 1) * BW]))
                ch.wait(s["v_turn"])
                ch.inc(v.bn_aggr(mv[:], stats[:].rearrange("p a b -> p (a b)")))
                ch.wait()
                v.tensor_scalar(sd[:, 0:1], mv[:, 1:2], 1.0, EPS, ALU.mult, ALU.add).then_inc(s["var_done"], 1)

            def norm_apply(n, xt, gamma, beta, name, count):
                dve.wait_ge(s["std_done"], n + 1)
                ch.inc(v.reciprocal(rstd[:, 15:16], sd[:, 1:2]))
                ch.wait()
                ch.inc(v.tensor_scalar(xt, xt, mv[:, 0:1], rstd[:, 15:16], ALU.subtract, ALU.mult))
                ch.wait()
                ch.inc(v.tensor_tensor(xt, xt, gamma, ALU.mult))
                ch.wait()
                v.tensor_tensor(xt, xt, beta, ALU.add).then_inc(s[name], 1)
                need(dve, name, count)

            def out_norm(l, per):
                n0 = n_tiles[l]
                dve.wait_ge(s["rows2_in"], 64 * (l + 1))
                with ch.loop(0, live[l] // 2, per) as r:
                    for b in range(2):
                        t = 2 * r + b
                        dve.wait_ge(s["y_mm"], n0 + t + 1)
                        xt = x_all[:, ds(t, 1), :].rearrange("p o d -> p (o d)")
                        norm_read(ps[:, 2 * b * BW:2 * (b + 1) * BW],
                                  rows2[:, ds(t // LAT, 1), :].rearrange("p o d -> p (o d)"), lt, "y_read", n0 + t + 1)
                        norm_stats(xt, lt)
                        norm_apply(2 * n0 + t, xt, rows2[:, 2, :], rows2[:, 3, :], "x_mid", n0 + t + 1)

            def next_h(n, t):
                dve.wait_ge(s["prow_in"], 32 * (n + 1))
                need(dve, "ht_mm", n)
                xt = tile_of(t)
                ch.inc(v.scalar_tensor_tensor(out=hn, in0=prow[:, 0, :], scalar=1.0, in1=xt, op0=ALU.add, op1=ALU.mult))
                ch.wait()
                v.tensor_tensor(hn, hn, prow[:, 1, :], ALU.add).then_inc(s["hn_done"], 1)
                need(dve, "hn_done", n + 1)
                dve.sem_inc(s["v_turn"], 1)

            h_cur = ps[:, 2 * BW:4 * BW]

            def head(i, at, at_j, gather, route, l, begins=None, norm=None, turns=None, mod=None):
                j = i + LAG if gather else i

                def mod_part(m):
                    if mod is not None:
                        r, part = mod
                        mod_block(1, 3 * r + (3 * part + m) // 2, (3 * part + m) % 2)

                def group_dots(q):
                    g = GROUPS * i + q
                    for k in range(GR):
                        dve.wait_ge(u_in[k], 16 * (g + 1))
                        v.tensor_tensor_reduce(ur[:, k, :], ur[:, k, :], h_cur, 1.0, 0.0, ALU.mult, ALU.add,
                                               dots[:, q % 2, k:k + 1]).then_inc(s["dots_done"], 1)

                def coefficients(q):
                    g = GROUPS * i + q
                    dve.wait_ge(s["gelu_done"], g + 1)
                    v.tensor_tensor(coef[:, q % 2, :], gl[:, q % 2, :], gates[:, ds(at * TOPK + q * GR, GR)], ALU.mult
                                    ).then_inc(s["coef_done"], 1)

                if gather:
                    group_dots(0)
                    coefficients(0)
                    if norm is not None:
                        n, t = begins
                        ends_read(n - 1, l)
                    if turns is not None:
                        next_h(*turns)
                    group_dots(1)
                    if norm is not None:
                        norm_stats(tile_of(t - 1), fx)
                if route:
                    highest_of_keys(j, gather)
                if gather:
                    coefficients(1)
                    group_dots(2)
                    if norm is not None:
                        norm_apply(norm, tile_of(t - 1), ln2[:, 0, :], ln2[:, 1, :], "x_new", n)
                    mod_part(0)
                if route:
                    highest_of_sums(j)
                if gather:
                    coefficients(2)
                    group_dots(3)
                    mod_part(1)
                    if not route:
                        coefficients(3)
                if route:
                    experts(j, at_j, l, (lambda: coefficients(3)) if gather else None)
                mod_part(2)

            def highest_of_keys(j, gather):
                need(dve, "sc_copied", j + 1)
                dve.sem_inc(s["v_turn"], 1)
                for p in range(2):
                    ch.inc(v.max(v16[:, p, 0:8], sc[:, p, :]))
                ch.wait(s["v_turn"])
                for p in range(2):
                    ch.inc(v.max_index(i16[:, p, 0:8], v16[:, p, 0:8], sc[:, p, :]))
                    ch.inc(v.match_replace(sc2[:, p, :], v16[:, p, 0:8], sc[:, p, :], LOWEST))
                ch.wait(s["v_turn"])
                for p in range(2):
                    ch.inc(v.max(v16[:, p, 8:16], sc2[:, p, :]))
                ch.wait(s["v_turn"])
                for p in range(2):
                    ch.inc(v.max_index(i16[:, p, 8:16], v16[:, p, 8:16], sc2[:, p, :]))
                ch.wait()

            def highest_of_sums(j):
                wide = lambda a, b: a.to_broadcast([P, TOPK, TOPK])
                first = v16[:, 0, :].rearrange("p (a o) -> p a o", o=1).to_broadcast([P, TOPK, TOPK])
                second = v16[:, 1, :].rearrange("p (o a) -> p o a", o=1).to_broadcast([P, TOPK, TOPK])
                ch.inc(v.tensor_tensor(cand, first, second, ALU.add))
                ch.wait(s["v_turn"])
                flat = cand.rearrange("p a b -> p (a b)")
                flat2 = cand2.rearrange("p a b -> p (a b)")
                ch.inc(v.max(top[:, 0:8], flat))
                ch.inc(v.tensor_copy(i16f[:], i16[:]))
                ch.wait(s["v_turn"])
                ch.inc(v.max_index(pos[:, 0:8], top[:, 0:8], flat))
                ch.inc(v.match_replace(flat2, top[:, 0:8], flat, LOWEST))
                ch.inc(v.tensor_scalar(ntop[:], top[:, 0:1], -1.0, None, ALU.mult))
                ch.wait(s["v_turn"])
                v.max(top[:, 8:16], flat2).then_inc(s["top_done"], 1)
                need(dve, "top_done", j + 1)
                dve.sem_inc(s["v_turn"], 1)

            def experts(j, at_j, l, between):
                flat2 = cand2.rearrange("p a b -> p (a b)")
                ch.inc(v.max_index(pos[:, 8:16], top[:, 8:16], flat2))
                ch.wait()
                ch.inc(v.tensor_scalar(ab[:, 0, :], pos[:], 4, None, ALU.logical_shift_right))
                ch.inc(v.tensor_scalar(ab[:, 1, :], pos[:], TOPK - 1, None, ALU.bitwise_and))
                ch.wait()
                ch.inc(v.tensor_copy(abf[:], ab[:]))
                if between is not None:
                    between()
                ch.wait()
                ch.inc(v.tensor_tensor(eq, abf[:].rearrange("p a (k o) -> p (a k) o", o=1).to_broadcast([P, 2 * TOPK, TOPK]),
                                       iota16[:].rearrange("p (o k) -> p o k", o=1).to_broadcast([P, 2 * TOPK, TOPK]), ALU.is_equal))
                ch.wait()
                for p in range(2):
                    e = eq[:, p * TOPK:(p + 1) * TOPK, :]
                    ch.inc(v.tensor_tensor(e, e, i16f[:, p:p + 1, :].to_broadcast([P, TOPK, TOPK]), ALU.mult))
                ch.wait()
                ch.inc(v.tensor_reduce(sel[:].rearrange("p a k -> p (a k)"), eq, AX, ALU.add))
                ch.wait()
                ch.inc(v.scalar_tensor_tensor(out=idxf[:], in0=sel[:, 0, :], scalar=float(NK), in1=sel[:, 1, :],
                                              op0=ALU.mult, op1=ALU.add))
                ch.wait()
                v.tensor_scalar(idx[:, ds(at_j * TOPK, TOPK)], idxf[:], float(l * EXPERTS), None, ALU.add
                                ).then_inc(s["idx_done"], 1)
                need(dve, "exp_done", j + 1)
                ch.inc(v.reciprocal(tsum[:, 1:2], tsum[:, 0:1]))
                ch.wait()
                v.tensor_scalar(gates[:, ds(at_j * TOPK, TOPK)], te[:], tsum[:, 1:2], None, ALU.mult
                                ).then_inc(s["gate_done"], 1)
                need(dve, "gate_done", j + 1)

            def tile(n, t, l, norm=None, last=False, mod=False):
                tile_begins()
                for h in range(2):
                    head(PH * n + h, h, h + LAG, True, True, l, *(((n, t), norm) if h == 0 else ()))
                dve.sem_inc(s["v_turn"], 1)
                with ch.loop(1, PH // 2 - 2, 2 * R_CHAIN) as r:
                    for b in range(2):
                        h = 2 * r + b
                        head(PH * n + h, h, h + LAG, True, True, l, mod=(r - 1, b) if mod else None)
                for h in range(PH - 2, PH):
                    head(PH * n + h, h, h + LAG - PH, True, not last, l,
                         turns=(n + 1, t + 1) if not last and h == PH - 2 else None)

            R_CHAIN = 26

            def tile_of(t):
                return x_all[:, ds(t, 1), :].rearrange("p o d -> p (o d)")

            def tile_begins():
                ch.inc(v.tensor_copy(h_cur, hn))
                ch.wait()

            def ends_read(n, l):
                need(dve, "v_used", TOPK * PH * (n + 1))
                dve.wait_ge(s["g2_in"], 16 * (n + 1))
                norm_read(ps[:, 0:D], prow[:, 2, :], fx, "f_read", n + 1)

            def peer(l, per):
                n0 = n_tiles[l]
                norm0 = 2 * n0 + live[l]
                dve.wait_ge(s["ln2_in"], 32 * (l + 1))
                next_h(n0, 0)
                for h in range(LAG):
                    head(PH * n0 + h, h, h, False, True, l)
                tile(n0, 0, l)
                with ch.loop(1, live[l] - 2, per) as t:
                    tile(n0 + t, t, l, norm0 + t - 1)
                t = live[l] - 1
                tile(n0 + t, t, l, norm0 + t - 1, True, l == 0)
                ends_read(n0 + t, l)
                norm_stats(tile_of(t), fx)
                norm_apply(norm0 + t, tile_of(t), ln2[:, 0, :], ln2[:, 1, :], "x_new", n0 + t + 1)

            for l in range(LAYERS):
                if l == 0:
                    with dve.Fori(0, MODS // 2) as r:
                        for b in range(2):
                            mod_block(l, r, b)
                for b in (0, 5):
                    ch.inc(v.memset(kTc[:, :, b * P:(b + 1) * P], 0.0))
                    ch.inc(v.memset(vc[:, b, :], 0.0))
                if l == 0:
                    dve.wait_ge(s["x_in"], 32)
                    dve.wait_ge(s["small_in"], 16 * 9)
                ch.wait()
                need(dve, "mod_mm", MODS * (l + 1))
                dve.wait_ge(s["rows1_in"], 64 * (l + 1))
                project(l)
                attention(l, ATTENTION_CHAIN[l])
                merge(l, 0)
                out_norm(l, 14)
                peer(l, 217)


def _rope_tables():
    import numpy as np
    quarter = HD // 4
    row = np.repeat(np.arange(LAT * P // 64), 64)
    col = np.tile(np.arange(64), LAT * P // 64)
    inv = np.power(np.float32(10000.0), -np.arange(quarter, dtype=np.float32) / np.float32(quarter)).astype(np.float32)
    ang = (np.stack([row, col], -1).astype(np.float32)[..., None] * inv).astype(np.float32)
    c, s = np.cos(ang), np.sin(ang)
    cos = np.ones((TILES * P, 2, 2, quarter), np.float32)
    sin = np.zeros((TILES * P, 2, 2, quarter), np.float32)
    cos[:LAT * P] = c[:, :, None, :]
    sin[:LAT * P, :, 0] = -s
    sin[:LAT * P, :, 1] = s
    place = lambda a: np.ascontiguousarray(a.reshape(TILES, P, HD).transpose(1, 0, 2))
    return place(cos), place(sin)


def kernel(x, c, ctx, c_ctx, w_mod, b_mod, w_in, q_norm, k_norm, conv_w, sink, w_branch, w_out, ln1_g, ln1_b,
           w_pq, sub_keys, u_tab, v_tab, ln2_g, ln2_b):
    import numpy as np
    import concourse.bacc as bacc
    from concourse.bass_utils import run_bass_kernel_spmd

    a = {n: np.asarray(v) for n, v in dict(
        x=x, ctx=ctx, b_mod=b_mod, q_norm=q_norm, k_norm=k_norm, sink=sink, ln1_g=ln1_g, ln1_b=ln1_b,
        u_tab=u_tab, v_tab=v_tab, ln2_g=ln2_g, ln2_b=ln2_b).items()}
    L = LAYERS
    w_in = np.asarray(w_in)
    rows_first = lambda w, k: w.reshape(L, k, P, -1).transpose(0, 2, 1, 3)
    cc = np.stack([np.asarray(c)[0], np.asarray(c_ctx)])
    a["cc"] = cc.reshape(2, KD, P).transpose(2, 1, 0)
    a["w_mod"] = np.asarray(w_mod).reshape(L, KD, P, MODS, MB).transpose(0, 3, 2, 1, 4)
    kc = QKV - 2 * P
    a["w_qkv"] = rows_first(np.concatenate([w_in[..., 0:BW], w_in[..., BW:BW + 2 * P], w_in[..., kc:QKV],
                                            w_in[..., BW + 2 * P:kc]], -1), KD)
    cv = w_in[..., QKV:QKV + 3 * BW].reshape(L, KD, P, 3, BC, P)[:, :, :, [0, 2, 1]]
    a["w_conv"] = cv.transpose(0, 4, 3, 2, 1, 5).reshape(L, 3 * BC, P, KD, P)
    gate = w_in[..., QKV + 3 * BW:].reshape(L, KD, P, 3, KD, P).transpose(0, 4, 3, 2, 1, 5)
    branch = np.asarray(w_branch).reshape(L, 3, BC, P, KD, P).transpose(0, 4, 1, 3, 2, 5)
    a["w_gb"] = np.concatenate([gate, branch], 4).reshape(L, 3 * KD, P, KD + BC, P)
    a["w_out"] = rows_first(np.asarray(w_out), KD)
    a["w_pq"] = np.asarray(w_pq).reshape(L, KD, P, PH, 2 * P).transpose(0, 2, 3, 1, 4).reshape(L, P, PH, KD * 2 * P)
    a["sub_keys"] = np.asarray(sub_keys).reshape(L, 2 * PH, NK, P).transpose(0, 3, 1, 2)
    a["conv_w"] = np.asarray(conv_w).reshape(L, 3, BC, P).transpose(3, 0, 2, 1)
    a["rope_c"], a["rope_s"] = _rope_tables()

    nc = bacc.Bacc("TRN2", target_bir_lowering=False, num_devices=1)
    arrays, aps = {}, {}
    for n, v in a.items():
        arrays[f"in_{n}"] = np.ascontiguousarray(v)
        aps[n] = nc.dram_tensor(f"in_{n}", v.shape, mybir.dt.from_np(v.dtype), kind="ExternalInput").ap()
    out = nc.dram_tensor("out_0", (1, LAT * P, D), F32, kind="ExternalOutput").ap()
    hybrid_dit_peer(nc, out=out, **aps)
    r = run_bass_kernel_spmd(nc, [arrays], core_ids=[0])
    return r.results[0]["out_0"]
```
